# Optimizing a Trainium2 kernel written in Bass

```python
import jax, jax.numpy as jnp
from jax import lax
import numpy as np

D_MODEL = 1024
BATCH = 1
SEQ = 256
DEPTH = 1

CTX_LEN = 256
GRID_W = 64
NORM_EPS = 1e-6
SGU_WIDTH = 1024
SGU_GROUPS = 8
SGU_GROUP_DIM = SGU_WIDTH // SGU_GROUPS
CHUNK = 128
TINY_DIM = 64
ATTN_BLOCK = 128
ROPE_BASE = 10000.0
NA_HEADS = 16
NA_HEAD_DIM = 32
NA_WIDTH = NA_HEADS * NA_HEAD_DIM
NA_ROWS = 8
NA_COLS = 16
N_EXPERTS = 64
TOP_K = 8
EXPERT_FF = 256
SHARED_FF = 256
ROUTE_SCALE = 2.5
EXPERT_BLOCK = 128
COL_U = 0
COL_V = COL_U + SGU_WIDTH
COL_TQ = COL_V + SGU_WIDTH
COL_TK = COL_TQ + TINY_DIM
COL_TV = COL_TK + TINY_DIM
COL_NQ = COL_TV + TINY_DIM
COL_NK = COL_NQ + NA_WIDTH
COL_NV = COL_NK + NA_WIDTH
COL_GA = COL_NV + NA_WIDTH
COL_GB = COL_GA + D_MODEL
IN_WIDTH = COL_GB + D_MODEL


def rms_norm(x, g):
    xf = x.astype(jnp.float32)
    y = xf * lax.rsqrt(jnp.mean(xf * xf, -1, keepdims=True) + NORM_EPS)
    return (y * g.astype(jnp.float32)).astype(x.dtype)

def layer_norm(x, g, b):
    xf = x.astype(jnp.float32)
    mu = jnp.mean(xf, -1, keepdims=True)
    var = jnp.mean(jnp.square(xf - mu), -1, keepdims=True)
    y = (xf - mu) * lax.rsqrt(var + NORM_EPS) * g.astype(jnp.float32) + b.astype(jnp.float32)
    return y.astype(x.dtype)

def modulate(h, shift, scale):
    return h * (1 + scale) + shift

def swiglu(x, wg, wu, wd):
    return (jax.nn.silu(x @ wg) * (x @ wu)) @ wd

def axial_rope(x, n_tokens):
    dh = x.shape[-1]
    quarter = dh // 4
    t = jnp.arange(n_tokens)
    pos = jnp.stack([t // GRID_W, t % GRID_W], -1).astype(jnp.float32)
    inv_freq = ROPE_BASE ** (-jnp.arange(quarter, dtype=jnp.float32) / quarter)
    ang = pos[:, :, None] * inv_freq
    cos, sin = jnp.cos(ang), jnp.sin(ang)
    xf = x.astype(jnp.float32).reshape(x.shape[:-1] + (2, 2, quarter))
    x1, x2 = xf[..., 0, :], xf[..., 1, :]
    out = jnp.stack([x1 * cos - x2 * sin, x2 * cos + x1 * sin], -2)
    return out.reshape(x.shape).astype(x.dtype)

def tiny_attention(q, k_lat, v_lat, k_ctx, v_ctx):
    b, s, t = q.shape
    k_all = jnp.concatenate([k_lat, k_ctx], 1)
    v_all = jnp.concatenate([v_lat, v_ctx], 1)
    q_blocks = q.reshape(b, s // ATTN_BLOCK, ATTN_BLOCK, t).transpose(1, 0, 2, 3)
    scale = t ** -0.5

    def one_block(qb):
        sc = jnp.einsum("bqt,bkt->bqk", qb, k_all, preferred_element_type=jnp.float32) * scale
        p = jax.nn.softmax(sc, -1).astype(v_all.dtype)
        return jnp.einsum("bqk,bkt->bqt", p, v_all)

    out = lax.map(one_block, q_blocks)
    return out.transpose(1, 0, 2, 3).reshape(b, s, t)

def spatial_gating(u, v, tiny, ln_g, ln_b, w_s, b_s):
    b, s, _ = v.shape
    vn = layer_norm(v, ln_g, ln_b).reshape(b, s // CHUNK, CHUNK, SGU_GROUPS, SGU_GROUP_DIM)
    mixed = jnp.einsum("gpq,bnqgc->bnpgc", w_s, vn) + b_s.T[:, :, None]
    return u * (mixed.reshape(b, s, SGU_WIDTH) + tiny)

def neighbourhood_attention(q, k, v, k_ctx, v_ctx, rpb, rows):
    b, s, h, dh = q.shape
    kh = min(NA_ROWS, rows)
    qg = q.reshape(b, rows, GRID_W, h, dh)
    kg = k.reshape(b, rows, GRID_W, h, dh)
    vg = v.reshape(b, rows, GRID_W, h, dh)
    cq = np.arange(GRID_W)
    c_start = np.clip(cq - NA_COLS // 2, 0, GRID_W - NA_COLS)
    col_mask = (cq[None, :] >= c_start[:, None]) & (cq[None, :] < c_start[:, None] + NA_COLS)
    band_mask = np.broadcast_to(col_mask[:, None, :], (GRID_W, kh, GRID_W)).reshape(GRID_W, kh * GRID_W)
    dc_idx = np.clip(cq[None, :] - cq[:, None], -(NA_COLS - 1), NA_COLS - 1) + NA_COLS - 1
    col_bias = rpb[:, :, dc_idx]
    scale = dh ** -0.5

    def one_row(r):
        r_start = jnp.clip(r - kh // 2, 0, rows - kh)
        qb = lax.dynamic_index_in_dim(qg, r, axis=1, keepdims=False)
        kb = lax.dynamic_slice_in_dim(kg, r_start, kh, axis=1).reshape(b, kh * GRID_W, h, dh)
        vb = lax.dynamic_slice_in_dim(vg, r_start, kh, axis=1).reshape(b, kh * GRID_W, h, dh)
        dr = r_start + jnp.arange(kh) - r + NA_ROWS - 1
        bias = jnp.take(col_bias, dr, axis=1).transpose(0, 2, 1, 3).reshape(h, GRID_W, kh * GRID_W)
        s_lat = jnp.einsum("bqhd,bkhd->bhqk", qb, kb, preferred_element_type=jnp.float32) * scale + bias
        s_lat = jnp.where(band_mask, s_lat, -jnp.inf)
        s_ctx = jnp.einsum("bqhd,bkhd->bhqk", qb, k_ctx, preferred_element_type=jnp.float32) * scale
        p = jax.nn.softmax(jnp.concatenate([s_lat, s_ctx], -1), -1).astype(v.dtype)
        n_lat = kh * GRID_W
        return (jnp.einsum("bhqk,bkhd->bqhd", p[..., :n_lat], vb)
                + jnp.einsum("bhqk,bkhd->bqhd", p[..., n_lat:], v_ctx))

    out = lax.map(one_row, jnp.arange(rows))
    return out.transpose(1, 0, 2, 3, 4).reshape(b, s, h * dh)

def moe_ffn(h, w_router, b_router, w_e_gate, w_e_up, w_e_down, w_sh_gate, w_sh_up, w_sh_down):
    n, d = h.shape
    scores = jax.nn.sigmoid(jnp.matmul(h, w_router, preferred_element_type=jnp.float32))
    _, idx = lax.top_k(scores + b_router.astype(jnp.float32), TOP_K)
    wts = jnp.take_along_axis(scores, idx, axis=-1)
    wts = (wts / jnp.sum(wts, -1, keepdims=True) * ROUTE_SCALE).astype(h.dtype)
    n_assign = n * TOP_K
    flat_e = idx.reshape(-1)
    flat_tok = jnp.repeat(jnp.arange(n, dtype=jnp.int32), TOP_K)
    flat_w = wts.reshape(-1)
    order = jnp.argsort(flat_e)
    se, st, sw = flat_e[order], flat_tok[order], flat_w[order]
    counts = jnp.bincount(flat_e, length=N_EXPERTS)
    starts = jnp.cumsum(counts) - counts
    pad_counts = (counts + EXPERT_BLOCK - 1) // EXPERT_BLOCK * EXPERT_BLOCK
    pad_ends = jnp.cumsum(pad_counts)
    pad_starts = pad_ends - pad_counts
    dest = pad_starts[se] + jnp.arange(n_assign) - starts[se]
    n_blocks = -(-n_assign // EXPERT_BLOCK) + N_EXPERTS
    n_rows = n_blocks * EXPERT_BLOCK
    row_tok = jnp.full((n_rows,), n, jnp.int32).at[dest].set(st)
    row_w = jnp.zeros((n_rows,), h.dtype).at[dest].set(sw)
    block_e = jnp.minimum(jnp.searchsorted(pad_ends, jnp.arange(n_blocks) * EXPERT_BLOCK, side="right"),
                          N_EXPERTS - 1)
    h_pad = jnp.concatenate([h, jnp.zeros((1, d), h.dtype)], 0)

    def expert_block(acc, blk):
        tok, wt, e = blk
        yb = swiglu(h_pad[tok], w_e_gate[e], w_e_up[e], w_e_down[e]) * wt[:, None]
        return acc.at[tok].add(yb), None

    routed, _ = lax.scan(expert_block, jnp.zeros((n + 1, d), h.dtype),
                         (row_tok.reshape(n_blocks, EXPERT_BLOCK), row_w.reshape(n_blocks, EXPERT_BLOCK), block_e))
    return swiglu(h, w_sh_gate, w_sh_up, w_sh_down) + routed[:n]

def hybrid_layer(x, c, ctx, c_ctx, w_ada, b_ada, norm_mix_g, norm_ffn_g, w_in, b_in,
                 sgu_ln_g, sgu_ln_b, sgu_w_s, sgu_b_s, tiny_w_o, na_rpb, w_up_a, w_up_b, w_out,
                 w_router, b_router, w_e_gate, w_e_up, w_e_down, w_sh_gate, w_sh_up, w_sh_down):
    b, s, d = x.shape
    rows = s // GRID_W
    ctx_len = ctx.shape[1]
    mod = (jax.nn.silu(c) @ w_ada + b_ada)[:, None, :]
    sh_mix, sc_mix, g_mix, sh_ffn, sc_ffn, g_ffn = jnp.split(mod, 6, -1)
    mod_ctx = jax.nn.silu(c_ctx) @ w_ada[:, :2 * d] + b_ada[:2 * d]

    h = modulate(rms_norm(x, norm_mix_g), sh_mix, sc_mix)
    p_in = h @ w_in + b_in
    u = jax.nn.gelu(p_in[..., COL_U:COL_V], approximate=False)
    v = jax.nn.gelu(p_in[..., COL_V:COL_TQ], approximate=False)
    tq = axial_rope(p_in[..., COL_TQ:COL_TK], s)
    tk = axial_rope(p_in[..., COL_TK:COL_TV], s)
    tv = p_in[..., COL_TV:COL_NQ]
    nq = p_in[..., COL_NQ:COL_NK].reshape(b, s, NA_HEADS, NA_HEAD_DIM)
    nk = p_in[..., COL_NK:COL_NV].reshape(b, s, NA_HEADS, NA_HEAD_DIM)
    nv = p_in[..., COL_NV:COL_GA].reshape(b, s, NA_HEADS, NA_HEAD_DIM)
    gate_a = jax.nn.sigmoid(p_in[..., COL_GA:COL_GB])
    gate_b = jax.nn.sigmoid(p_in[..., COL_GB:IN_WIDTH])

    hc = modulate(rms_norm(ctx, norm_mix_g), mod_ctx[:d], mod_ctx[d:])
    c_tiny = hc @ w_in[:, COL_TK:COL_NQ] + b_in[COL_TK:COL_NQ]
    tk_c, tv_c = c_tiny[..., :TINY_DIM], c_tiny[..., TINY_DIM:]
    c_na = hc @ w_in[:, COL_NK:COL_GA] + b_in[COL_NK:COL_GA]
    nk_c = c_na[..., :NA_WIDTH].reshape(b, ctx_len, NA_HEADS, NA_HEAD_DIM)
    nv_c = c_na[..., NA_WIDTH:].reshape(b, ctx_len, NA_HEADS, NA_HEAD_DIM)

    tiny = tiny_attention(tq, tk, tv, tk_c, tv_c) @ tiny_w_o
    o_a = spatial_gating(u, v, tiny, sgu_ln_g, sgu_ln_b, sgu_w_s, sgu_b_s)
    o_b = neighbourhood_attention(nq, nk, nv, nk_c, nv_c, na_rpb, rows)

    merged = gate_a * (o_a @ w_up_a) + gate_b * (o_b @ w_up_b)
    x = x + g_mix * (merged @ w_out)

    h2 = modulate(rms_norm(x, norm_ffn_g), sh_ffn, sc_ffn).reshape(b * s, d)
    y = moe_ffn(h2, w_router, b_router, w_e_gate, w_e_up, w_e_down, w_sh_gate, w_sh_up, w_sh_down)
    return x + g_ffn * y.reshape(b, s, d)

def first_inputs(seed: int = 0) -> dict:
    key = jax.random.key(seed)
    ks = jax.random.split(key, 32)
    f32 = jnp.float32
    L, D = DEPTH, D_MODEL

    def nrm(k, shape, scale):
        return jax.random.normal(k, shape, f32) * scale

    return {
        "x": nrm(ks[0], (BATCH, SEQ, D), 1.0),
        "c": nrm(ks[1], (BATCH, D), 1.0),
        "ctx": nrm(ks[2], (BATCH, CTX_LEN, D), 1.0),
        "c_ctx": nrm(ks[3], (D,), 1.0),
        "w_ada": nrm(ks[4], (L, D, 6 * D), 0.5 * D ** -0.5),
        "b_ada": nrm(ks[5], (L, 6 * D), 0.01),
        "norm_mix_g": 1.0 + nrm(ks[6], (L, D), 0.1),
        "norm_ffn_g": 1.0 + nrm(ks[7], (L, D), 0.1),
        "w_in": nrm(ks[8], (L, D, IN_WIDTH), D ** -0.5),
        "b_in": nrm(ks[9], (L, IN_WIDTH), 0.01),
        "sgu_ln_g": 1.0 + nrm(ks[10], (L, SGU_WIDTH), 0.1),
        "sgu_ln_b": nrm(ks[11], (L, SGU_WIDTH), 0.01),
        "sgu_w_s": nrm(ks[12], (L, SGU_GROUPS, CHUNK, CHUNK), CHUNK ** -0.5),
        "sgu_b_s": 1.0 + nrm(ks[13], (L, SGU_GROUPS, CHUNK), 0.1),
        "tiny_w_o": nrm(ks[14], (L, TINY_DIM, SGU_WIDTH), TINY_DIM ** -0.5),
        "na_rpb": nrm(ks[15], (L, NA_HEADS, 2 * NA_ROWS - 1, 2 * NA_COLS - 1), 0.1),
        "w_up_a": nrm(ks[16], (L, SGU_WIDTH, D), SGU_WIDTH ** -0.5),
        "w_up_b": nrm(ks[17], (L, NA_WIDTH, D), NA_WIDTH ** -0.5),
        "w_out": nrm(ks[18], (L, D, D), D ** -0.5),
        "w_router": nrm(ks[19], (L, D, N_EXPERTS), D ** -0.5),
        "b_router": nrm(ks[20], (L, N_EXPERTS), 0.01),
        "w_e_gate": nrm(ks[21], (L, N_EXPERTS, D, EXPERT_FF), D ** -0.5),
        "w_e_up": nrm(ks[22], (L, N_EXPERTS, D, EXPERT_FF), D ** -0.5),
        "w_e_down": nrm(ks[23], (L, N_EXPERTS, EXPERT_FF, D), EXPERT_FF ** -0.5),
        "w_sh_gate": nrm(ks[24], (L, D, SHARED_FF), D ** -0.5),
        "w_sh_up": nrm(ks[25], (L, D, SHARED_FF), D ** -0.5),
        "w_sh_down": nrm(ks[26], (L, SHARED_FF, D), SHARED_FF ** -0.5),
        "final_norm_g": 1.0 + nrm(ks[27], (D,), 0.1),
    }

def first_block(x, c, ctx, c_ctx, w_ada, b_ada, norm_mix_g, norm_ffn_g, w_in, b_in,
              sgu_ln_g, sgu_ln_b, sgu_w_s, sgu_b_s, tiny_w_o, na_rpb, w_up_a, w_up_b, w_out,
              w_router, b_router, w_e_gate, w_e_up, w_e_down, w_sh_gate, w_sh_up, w_sh_down,
              final_norm_g):
    for i in range(DEPTH):
        x = hybrid_layer(x, c, ctx, c_ctx, w_ada[i], b_ada[i], norm_mix_g[i], norm_ffn_g[i], w_in[i], b_in[i],
                         sgu_ln_g[i], sgu_ln_b[i], sgu_w_s[i], sgu_b_s[i], tiny_w_o[i], na_rpb[i],
                         w_up_a[i], w_up_b[i], w_out[i], w_router[i], b_router[i],
                         w_e_gate[i], w_e_up[i], w_e_down[i], w_sh_gate[i], w_sh_up[i], w_sh_down[i])
    return rms_norm(x, final_norm_g)


DEPTH_2 = 2

HEAD_DIM = 64
SB_HEADS = 8
MOBA_HEADS = 8
SB_WIDTH = SB_HEADS * HEAD_DIM
MOBA_WIDTH = MOBA_HEADS * HEAD_DIM
SB_Q_BLOCK = 128
MOBA_BLOCK = 256
MOBA_TOPK = 3
MOBA_Q_CHUNK = 128
ROPE_THETA = 500000.0
ROPE_DIM = HEAD_DIM // 4
D_FF = -(-8 * D_MODEL // (3 * 256)) * 256
DEEPNORM_ALPHA = (2 * DEPTH_2) ** 0.25
DEEPNORM_BETA = (8 * DEPTH_2) ** -0.25
LN_EPS = 1e-5
IN_COLS = 3 * SB_WIDTH + 3 * MOBA_WIDTH + 2 * D_MODEL


def layer_norm_2(x, g, b):
    xf = x.astype(jnp.float32)
    mu = jnp.mean(xf, axis=-1, keepdims=True)
    var = jnp.mean(jnp.square(xf - mu), axis=-1, keepdims=True)
    y = (xf - mu) * lax.rsqrt(var + LN_EPS) * g.astype(jnp.float32) + b.astype(jnp.float32)
    return y.astype(x.dtype)

def partial_rope(x, pos):
    half = ROPE_DIM // 2
    inv_freq = ROPE_THETA ** (-jnp.arange(0, ROPE_DIM, 2, dtype=jnp.float32) / ROPE_DIM)
    ang = pos.astype(jnp.float32)[:, None] * inv_freq[None, :]
    cos, sin = jnp.cos(ang), jnp.sin(ang)
    xf = x.astype(jnp.float32)
    x1, x2, rest = xf[..., :half], xf[..., half:ROPE_DIM], xf[..., ROPE_DIM:]
    out = jnp.concatenate([x1 * cos - x2 * sin, x2 * cos + x1 * sin, rest], axis=-1)
    return out.astype(x.dtype)

def stick_breaking_attention(q, k, v):
    B, H, S, dh = q.shape
    nblk = S // SB_Q_BLOCK
    scale = dh ** -0.5
    kpos = jnp.arange(S)
    qb = q.reshape(B, H, nblk, SB_Q_BLOCK, dh).transpose(2, 0, 1, 3, 4)

    def block(args):
        qi, i = args
        qpos = i * SB_Q_BLOCK + jnp.arange(SB_Q_BLOCK)
        z = jnp.einsum('bhqd,bhkd->bhqk', qi, k).astype(jnp.float32) * scale
        past = kpos[None, :] < qpos[:, None]
        log_keep = jnp.where(past, jax.nn.log_sigmoid(-z), 0.0)
        suffix = lax.cumsum(log_keep, axis=3, reverse=True) - log_keep
        w = jnp.where(past, jnp.exp(jax.nn.log_sigmoid(z) + suffix), 0.0)
        return jnp.einsum('bhqk,bhkd->bhqd', w.astype(v.dtype), v)

    out = lax.map(block, (qb, jnp.arange(nblk)))
    return out.transpose(1, 2, 0, 3, 4).reshape(B, H, S, dh)

def moba_attention(q, k, v):
    B, H, S, dh = q.shape
    nb = -(-S // MOBA_BLOCK)
    pad = nb * MOBA_BLOCK - S
    kp = jnp.pad(k, ((0, 0), (0, 0), (0, pad), (0, 0)))
    vp = jnp.pad(v, ((0, 0), (0, 0), (0, pad), (0, 0)))
    kb = kp.reshape(B, H, nb, MOBA_BLOCK, dh)
    vb = vp.reshape(B, H, nb, MOBA_BLOCK, dh)
    kmean = jnp.mean(kb.astype(jnp.float32), axis=3).astype(k.dtype)
    topk = min(MOBA_TOPK, nb)
    nchunk = S // MOBA_Q_CHUNK
    qc = q.reshape(B, H, nchunk, MOBA_Q_CHUNK, dh).transpose(2, 0, 1, 3, 4)
    bi = jnp.arange(B)[:, None, None, None]
    hi = jnp.arange(H)[None, :, None, None]
    blk_ids = jnp.arange(nb)
    scale = dh ** -0.5

    def chunk(args):
        qi, c = args
        qpos = c * MOBA_Q_CHUNK + jnp.arange(MOBA_Q_CHUNK)
        own = (c * MOBA_Q_CHUNK) // MOBA_BLOCK
        gate = jnp.einsum('bhqd,bhnd->bhqn', qi, kmean).astype(jnp.float32)
        gate = jnp.where(blk_ids < own, gate, -jnp.inf)
        _, idx = lax.top_k(gate, topk)
        valid = idx < own
        k_sel = kb[bi, hi, idx]
        v_sel = vb[bi, hi, idx]
        s_sel = jnp.einsum('bhqd,bhqnkd->bhqnk', qi, k_sel).astype(jnp.float32) * scale
        s_sel = jnp.where(valid[..., None], s_sel, -jnp.inf).reshape(B, H, MOBA_Q_CHUNK, topk * MOBA_BLOCK)
        k_own = lax.dynamic_slice_in_dim(kb, own, 1, axis=2)[:, :, 0]
        v_own = lax.dynamic_slice_in_dim(vb, own, 1, axis=2)[:, :, 0]
        s_own = jnp.einsum('bhqd,bhkd->bhqk', qi, k_own).astype(jnp.float32) * scale
        own_pos = own * MOBA_BLOCK + jnp.arange(MOBA_BLOCK)
        s_own = jnp.where(own_pos[None, :] <= qpos[:, None], s_own, -jnp.inf)
        p = jax.nn.softmax(jnp.concatenate([s_sel, s_own], axis=-1), axis=-1).astype(v.dtype)
        p_sel = p[..., :topk * MOBA_BLOCK].reshape(B, H, MOBA_Q_CHUNK, topk, MOBA_BLOCK)
        p_own = p[..., topk * MOBA_BLOCK:]
        return (jnp.einsum('bhqnk,bhqnkd->bhqd', p_sel, v_sel)
                + jnp.einsum('bhqk,bhkd->bhqd', p_own, v_own))

    out = lax.map(chunk, (qc, jnp.arange(nchunk)))
    return out.transpose(1, 2, 0, 3, 4).reshape(B, H, S, dh)

def heads(t, n_heads):
    B, S, _ = t.shape
    return t.reshape(B, S, n_heads, HEAD_DIM).transpose(0, 2, 1, 3)

def merge_heads(t):
    B, H, S, dh = t.shape
    return t.transpose(0, 2, 1, 3).reshape(B, S, H * dh)

def hybrid_mixer(x, w_in, w_branch_sb, w_branch_moba, w_out):
    S = x.shape[1]
    proj = x @ w_in
    cuts = np.cumsum([SB_WIDTH, SB_WIDTH, SB_WIDTH, MOBA_WIDTH, MOBA_WIDTH, MOBA_WIDTH, D_MODEL]).tolist()
    q_sb, k_sb, v_sb, q_mb, k_mb, v_mb, g_sb, g_mb = jnp.split(proj, cuts, axis=-1)
    pos = jnp.arange(S)
    o_sb = stick_breaking_attention(heads(q_sb, SB_HEADS), heads(k_sb, SB_HEADS), heads(v_sb, SB_HEADS))
    o_mb = moba_attention(partial_rope(heads(q_mb, MOBA_HEADS), pos),
                          partial_rope(heads(k_mb, MOBA_HEADS), pos),
                          heads(v_mb, MOBA_HEADS))
    branch_sb = merge_heads(o_sb) @ w_branch_sb
    branch_mb = merge_heads(o_mb) @ w_branch_moba
    merged = jax.nn.sigmoid(g_sb) * branch_sb + jax.nn.sigmoid(g_mb) * branch_mb
    return merged @ w_out

def swiglu_2(x, w_gate, w_up, w_down):
    return (jax.nn.silu(x @ w_gate) * (x @ w_up)) @ w_down

def second_inputs(seed: int = 0) -> dict:
    key = jax.random.key(seed)
    ks = jax.random.split(key, 12)
    nrm = lambda k, shape, s: jax.random.normal(k, shape, jnp.float32) * s
    L = DEPTH_2
    return {
        "x": jax.random.normal(ks[0], (BATCH, SEQ, D_MODEL), jnp.float32),
        "w_in": nrm(ks[1], (L, D_MODEL, IN_COLS), D_MODEL ** -0.5),
        "w_branch_sb": nrm(ks[2], (L, SB_WIDTH, D_MODEL), SB_WIDTH ** -0.5),
        "w_branch_moba": nrm(ks[3], (L, MOBA_WIDTH, D_MODEL), MOBA_WIDTH ** -0.5),
        "w_out": nrm(ks[4], (L, D_MODEL, D_MODEL), D_MODEL ** -0.5 * DEEPNORM_BETA),
        "ln_mix_g": 1.0 + nrm(ks[5], (L, D_MODEL), 0.02),
        "ln_mix_b": nrm(ks[6], (L, D_MODEL), 0.02),
        "w_ffn_gate": nrm(ks[7], (L, D_MODEL, D_FF), D_MODEL ** -0.5),
        "w_ffn_up": nrm(ks[8], (L, D_MODEL, D_FF), D_MODEL ** -0.5),
        "w_ffn_down": nrm(ks[9], (L, D_FF, D_MODEL), D_FF ** -0.5 * DEEPNORM_BETA),
        "ln_ffn_g": 1.0 + nrm(ks[10], (L, D_MODEL), 0.02),
        "ln_ffn_b": nrm(ks[11], (L, D_MODEL), 0.02),
    }

def second_block(x, w_in, w_branch_sb, w_branch_moba, w_out, ln_mix_g, ln_mix_b,
              w_ffn_gate, w_ffn_up, w_ffn_down, ln_ffn_g, ln_ffn_b):
    for l in range(DEPTH_2):
        mix = hybrid_mixer(x, w_in[l], w_branch_sb[l], w_branch_moba[l], w_out[l])
        x = layer_norm_2(DEEPNORM_ALPHA * x + mix, ln_mix_g[l], ln_mix_b[l])
        ffn = swiglu_2(x, w_ffn_gate[l], w_ffn_up[l], w_ffn_down[l])
        x = layer_norm_2(DEEPNORM_ALPHA * x + ffn, ln_ffn_g[l], ln_ffn_b[l])
    return x


def setup_inputs(seed=0):
    out = dict(first_inputs(seed))
    for name, value in second_inputs(seed + 1).items():
        if name != "x":
            out[name + "_2"] = value
    return out


def reference(
    x, c, ctx, c_ctx, w_ada, b_ada, norm_mix_g, norm_ffn_g, w_in, b_in, sgu_ln_g, sgu_ln_b,
    sgu_w_s, sgu_b_s, tiny_w_o, na_rpb, w_up_a, w_up_b, w_out, w_router, b_router, w_e_gate,
    w_e_up, w_e_down, w_sh_gate, w_sh_up, w_sh_down, final_norm_g, w_in_2, w_branch_sb_2,
    w_branch_moba_2, w_out_2, ln_mix_g_2, ln_mix_b_2, w_ffn_gate_2, w_ffn_up_2, w_ffn_down_2,
    ln_ffn_g_2, ln_ffn_b_2,
):
    x = first_block(
        x, c, ctx, c_ctx, w_ada, b_ada, norm_mix_g, norm_ffn_g, w_in, b_in, sgu_ln_g, sgu_ln_b,
        sgu_w_s, sgu_b_s, tiny_w_o, na_rpb, w_up_a, w_up_b, w_out, w_router, b_router, w_e_gate,
        w_e_up, w_e_down, w_sh_gate, w_sh_up, w_sh_down, final_norm_g,
    )
    return second_block(
        x, w_in_2, w_branch_sb_2, w_branch_moba_2, w_out_2, ln_mix_g_2, ln_mix_b_2,
        w_ffn_gate_2, w_ffn_up_2, w_ffn_down_2, ln_ffn_g_2, ln_ffn_b_2,
    )


_drawn_inputs = setup_inputs


def setup_inputs(seed=0):
    import zlib

    import numpy as np

    out = dict(_drawn_inputs(seed))
    spreads = {}
    factors = {'b_in': 4.1, 'sgu_ln_b': 8.0, 'na_rpb': 21.678}
    for name, (base, spread) in spreads.items():
        noise = np.random.default_rng([zlib.crc32(name.encode()), seed]).standard_normal(out[name].shape)
        drawn = base * np.exp(spread * noise) if base else spread * noise
        out[name] = __import__('jax').numpy.asarray(drawn.astype(out[name].dtype))
    for name, factor in factors.items():
        out[name] = (out[name] * factor).astype(out[name].dtype)
    return out
```

```python
from contextlib import ExitStack

import numpy as np

import concourse.bass as bass
from concourse import mybir

ALU = mybir.AluOpType
ACT = mybir.ActivationFunctionType
AX_X = mybir.AxisListType.X
F32 = mybir.dt.float32
U32 = mybir.dt.uint32

P = 128
D = 1024
S = 256
TT = S // P
KT = D // P
CTX = 256
GRID_W = 64
ROWS = S // GRID_W
NORM_EPS = 1e-6
LN_EPS = 1e-5
GROUPS = 8
TINY = 64
NH, NDH = 16, 32
NW = NH * NDH
NA_ROWS, NA_COLS = 8, 16
E = 64
TOP_K = 8
FF = 256
ROUTE_SCALE = 2.5
COL_U, COL_V, COL_TQ = 0, D, 2 * D
COL_NQ = COL_TQ + 3 * TINY
COL_NK, COL_NV = COL_NQ + NW, COL_NQ + 2 * NW
COL_GA = COL_NQ + 3 * NW
COL_GB = COL_GA + D
L2 = 2
H2, DH2 = 8, 64
W2 = H2 * DH2
ROPE2 = DH2 // 4
DFF = 2816
FT = DFF // P
ALPHA = (2 * L2) ** 0.25
CHUNK = 512
MASKED = -1e30
SLOTS = 9
SLOT = 2048
DR = 6

CONST = {}
_at = 0
for _name, _n in [("ident", P), ("ones", P), ("past01", P), ("future", P), ("own_future", P),
                  ("window", GRID_W), ("zeros", S), ("tcos", TT * 32), ("tsin", TT * 32),
                  ("pcos", TT * 8), ("psin", TT * 8)]:
    CONST[_name] = (_at, _n)
    _at += _n
N_CONST = _at


def constants():
    c = np.zeros((P, N_CONST), np.float32)

    def put(name, value):
        at, n = CONST[name]
        c[:, at:at + n] = np.asarray(value, np.float32).reshape(P, n)

    q, k = np.arange(P)[:, None], np.arange(P)[None, :]
    put("ident", q == k)
    put("ones", np.ones((P, P)))
    put("past01", k < q)
    put("future", np.where(k <= q, 0.0, MASKED))
    put("own_future", np.where(k < q, 0.0, MASKED))
    cq, ck = (np.arange(P) % GRID_W)[:, None], np.arange(GRID_W)[None, :]
    start = np.clip(cq - NA_COLS // 2, 0, GRID_W - NA_COLS)
    put("window", np.where((ck >= start) & (ck < start + NA_COLS), 0.0, MASKED))
    tok = np.arange(S)
    quarter = TINY // 4
    pos = np.stack([tok // GRID_W, tok % GRID_W], -1).astype(np.float32)
    inv = np.float32(10000.0) ** (-np.arange(quarter, dtype=np.float32) / np.float32(quarter))
    ang = (pos[:, :, None] * inv).astype(np.float32).reshape(TT, P, 2 * quarter).transpose(1, 0, 2)
    put("tcos", np.cos(ang))
    put("tsin", np.sin(ang))
    inv = np.float32(500000.0) ** (-np.arange(0, ROPE2, 2, dtype=np.float32) / np.float32(ROPE2))
    ang = (tok.astype(np.float32)[:, None] * inv).astype(np.float32).reshape(TT, P, ROPE2 // 2).transpose(1, 0, 2)
    put("pcos", np.cos(ang))
    put("psin", np.sin(ang))
    return c


class Ring:

    def __init__(self, slots):
        self.slots = list(slots)
        self.at = 0
        self.count = {s: 0 for s in self.slots}
        self.place = {}
        self.owner = {s: None for s in self.slots}
        self.before = {}
        self.in_loop = None

    def take(self, key):
        s = self.slots[self.at % len(self.slots)]
        assert key not in self.place, key
        self.place[key] = (s, self.count[s], 0)
        self.before[key] = [self.owner[s]] if self.owner[s] is not None else []
        self.owner[s] = key
        self.count[s] += 1
        self.at += 1
        if self.in_loop is not None:
            self.in_loop[1].append(key)

    def loop(self):
        self.in_loop = (self.at, [], dict(self.count), dict(self.owner))

    def end_loop(self, iterations):
        at0, keys, start, owner0 = self.in_loop
        first = {}
        for key in keys:
            s, n, _ = self.place[key]
            self.place[key] = (s, n, self.count[s] - start[s])
            first.setdefault(s, key)
        for s, key in first.items():
            self.before[key] = self.before[key] + [("previous iteration", self.owner[s])]
        for s in self.slots:
            self.count[s] = start[s] + iterations * (self.count[s] - start[s])
        self.in_loop = None


HEAD = [2 * j + side for side in range(P // DH2) for j in range(H2 * DH2 // P)]
ITEMS = [(t, h, CHUNK // (P * (t + 1)), P * (t + 1))
         for t in range(TT) for h in range(0, H2, CHUNK // (P * (t + 1)))]
NI = len(ITEMS)
LAST_OF_TILE = [max(i for i, it in enumerate(ITEMS) if it[0] == t) for t in range(TT)]
NA_STEPS = TT * NH


def plan():
    main, long, hold = Ring([0, 1, 2]), Ring([3, 4, 5, 6]), Ring([7])
    units = Ring(range(SLOTS))
    freed_by, sources, order = {}, {}, []

    def unit(key, job, *source):
        units.take(key)
        freed_by[key] = job
        sources[key] = source
        order.append(key)

    def chunk(key, job, *source):
        for half in range(2):
            unit(key + (half,), job, "rows", *source, half)

    for n in range(4):
        chunk(("ada", n), ("mod", 0), "w_ada", n * CHUNK)
    main.take(("mod", 0))
    for g in range(4):
        main.take(("xT", g))
        main.take(("cT", g))
    unit(("win", "tiny"), ("tiny", 3), "tiny")
    for t in range(4):
        long.take(("tiny", t))
    chunk(("win", "nq"), ("nq", 1), "w_in", COL_NQ)
    for p in range(2):
        long.take(("nq", p))
    chunk(("win", "nk"), ("nk", 3), "w_in", COL_NK)
    for f in range(4):
        long.take(("nk", f))
    chunk(("win", "nv"), ("nv", 3), "w_in", COL_NV)
    for t in range(4):
        long.take(("nv", t))
    main.take(("tqT", 0))
    main.take(("tkT", 0))
    for t in range(TT):
        main.take(("ts", t))
    for t in range(TT):
        main.take(("tpT", t))
        main.take(("tO", t))
    for name, col in (("v", COL_V), ("u", COL_U)):
        for n in range(2):
            chunk(("win", name, n), (name, n, 1), "w_in", col + n * CHUNK)
            for t in range(TT):
                long.take((name, n, t))
    for i in range(NA_STEPS + 2):
        if i < NA_STEPS:
            main.take(("ns", i))
        if 1 <= i <= NA_STEPS:
            main.take(("npT", i - 1))
    for t in range(TT):
        hold.take(("nO", t))
    for name, col in (("ga", COL_GA), ("gb", COL_GB)):
        for n in range(2):
            chunk(("win", name, n), (name, n, 1), "w_in", col + n * CHUNK)
            for t in range(TT):
                long.take((name, n, t))
    for n in range(4, 12):
        chunk(("ada", n), ("mod", n // 2 - 1), "w_ada", n * CHUNK)
        if n % 2:
            long.take(("mod", n // 2 - 1))
    for v in range(4):
        for n in range(2):
            long.take(("row", v, n))
    for t in range(TT):
        for n in range(2):
            main.take(("sg", t, n))
    for g in range(4):
        main.take(("oaT", g))
    for g in range(2):
        main.take(("obT", g))
    for n in range(2):
        chunk(("upa", n), ("upa", n, 1), "w_up_a", n * CHUNK)
        unit(("upb", n), ("upb", n, 1), "half", "w_up_b", n * CHUNK)
        for t in range(TT):
            long.take(("upa", n, t))
            long.take(("upb", n, t))
    for g in range(4):
        main.take(("mT", g))
    for n in range(2):
        chunk(("wo", n), ("wo", n, 1), "w_out", n * CHUNK)
        for t in range(TT):
            long.take(("wo", n, t))
    for g in range(4):
        main.take(("h2T", g))
    for t in range(TT):
        main.take(("rt", t))
    unit(("shg",), ("shg", 1), "ff", "w_sh_gate", 0)
    unit(("shu",), ("shg", 1), "ff", "w_sh_up", 0)
    unit(("shd",), ("shd", 1, 1), "down", "w_sh_down", 0)
    for f in range(2):
        main.take(("shg", f))
    for n in range(2):
        for t in range(TT):
            long.take(("shd", n, t))
    for r in (main, long, units):
        r.loop()
    unit(("eg",), ("eg", 1), "expert", "w_e_gate")
    unit(("eu",), ("eg", 1), "expert", "w_e_up")
    unit(("ed",), ("ed", 1, 1), "expert", "w_e_down")
    for f in range(2):
        main.take(("eg", f))
    for n in range(2):
        for t in range(TT):
            long.take(("ed", n, t))
    for r in (main, long, units):
        r.end_loop(E)
    for r in (main, long, hold, units):
        r.loop()
    for g in range(4):
        main.take(("l_xT", g))
    for name, at in (("qs", 0), ("ks", 1)):
        chunk(("l_in", name), (name, 1), "w_in_2", at * W2)
        for p in range(2):
            long.take((name, p))
    chunk(("l_in", "vs"), ("vs", 1), "w_in_2", 2 * W2)
    for t in range(TT):
        long.take(("vs", t))
    for i in range(2 * NI + 2):
        if i < 2 * NI:
            main.take(("sc", i))
        if i < len(FILLERS):
            name, n, t = FILLERS[i]
            if t == 0:
                chunk(("l_in", name, n), (name, n, 1), "w_in_2", 3 * W2 + FILL_NAMES.index((name, n)) * CHUNK)
            long.take((name, n, t))
        if 1 <= i <= 2 * NI:
            main.take(("wT", i - 1))
        if i == NI - 1:
            for name in ("qmT", "kmT"):
                for p in range(2):
                    long.take((name, p))
    for b in range(2):
        for t in range(TT):
            hold.take(("o", b, t))
    for b in range(2):
        for p in range(2):
            main.take(("oT", b, p))
    for n in range(2):
        unit(("bs", n), ("bs", n, 1), "half", "w_branch_sb_2", n * CHUNK)
        unit(("bm", n), ("bm", n, 1), "half", "w_branch_moba_2", n * CHUNK)
        for t in range(TT):
            long.take(("bs", n, t))
            long.take(("bm", n, t))
    for g in range(4):
        main.take(("l_mT", g))
    for n in range(2):
        chunk(("l_wo", n), ("l_wo", n, 1), "w_out_2", n * CHUNK)
        for t in range(TT):
            long.take(("l_wo", n, t))
    for g in range(4):
        main.take(("l_yT", g))
    for n in range(2):
        for t in range(TT):
            long.take(("fd", n, t))
    for pair in range(FT // 2 + 1):
        if pair < FT // 2:
            unit(("fg", pair), ("fg", 2 * pair + 1), "ff", "w_ffn_gate_2", pair * FF)
            unit(("fu", pair), ("fg", 2 * pair + 1), "ff", "w_ffn_up_2", pair * FF)
            for f in (2 * pair, 2 * pair + 1):
                main.take(("fg", f))
        if pair:
            d = pair - 1
            after = ("fg", 2 * (d + 2)) if d + 2 < FT // 2 else ("fd", 0, 0) if d + 2 == FT // 2 else ("fd", 1, 1)
            unit(("fd", d), after, "down", "w_ffn_down_2", d * FF)
    for r in (main, long, hold, units):
        r.end_loop(L2)
    banks = {**main.place, **long.place, **hold.place}
    return banks, units, freed_by, sources, order


FILL_NAMES = [("qm", 0), ("km", 0), ("vm", 0), ("gs", 0), ("gs", 1), ("gm", 0), ("gm", 1)]
FILLERS = [(name, n, t) for name, n in FILL_NAMES for t in range(TT)]
LAYER_KEYS = ("l_in", "bs", "bm", "l_wo", "fg", "fu", "fd")
DVE_STEPS_PER_LAYER = 104


def build(nc, a):
    banks, units, freed_by, sources, order = plan()
    ctx = ExitStack()
    with ctx:
        def sb(name, *dims, dt=F32):
            return ctx.enter_context(nc.sbuf_tensor(name, [P, *dims], dt))

        sems = {}

        def sem(name):
            if name not in sems:
                sems[name] = ctx.enter_context(nc.semaphore(name))
            return sems[name]

        psum = [ctx.enter_context(nc.psum_tensor(f"bank{b}", [P, CHUNK], F32)) for b in range(8)]
        bank_full = [sem(f"bank_full{b}") for b in range(8)]
        bank_free = [sem(f"bank_free{b}") for b in range(8)]
        landed = [sem(f"weights_landed{s}") for s in range(SLOTS)]

        ring = sb("weight_ring", SLOTS, SLOT)
        const = sb("const", N_CONST)
        x = sb("x", TT, D)
        cols = sb("cols", 400)
        arena = sb("arena", 30720)

        def k(name, *dims):
            at, n = CONST[name]
            v = const[:, at:at + n]
            return v

        class Columns:
            def __init__(self):
                self.at = 0

            def take(self, n):
                self.at += n
                assert self.at <= 400
                return cols[:, self.at - n:self.at]

        cc = Columns()
        c_col = cc.take(2 * KT)
        sc_col = cc.take(2 * KT)
        ada_b = cc.take(48)
        mod = cc.take(96)
        gain = cc.take(2 * KT)
        mixA = cc.take(2 * KT)
        in_b = cc.take(8)
        bs = cc.take(GROUPS)
        small = cc.take(64)
        cols_na = cc.take(NA_STEPS), cc.take(NA_STEPS)
        mbn, mbs = cc.take(TT * H2), cc.take(TT * H2)
        lnm, lnv = cc.take(2 * TT), cc.take(2 * TT)

        def area(at, *dims):
            n = int(np.prod(dims))
            assert at + n <= 30720
            v = arena[:, at:at + n]
            if len(dims) == 2:
                return v.rearrange("p (a b) -> p a b", b=dims[1])
            if len(dims) == 3:
                return v.rearrange("p (a b c) -> p a b c", b=dims[1], c=dims[2])
            return v

        posb = area(0, NH, DR, GRID_W)
        ga, gb, mg = area(0, TT, D), area(2048, TT, D), area(4096, TT, D)
        hT = area(6144, KT, 2 * S)
        oaT, mT = area(6144, KT, S), area(8192, KT, S)
        xn, cn = area(10240, TT, D), area(12288, TT, D)
        v_, u_ = xn, cn
        nqT, nkT, nv = area(14336, 4, S), area(15360, 4, 2 * S), area(17408, 4, NW)
        rows = area(14336, 4, D)
        pr, prT = area(19456, 2, CHUNK), area(20480, 2, CHUNK)
        junk = area(19456, 2048)
        ln_g, ln_b = area(21504, D), area(22528, D)
        wsT = area(23552, GROUPS, P)
        w_tiny = area(24576, D)
        tqkv = area(25600, 4, 3 * TINY)
        tT = area(26368, 6 * P)
        ttT = area(27136, S)
        bias = area(27392, 2, CHUNK)
        ob, obT = area(28416, TT, NW), area(29440, 4, S)
        fin_g = area(28416, D)
        h2, h2T = area(0, TT, D), area(2048, KT, S)
        y = area(4096, TT, D)
        act_ff = area(6144, 2, S)
        ffs = area(6656, 2, S)
        w_rt = area(7168, KT, E)
        rt_b = area(7680, E)
        score, biased, rep, wt = (area(7744 + 128 * i, TT, E) for i in range(4))
        top = area(8256, TT, 8)
        xT = area(0, KT, S)
        qsT, ksT, vs = area(2048, 4, S), area(3072, 4, S), area(4096, TT, W2)
        qk = area(5120, 2, TT, W2)
        qmT, kmT, vm = area(7168, 4, S), area(8192, 4, S), area(9216, TT, W2)
        gates = area(10240, 2, TT, D)
        o = area(14336, 2, TT, W2)
        oT = area(16384, 2, 4 * S)
        lmg, lmT = area(18432, TT, D), area(20480, KT, S)
        ln = area(22528, 4, D)
        es, rw, wT_ = area(26624, 2, CHUNK), area(27648, 2, CHUNK), area(28672, 2, CHUNK)
        rope = area(29696, 4, 128)
        fh = area(2048, FT, S)
        silu = area(26624, 2, S)

        def bank(key):
            return psum[banks[key][0]]

        def wait_bank(eng, key, it=0):
            b, n, per = banks[key]
            if n or per:
                eng.wait_ge(bank_free[b], n + it * per)

        def wait_full(eng, key, it=0):
            b, n, per = banks[key]
            eng.wait_ge(bank_full[b], n + 1 + it * per)

        def wait_out(eng, key, it=0):
            b, n, per = banks[key]
            eng.wait_ge(bank_free[b], n + 1 + it * per)

        def full(ins, key):
            ins.then_inc(bank_full[banks[key][0]], 1)

        def out(ins, key):
            ins.then_inc(bank_free[banks[key][0]], 1)

        def wait_weights(eng, key, it=0):
            s, n, per = units.place[key]
            eng.wait_ge(landed[s], 16 * (n + 1 + it * per))

        def w(key, rows_, cols_):
            s = units.place[key][0]
            return ring[:, s, 0:rows_ * cols_].rearrange("p (k n) -> p k n", n=cols_)

        pieces = [(COL_TQ, 3 * TINY, ("tiny", 3)), (COL_NV, CHUNK, ("nv", 3))]
        for name, col in (("v", COL_V), ("u", COL_U), ("ga", COL_GA), ("gb", COL_GB)):
            for n in range(2):
                pieces.append((col + n * CHUNK, CHUNK, (name, n, 1)))
        piece_of = {p[2][:-1]: i for i, p in enumerate(pieces)}

        def wait_piece(eng, i):
            eng.wait_ge(sem(f"bias_landed{i % 2}"), 16 * (i // 2 + 1))

        block = ctx.enter_context(nc.Block())

        @block.sync
        def _(sp):
            def load(key, it=0):
                s = units.place[key][0]
                for before in units.before[key]:
                    back = before[0] == "previous iteration"
                    job = freed_by[before[1] if back else before]
                    at = (it - 1) if back else it
                    b, n, per = banks[job]
                    if back:
                        assert n + 1 > per, (key, job)
                    if per:
                        sp.wait_ge(bank_full[b], n + 1 + at * per)
                        sp.sem_inc(sem("slots_freed"), 1)
                    else:
                        sp.wait_ge(bank_full[b], n + 1)
                kind, *src = sources[key]
                if kind == "rows":
                    name, col, half = src
                    m = a[name][it] if name.endswith("_2") else a[name]
                    dst = w(key, 4, CHUNK)
                    view = m[half * CHUNK:(half + 1) * CHUNK, col:col + CHUNK]
                elif kind == "half":
                    name, col = src
                    m = a[name][it] if name.endswith("_2") else a[name]
                    dst, view = w(key, 4, CHUNK), m[:, col:col + CHUNK]
                elif kind == "tiny":
                    dst, view = w(key, KT, 3 * TINY), a["w_in"][:, COL_TQ:COL_NQ]
                elif kind == "ff":
                    name, col = src
                    m = a[name][it] if name.endswith("_2") else a[name]
                    dst, view = w(key, KT, FF), m[:, col:col + FF]
                elif kind == "down":
                    name, row = src
                    m = a[name][it] if name.endswith("_2") else a[name]
                    dst, view = w(key, 2, D), m[row:row + FF, :]
                else:
                    view = a[src[0]][it]
                    dst = w(key, 2, D) if src[0] == "w_e_down" else w(key, KT, FF)
                sp.dma_start(dst, view.rearrange("(k p) n -> p k n", p=P)).then_inc(landed[s], 16)

            def is_expert(key):
                return key[0] in ("eg", "eu", "ed")

            sp.dma_start(x[:, :, :], a["x"].rearrange("(t p) d -> p t d", p=P)).then_inc(sem("x_landed"), 16)
            sp.dma_start(cn, a["ctx"].rearrange("(t p) d -> p t d", p=P)).then_inc(sem("ctx_landed"), 16)
            for key in order:
                if not is_expert(key) and key[0] not in LAYER_KEYS:
                    load(key)
            with sp.Fori(0, E) as e:
                for key in order:
                    if is_expert(key):
                        load(key, e)
            with sp.Fori(0, L2) as layer:
                for key in order:
                    if key[0] in LAYER_KEYS:
                        load(key, layer)
            sp.wait_ge(sem("x_new"), TT + 2 * TT * L2)
            sp.dma_start(a["out"].rearrange("(t p) d -> p t d", p=P), x[:, :, :]).then_inc(sem("stored"), 16)
            sp.wait_ge(sem("stored"), 16)

        @block.gpsimd
        def _(pool):
            def bcast(name, at, n):
                return bass.AP(tensor=a[name].tensor, offset=at, ap=[[0, P], [1, n]])

            s = sem("small_landed")
            pool.dma_start(c_col, a["c_cols"]).then_inc(s, 16)
            pool.dma_start(ada_b, a["b_ada_cols"]).then_inc(s, 16)
            pool.dma_start(gain, a["gains"]).then_inc(s, 16)
            pool.dma_start(in_b, a["b_in_cols"]).then_inc(s, 16)
            pool.dma_start(bs, a["b_s_cols"]).then_inc(s, 16)
            pool.dma_start(const[:, :], a["consts"]).then_inc(s, 16)
            for i, (col, n, _) in enumerate(pieces[:2]):
                pool.dma_start(bias[:, i, 0:n], bcast("b_in", col, n)).then_inc(sem(f"bias_landed{i}"), 16)
            width = 2 * NA_COLS - 1
            table = NH * (2 * NA_ROWS - 1) * width
            pool.dma_start(a["rpb_copies"], bass.AP(tensor=a["na_rpb"].tensor, offset=0, ap=[[0, GRID_W], [1, table]]))\
                .then_inc(sem("copies_stored"), 16)
            pool.wait_ge(sem("copies_stored"), 16)
            for half in range(2):
                first = NA_ROWS - 1 - (TT - 1) * 2 - half
                for r in range(DR):
                    pool.dma_start(
                        posb[half * GRID_W:(half + 1) * GRID_W, :, r, :],
                        bass.AP(tensor=a["rpb_copies"].tensor, offset=(first + r) * width + NA_COLS - 1,
                                ap=[[table - 1, GRID_W], [(2 * NA_ROWS - 1) * width, NH], [1, GRID_W]]),
                    ).then_inc(sem("posb_landed"), 16)
            pool.dma_start(ln_g, bcast("sgu_ln_g", 0, D)).then_inc(sem("sgu_landed"), 16)
            pool.dma_start(ln_b, bcast("sgu_ln_b", 0, D)).then_inc(sem("sgu_landed"), 16)
            pool.dma_start(wsT, a["w_sT"]).then_inc(sem("sgu_landed"), 16)
            pool.dma_start(w_tiny[0:TINY, :], a["tiny_w_o"]).then_inc(sem("sgu_landed"), 16)
            pool.wait_ge(s, 16 * 6)
            pool.wait_ge(sem("posb_landed"), 16 * 2 * DR)
            flat = posb.rearrange("p h r c -> p (h r) c")
            nc.gpsimd.tensor_tensor(flat, flat, k("window").unsqueeze(1).to_broadcast([P, NH * DR, GRID_W]),
                                    ALU.add).then_inc(sem("posb_ready"), 1)
            for i, (col, n, _) in enumerate(pieces):
                if i >= 2:
                    wait_out(pool, pieces[i - 2][2])
                    pool.dma_start(bias[:, i % 2, 0:n], bcast("b_in", col, n)).then_inc(sem(f"bias_landed{i % 2}"), 16)
            wait_out(pool, ("oaT", 3))
            wait_out(pool, ("obT", 1))
            pool.dma_start(fin_g, bcast("final_norm_g", 0, D)).then_inc(sem("fin_landed"), 16)
            wait_out(pool, ("h2T", 3))
            pool.dma_start(w_rt, a["w_router"].rearrange("(k p) n -> p k n", p=P)).then_inc(sem("router_landed"), 16)
            pool.dma_start(rt_b, bcast("b_router", 0, E)).then_inc(sem("router_landed"), 16)
            with pool.Fori(0, L2) as layer:
                pool.wait_ge(sem("x_new"), TT + 2 * TT * layer)
                for j, name in enumerate(("ln_mix_g_2", "ln_mix_b_2", "ln_ffn_g_2", "ln_ffn_b_2")):
                    row = a[name][layer]
                    pool.dma_start(ln[:, j, :], row.partition_broadcast(P)).then_inc(sem("ln_landed"), 16)

        def wait_weights_of_item(eng, i, it):
            if i < NI:
                eng.wait_ge(sem("stick_weights"), NI * it + i + 1)
            else:
                wait_out(eng, ("sc", i), it)

        @block.tensor
        def _(pe):
            mm = nc.tensor.matmul

            def turn(dst, src, m=P):
                return nc.tensor.transpose(dst, src, k("ident")[0:m, 0:m])

            def turns(key, pieces_, it=0):
                wait_bank(pe, key, it)
                for j, src in enumerate(pieces_):
                    last = turn(bank(key)[0:src.shape[1], j * P:(j + 1) * P], src)
                full(last, key)

            def turn_tiles(key, src, g, it=0):
                turns(key, [src[:, t, (2 * g + j) * P:(2 * g + j + 1) * P] for j in range(2) for t in range(TT)], it)

            def token_major(key, left, t, units_, kts, it=0, cols_=CHUNK, done=True):
                wait_bank(pe, key, it)
                n = 0
                for uk in units_:
                    wait_weights(pe, uk, it)
                    wv = w(uk, kts, cols_)
                    for j in range(kts):
                        last = mm(bank(key)[:, 0:cols_], left[:, n, t * P:(t + 1) * P], wv[:, j, :],
                                  start=(n == 0), stop=(n == kts * len(units_) - 1))
                        n += 1
                full(last, key)

            def feature_major(key, right, tokens, units_, fts, it=0):
                wait_bank(pe, key, it)
                for s_, f in enumerate(fts):
                    for n in range(KT):
                        uk = units_[n // 4]
                        if s_ == 0 and n % 4 == 0:
                            wait_weights(pe, uk, it)
                        last = mm(bank(key)[:, s_ * tokens:(s_ + 1) * tokens],
                                  w(uk, 4, CHUNK)[:, n % 4, f * P:(f + 1) * P], right[:, n, 0:tokens],
                                  start=(n == 0), stop=(n == KT - 1))
                full(last, key)

            def both(key):
                return [key + (0,), key + (1,)]

            def modulation(job, chunks):
                wait_bank(pe, job)
                for i, n in enumerate(chunks):
                    for u in both(("ada", n)):
                        wait_weights(pe, u)
                    for f in range(4):
                        for kt in range(KT):
                            at = 2 * (4 * i + f)
                            last = mm(bank(job)[:, at:at + 2], w(("ada", n, kt // 4), 4, CHUNK)[:, kt % 4, f * P:(f + 1) * P],
                                      sc_col[:, 2 * kt:2 * kt + 2], start=(kt == 0), stop=(kt == KT - 1))
                full(last, job)

            pe.wait_ge(sem("silu_ready"), 1)
            modulation(("mod", 0), range(4))
            for g in range(4):
                pe.wait_ge(sem("x_normed"), 2 * TT)
                turn_tiles(("xT", g), xn, g)
                turn_tiles(("cT", g), cn, g)
            for g in range(4):
                wait_out(pe, ("xT", g))
                wait_out(pe, ("cT", g))
            for t in range(4):
                token_major(("tiny", t), hT, t, [("win", "tiny")], KT, cols_=3 * TINY)
            for p in range(2):
                feature_major(("nq", p), hT, S, both(("win", "nq")), (2 * p, 2 * p + 1))
            for f in range(4):
                feature_major(("nk", f), hT, 2 * S, both(("win", "nk")), (f,))
            for t in range(4):
                token_major(("nv", t), hT, t, both(("win", "nv")), 4)
            pe.wait_ge(sem("tiny_roped"), 1)
            turns(("tqT", 0), [tqkv[:, t, 0:TINY] for t in range(TT)])
            turns(("tkT", 0), [tqkv[:, t, TINY:2 * TINY] for t in range(4)])
            wait_out(pe, ("tqT", 0))
            wait_out(pe, ("tkT", 0))
            for t in range(TT):
                wait_bank(pe, ("ts", t))
                full(mm(bank(("ts", t))[:, :], tT[0:TINY, t * P:(t + 1) * P], tT[0:TINY, S:S + CHUNK],
                        start=True, stop=True), ("ts", t))
            for t in range(TT):
                pe.wait_ge(sem("tiny_probs"), t + 1)
                turns(("tpT", t), [pr[:, t, j * P:(j + 1) * P] for j in range(4)])
                wait_out(pe, ("tpT", t))
                wait_bank(pe, ("tO", t))
                for j in range(4):
                    last = mm(bank(("tO", t))[0:TINY, 0:P], tqkv[:, j, 2 * TINY:3 * TINY],
                              prT[:, t, j * P:(j + 1) * P], start=(j == 0), stop=(j == 3))
                full(last, ("tO", t))

            fill = [(name, n, t) for name in "vu" for n in range(2) for t in range(TT)]
            for p in range(2):
                wait_out(pe, ("nq", p))
            for f in range(4):
                wait_out(pe, ("nk", f))
            for t in range(4):
                wait_out(pe, ("nv", t))
            for i in range(NA_STEPS + 2):
                if i < NA_STEPS:
                    t, h = divmod(i, NH)
                    r = h % 4 * NDH
                    wait_bank(pe, ("ns", i))
                    full(mm(bank(("ns", i))[:, :], nqT[r:r + NDH, h // 4, t * P:(t + 1) * P],
                            nkT[r:r + NDH, h // 4, :], start=True, stop=True), ("ns", i))
                if i % 4 == 1 and i // 4 < len(fill):
                    name, n, t = fill[i // 4]
                    token_major((name, n, t), hT, t, both(("win", name, n)), 4)
                if 1 <= i <= NA_STEPS:
                    wait_out(pe, ("ns", i - 1))
                    turns(("npT", i - 1), [pr[:, (i - 1) % 2, j * P:(j + 1) * P] for j in range(4)])
                if i >= 2:
                    t, h = divmod(i - 2, NH)
                    wait_out(pe, ("npT", i - 2))
                    if h == 0:
                        wait_bank(pe, ("nO", t))
                    for j in range(4):
                        last = mm(bank(("nO", t))[:, h * NDH:(h + 1) * NDH], prT[:, (i - 2) % 2, j * P:(j + 1) * P],
                                  nv[:, j, h * NDH:(h + 1) * NDH], start=(j == 0), stop=(j == 3))
                    last.then_inc(sem("na_summed"), 1)
            for name in ("ga", "gb"):
                for n in range(2):
                    for t in range(TT):
                        token_major((name, n, t), hT, t, both(("win", name, n)), 4)
            for v in range(4):
                modulation(("mod", v + 1), (4 + 2 * v, 5 + 2 * v))
            for v in range(4):
                for n in range(2):
                    key = ("row", v, n)
                    pe.wait_ge(sem("diag_ready"), 2 * v + n + 1)
                    wait_bank(pe, key)
                    full(mm(bank(key)[:, :], k("ones"), mg[:, n, (v % 2) * CHUNK:(v % 2 + 1) * CHUNK],
                            start=True, stop=True), key)
            pe.wait_ge(sem("sgu_landed"), 64)
            for t in range(TT):
                wait_out(pe, ("tO", t))
                pe.wait_ge(sem("v_normed"), t + 1)
                for n in range(2):
                    key = ("sg", t, n)
                    wait_bank(pe, key)
                    for g in range(4):
                        at = (4 * n + g) * P
                        mm(bank(key)[:, g * P:(g + 1) * P], ttT[0:TINY, t * P:(t + 1) * P], w_tiny[0:TINY, at:at + P],
                           start=True, stop=False)
                        last = mm(bank(key)[:, g * P:(g + 1) * P], wsT[:, 4 * n + g, :], v_[:, t, at:at + P],
                                  start=False, stop=True)
                    full(last, key)
            for t in range(TT):
                for n in range(2):
                    wait_out(pe, ("sg", t, n))
            for g in range(4):
                turn_tiles(("oaT", g), u_, g)
            for t in range(TT):
                wait_out(pe, ("nO", t))
            for g in range(2):
                turn_tiles(("obT", g), ob, g)
            for g in range(4):
                wait_out(pe, ("oaT", g))
            for g in range(2):
                wait_out(pe, ("obT", g))
            for n in range(2):
                for t in range(TT):
                    token_major(("upa", n, t), oaT, t, both(("upa", n)), 4)
                    token_major(("upb", n, t), obT, t, [("upb", n)], 4)
            pe.wait_ge(sem("merged"), 2 * TT)
            for g in range(4):
                turn_tiles(("mT", g), mg, g)
            for g in range(4):
                wait_out(pe, ("mT", g))
            for n in range(2):
                for t in range(TT):
                    token_major(("wo", n, t), mT, t, both(("wo", n)), 4)
            pe.wait_ge(sem("h2_ready"), TT)
            for g in range(4):
                turn_tiles(("h2T", g), h2, g)
            for g in range(4):
                wait_out(pe, ("h2T", g))
            pe.wait_ge(sem("router_landed"), 32)
            for t in range(TT):
                wait_bank(pe, ("rt", t))
                for kt in range(KT):
                    last = mm(bank(("rt", t))[:, 0:E], h2T[:, kt, t * P:(t + 1) * P], w_rt[:, kt, :],
                              start=(kt == 0), stop=(kt == KT - 1))
                full(last, ("rt", t))

            def gate_up(key, right, gk, uk, f, f_in_unit, it=0):
                wait_bank(pe, key, it)
                for j, unit_key in enumerate((gk, uk)):
                    wait_weights(pe, unit_key, it)
                    for kt in range(KT):
                        last = mm(bank(key)[:, j * S:(j + 1) * S], w(unit_key, KT, FF)[:, kt, f_in_unit * P:(f_in_unit + 1) * P],
                                  right[:, kt, :], start=(kt == 0), stop=(kt == KT - 1))
                full(last, key)

            def expert(gk, uk, dk, gj, dj, hidden, it=0):
                for f in range(2):
                    gate_up((gj, f), h2T, gk, uk, f, f, it)
                for f in range(2):
                    wait_out(pe, (gj, f), it)
                wait_weights(pe, dk, it)
                for n in range(2):
                    for t in range(TT):
                        key = (dj, n, t)
                        wait_bank(pe, key, it)
                        for f in range(2):
                            last = mm(bank(key)[:, :], hidden[:, f, t * P:(t + 1) * P],
                                      w(dk, 2, D)[:, f, n * CHUNK:(n + 1) * CHUNK], start=(f == 0), stop=(f == 1))
                        full(last, key)

            expert(("shg",), ("shu",), ("shd",), "shg", "shd", ffs)
            with pe.Fori(0, E) as e:
                expert(("eg",), ("eu",), ("ed",), "eg", "ed", ffs, e)

            with pe.Fori(0, L2) as layer:
                pe.wait_ge(sem("x_new"), TT + 2 * TT * layer)
                for g in range(4):
                    turn_tiles(("l_xT", g), x, g, layer)
                for g in range(4):
                    wait_out(pe, ("l_xT", g), layer)
                for name in ("qs", "ks"):
                    for p in range(2):
                        feature_major((name, p), xT, S, both(("l_in", name)), (2 * p, 2 * p + 1), layer)
                for t in range(TT):
                    token_major(("vs", t), xT, t, both(("l_in", "vs")), 4, layer)
                for name in ("qs", "ks", "vs"):
                    for p in range(2):
                        wait_out(pe, (name, p), layer)
                for i in range(2 * NI + 2):
                    if i < 2 * NI:
                        b = i // NI
                        if i == NI:
                            for name in ("qmT", "kmT"):
                                for p in range(2):
                                    wait_out(pe, (name, p), layer)
                            for t in range(TT):
                                wait_out(pe, ("vm", 0, t), layer)
                        t, h0, nh, keys = ITEMS[i % NI]
                        q, kk = ((qsT, ksT), (qmT, kmT))[b]
                        wait_bank(pe, ("sc", i), layer)
                        for j in range(nh):
                            h = HEAD[h0 + j]
                            r = h % 2 * DH2
                            last = mm(bank(("sc", i))[:, j * keys:(j + 1) * keys], q[r:r + DH2, h // 2, t * P:(t + 1) * P],
                                      kk[r:r + DH2, h // 2, 0:keys], start=True, stop=True)
                        full(last, ("sc", i))
                    if i < len(FILLERS):
                        name, n, t = FILLERS[i]
                        token_major((name, n, t), xT, t, both(("l_in", name, n)), 4, layer)
                    if 1 <= i <= 2 * NI:
                        wait_weights_of_item(pe, i - 1, layer)
                        turns(("wT", i - 1), [rw[:, (i - 1) % 2, j * P:(j + 1) * P] for j in range(4)], layer)
                    if i >= 2:
                        b, (t, h0, nh, keys) = (i - 2) // NI, ITEMS[(i - 2) % NI]
                        wait_out(pe, ("wT", i - 2), layer)
                        if h0 == 0:
                            wait_bank(pe, ("o", b, t), layer)
                        val = (vs, vm)[b]
                        kts = keys // P
                        for j in range(nh):
                            h, to = HEAD[h0 + j], (h0 + j) * DH2
                            for kt in range(kts):
                                at = (j * kts + kt) * P
                                last = mm(bank(("o", b, t))[:, to:to + DH2], wT_[:, i % 2, at:at + P],
                                          val[:, kt, h * DH2:(h + 1) * DH2], start=(kt == 0), stop=(kt == kts - 1))
                        last.then_inc(sem("item_summed"), 1)
                    if i == NI - 1:
                        pe.wait_ge(sem("roped"), 2 * TT * (layer + 1))
                        for which, name in enumerate(("qmT", "kmT")):
                            for p in range(2):
                                turn_tiles((name, p), qk[:, which], p, layer)
                for b in range(2):
                    for t in range(TT):
                        wait_out(pe, ("o", b, t), layer)
                    for p in range(2):
                        turn_tiles(("oT", b, p), o[:, b], p, layer)
                for b in range(2):
                    for p in range(2):
                        wait_out(pe, ("oT", b, p), layer)
                ot = [oT[:, b, :].rearrange("p (f t) -> p f t", t=S) for b in range(2)]
                for n in range(2):
                    for t in range(TT):
                        token_major(("bs", n, t), ot[0], t, [("bs", n)], 4, layer)
                        token_major(("bm", n, t), ot[1], t, [("bm", n)], 4, layer)
                pe.wait_ge(sem("l_merged"), 2 * TT * (layer + 1))
                for g in range(4):
                    turn_tiles(("l_mT", g), lmg, g, layer)
                for g in range(4):
                    wait_out(pe, ("l_mT", g), layer)
                for n in range(2):
                    for t in range(TT):
                        token_major(("l_wo", n, t), lmT, t, both(("l_wo", n)), 4, layer)
                pe.wait_ge(sem("x_new"), 2 * TT + 2 * TT * layer)
                for g in range(4):
                    turn_tiles(("l_yT", g), x, g, layer)
                for g in range(4):
                    wait_out(pe, ("l_yT", g), layer)
                for pair in range(FT // 2 + 1):
                    if pair < FT // 2:
                        for f in range(2):
                            gate_up(("fg", 2 * pair + f), xT, ("fg", pair), ("fu", pair), f, f, layer)
                    if pair:
                        d = pair - 1
                        for f in (2 * d, 2 * d + 1):
                            wait_out(pe, ("fg", f), layer)
                        wait_weights(pe, ("fd", d), layer)
                        for n in range(2):
                            for t in range(TT):
                                key = ("fd", n, t)
                                if d == 0:
                                    wait_bank(pe, key, layer)
                                for f in range(2):
                                    last = mm(bank(key)[:, :], fh[:, 2 * d + f, t * P:(t + 1) * P],
                                              w(("fd", d), 2, D)[:, f, n * CHUNK:(n + 1) * CHUNK],
                                              start=(d == 0 and f == 0), stop=(d == FT // 2 - 1 and f == 1))
                                if d == FT // 2 - 1:
                                    full(last, key)

        @block.scalar
        def _(act):
            A = nc.scalar.activation
            act.wait_ge(sem("small_landed"), 16 * 6)
            A(sc_col, c_col, ACT.Silu).then_inc(sem("silu_ready"), 1)
            act.wait_ge(sem("norm_sums"), 1)
            A(small[:, 4:8], small[:, 0:4], ACT.Sqrt).then_inc(sem("norm_roots"), 1)
            act.wait_ge(sem("mix_scale"), 1)
            for g in range(4):
                wait_full(act, ("cT", g))
                for j in range(2):
                    ft = 2 * g + j
                    last = A(hT[:, ft, S:2 * S], bank(("cT", g))[:, j * S:(j + 1) * S], ACT.Identity,
                             bias=mod[:, 2 * ft + 1:2 * ft + 2], scale=mixA[:, 2 * ft + 1:2 * ft + 2])
                out(last, ("cT", g))
            for f in range(4):
                wait_full(act, ("nk", f))
                out(A(nkT[:, f, :], bank(("nk", f))[:, :], ACT.Identity, bias=in_b[:, 4 + f:5 + f]), ("nk", f))
            wait_full(act, ("tqT", 0))
            out(A(tT[0:TINY, 0:S], bank(("tqT", 0))[0:TINY, 0:S], ACT.Copy), ("tqT", 0))
            wait_full(act, ("tkT", 0))
            out(A(tT[0:TINY, S:S + CHUNK], bank(("tkT", 0))[0:TINY, :], ACT.Copy), ("tkT", 0))
            for t in range(TT):
                act.wait_ge(sem("tiny_max"), t + 1)
                out(A(pr[:, t, :], bank(("ts", t))[:, :], ACT.Exp, bias=small[:, 10 + t:11 + t], scale=TINY ** -0.5,
                      accum_out=small[:, 12 + t:13 + t]), ("ts", t))
            for t in range(TT):
                wait_full(act, ("tpT", t))
                out(A(prT[:, t, :], bank(("tpT", t))[:, :], ACT.Copy), ("tpT", t))
                wait_full(act, ("tO", t))
                out(A(ttT[0:TINY, t * P:(t + 1) * P], bank(("tO", t))[0:TINY, 0:P], ACT.Copy), ("tO", t))
            for i in range(NA_STEPS + 1):
                if i < NA_STEPS:
                    act.wait_ge(sem("na_max"), i + 1)
                    if i >= 2:
                        wait_full(act, ("npT", i - 2))
                    out(A(pr[:, i % 2, :], bank(("ns", i))[:, :], ACT.Exp, bias=cols_na[0][:, i:i + 1],
                          accum_out=cols_na[1][:, i:i + 1]), ("ns", i))
                if i >= 1:
                    j = i - 1
                    wait_full(act, ("npT", j))
                    if j >= 2:
                        act.wait_ge(sem("na_summed"), j - 1)
                    out(A(prT[:, j % 2, :], bank(("npT", j))[:, :], ACT.Copy), ("npT", j))
            for which, (buf, name) in enumerate(((v_, "v"), (u_, "u"))):
                for t in range(TT):
                    for n in range(2):
                        wait_out(act, (name, n, t))
                    A(buf[:, t, :], buf[:, t, :], ACT.Gelu).then_inc(sem("gelu_done"), 1)
            act.wait_ge(sem("v_var"), 1)
            A(small[:, 20:22], small[:, 18:20], ACT.Sqrt).then_inc(sem("v_root"), 1)
            for buf, name in ((ga, "ga"), (gb, "gb")):
                for t in range(TT):
                    for n in range(2):
                        wait_out(act, (name, n, t))
                    A(buf[:, t, :], buf[:, t, :], ACT.Sigmoid).then_inc(sem("gates_done"), 1)
            for g in range(4):
                wait_full(act, ("oaT", g))
                out(A(oaT[:, 2 * g:2 * g + 2, :].rearrange("p a b -> p (a b)"), bank(("oaT", g))[:, :], ACT.Copy), ("oaT", g))
            for g in range(2):
                wait_full(act, ("obT", g))
                out(A(obT[:, 2 * g:2 * g + 2, :].rearrange("p a b -> p (a b)"), bank(("obT", g))[:, :], ACT.Copy), ("obT", g))
            for g in range(4):
                wait_full(act, ("mT", g))
                out(A(mT[:, 2 * g:2 * g + 2, :].rearrange("p a b -> p (a b)"), bank(("mT", g))[:, :], ACT.Copy), ("mT", g))
            act.wait_ge(sem("sums2"), 1)
            A(small[:, 26:28], small[:, 24:26], ACT.Sqrt).then_inc(sem("roots2"), 1)
            for g in range(4):
                wait_full(act, ("h2T", g))
                out(A(h2T[:, 2 * g:2 * g + 2, :].rearrange("p a b -> p (a b)"), bank(("h2T", g))[:, :], ACT.Copy), ("h2T", g))
            for t in range(TT):
                wait_full(act, ("rt", t))
                out(A(score[:, t, :], bank(("rt", t))[:, 0:E], ACT.Sigmoid), ("rt", t))

            def silus(job, it=0):
                for f in range(2):
                    wait_full(act, (job, f), it)
                    A(act_ff[:, f, :], bank((job, f))[:, 0:S], ACT.Silu).then_inc(sem("silu_done"), 1)

            silus("shg")
            with act.Fori(0, E) as e:
                silus("eg", e)
            act.wait_ge(sem("sums3"), 1)
            A(small[:, 34:36], small[:, 32:34], ACT.Sqrt).then_inc(sem("roots3"), 1)

            with act.Fori(0, L2) as layer:
                for g in range(4):
                    wait_full(act, ("l_xT", g), layer)
                    out(A(xT[:, 2 * g:2 * g + 2, :].rearrange("p a b -> p (a b)"), bank(("l_xT", g))[:, :], ACT.Copy), ("l_xT", g))
                for p in range(2):
                    wait_full(act, ("ks", p), layer)
                    out(A(ksT[:, 2 * p:2 * p + 2, :].rearrange("p a b -> p (a b)"), bank(("ks", p))[:, :], ACT.Copy), ("ks", p))
                for i in range(2 * NI + 3):
                    if 1 <= i <= len(FILLERS):
                        name, n, t = FILLERS[i - 1]
                        if name in ("gs", "gm"):
                            wait_full(act, (name, n, t), layer)
                            out(A(gates[:, ("gs", "gm").index(name), t, n * CHUNK:(n + 1) * CHUNK],
                                  bank((name, n, t))[:, :], ACT.Exp, scale=-1.0), (name, n, t))
                    if 2 <= i <= 2 * NI + 1:
                        j = i - 2
                        wait_full(act, ("wT", j), layer)
                        act.wait_ge(sem("item_summed"), 2 * NI * layer + j - 1) if j >= 2 else None
                        out(A(wT_[:, j % 2, :], bank(("wT", j))[:, :], ACT.Copy), ("wT", j))
                    if i == NI:
                        for name, dst in (("qmT", qmT), ("kmT", kmT)):
                            for p in range(2):
                                wait_full(act, (name, p), layer)
                                out(A(dst[:, 2 * p:2 * p + 2, :].rearrange("p a b -> p (a b)"), bank((name, p))[:, :],
                                      ACT.Copy), (name, p))
                    if i < NI:
                        wait_full(act, ("sc", i), layer)
                        A(es[:, i % 2, :], bank(("sc", i))[:, :], ACT.Abs).then_inc(sem("abs_ready"), 1)
                        act.wait_ge(sem("abs_ready"), NI * layer + i + 1)
                        A(es[:, i % 2, :], es[:, i % 2, :], ACT.Exp, scale=-1.0).then_inc(sem("exp_done"), 1)
                        act.wait_ge(sem("exp_done"), NI * layer + i + 1)
                        A(es[:, i % 2, :], es[:, i % 2, :], ACT.Ln, bias=1.0).then_inc(sem("ln_done"), 1)
                    if NI <= i < 2 * NI:
                        t, h0, nh, keys = ITEMS[i - NI]
                        act.wait_ge(sem("mb_max"), NI * layer + i - NI + 1)
                        if i >= 2:
                            wait_full(act, ("wT", i - 2), layer)
                        for j in range(nh):
                            hh = t * H2 + h0 + j
                            last = A(rw[:, i % 2, j * keys:(j + 1) * keys], bank(("sc", i))[:, j * keys:(j + 1) * keys],
                                     ACT.Exp, bias=mbn[:, hh:hh + 1], accum_out=mbs[:, hh:hh + 1])
                        out(last, ("sc", i))
                    if 1 <= i <= NI:
                        act.wait_ge(sem("log_weights"), NI * layer + i)
                        A(rw[:, (i - 1) % 2, :], rw[:, (i - 1) % 2, :], ACT.Exp).then_inc(sem("stick_weights"), 1)
                for b in range(2):
                    for p in range(2):
                        wait_full(act, ("oT", b, p), layer)
                        out(A(oT[:, b, p * CHUNK:(p + 1) * CHUNK], bank(("oT", b, p))[:, :], ACT.Copy), ("oT", b, p))
                for g in range(4):
                    wait_full(act, ("l_mT", g), layer)
                    out(A(lmT[:, 2 * g:2 * g + 2, :].rearrange("p a b -> p (a b)"), bank(("l_mT", g))[:, :], ACT.Copy), ("l_mT", g))
                act.wait_ge(sem("l_var"), 2 * layer + 1)
                A(lnv[:, 2:4], lnv[:, 0:2], ACT.Sqrt).then_inc(sem("l_root"), 1)
                for g in range(4):
                    wait_full(act, ("l_yT", g), layer)
                    out(A(xT[:, 2 * g:2 * g + 2, :].rearrange("p a b -> p (a b)"), bank(("l_yT", g))[:, :], ACT.Copy), ("l_yT", g))
                for f in range(FT):
                    wait_full(act, ("fg", f), layer)
                    if f >= 2:
                        wait_out(act, ("fg", f - 2), layer)
                    A(silu[:, f % 2, :], bank(("fg", f))[:, 0:S], ACT.Silu).then_inc(sem("l_silu"), 1)
                act.wait_ge(sem("l_var"), 2 * layer + 2)
                A(lnv[:, 2:4], lnv[:, 0:2], ACT.Sqrt).then_inc(sem("l_root"), 1)

        @block.vector
        def _(dve):
            V = nc.vector
            own = sem("vector_step")
            count = [0, 0, 0]

            def step(ins, it=0):
                ins.then_inc(own, 1)
                count[0] += 1
                return ins

            def settle(it=None):
                dve.wait_ge(own, count[0] if it is None else count[0] + it * count[2])

            def rms(src, at, slot):
                for t in range(TT):
                    step(V.tensor_tensor_reduce(junk[:, 0:D], src[:, t, :], src[:, t, :], 1.0 / D, NORM_EPS,
                                                ALU.mult, ALU.add, small[:, at + t:at + t + 1]))
                    settle()

            dve.wait_ge(sem("x_landed"), 16)
            rms(x, 0, 0)
            dve.wait_ge(sem("ctx_landed"), 16)
            rms(cn, 2, 0)
            step(V.tensor_copy(small[:, 0:4], small[:, 0:4]))
            settle()
            V.tensor_copy(small[:, 0:4], small[:, 0:4]).then_inc(sem("norm_sums"), 1)
            dve.wait_ge(sem("norm_roots"), 1)
            step(V.reciprocal(small[:, 4:8], small[:, 4:8]))
            settle()
            for t in range(TT):
                V.tensor_scalar(xn[:, t, :], x[:, t, :], small[:, 4 + t:5 + t], None, ALU.mult).then_inc(sem("x_normed"), 1)
                V.tensor_scalar(cn[:, t, :], cn[:, t, :], small[:, 6 + t:7 + t], None, ALU.mult).then_inc(sem("x_normed"), 1)

            dve.wait_ge(sem("small_landed"), 16 * 6)
            wait_full(dve, ("mod", 0))
            m3 = mod.rearrange("p (f w) -> p f w", w=2)

            def add_bias(key, f0, nf):
                out(V.tensor_tensor(m3[:, f0:f0 + nf, :], bank(key)[:, 0:2 * nf].rearrange("p (f w) -> p f w", w=2),
                                    ada_b[:, f0:f0 + nf].unsqueeze(2).to_broadcast([P, nf, 2]), ALU.add), key)
                wait_out(dve, key)

            add_bias(("mod", 0), 0, 16)
            step(V.tensor_scalar(mixA, mod[:, 2 * KT:4 * KT], 1.0, None, ALU.add))
            settle()
            a3 = mixA.rearrange("p (f w) -> p f w", w=2)
            V.tensor_tensor(a3, a3, gain[:, 0:KT].unsqueeze(2).to_broadcast([P, KT, 2]), ALU.mult).then_inc(sem("mix_scale"), 1)
            dve.wait_ge(sem("mix_scale"), 1)
            for g in range(4):
                wait_full(dve, ("xT", g))
                for j in range(2):
                    ft = 2 * g + j
                    last = V.tensor_scalar(hT[:, ft, 0:S], bank(("xT", g))[:, j * S:(j + 1) * S],
                                           mixA[:, 2 * ft:2 * ft + 1], mod[:, 2 * ft:2 * ft + 1], ALU.mult, ALU.add)
                    if j == 0:
                        step(last)
                out(last, ("xT", g))

            def biased_out(key, dst, n=CHUNK, lo=0):
                wait_full(dve, key)
                i = piece_of[key[:-1]]
                wait_piece(dve, i)
                out(V.tensor_tensor(dst, bank(key)[:, lo:n], bias[:, i % 2, lo:n], ALU.add), key)

            for t in range(4):
                lo = 0 if t < TT else TINY
                biased_out(("tiny", t), tqkv[:, t, lo:], 3 * TINY, lo)
            for p in range(2):
                wait_full(dve, ("nq", p))
                for j in range(2):
                    f = 2 * p + j
                    last = V.tensor_scalar(nqT[:, f, :], bank(("nq", p))[:, j * S:(j + 1) * S], in_b[:, f:f + 1],
                                           NDH ** -0.5, ALU.add, ALU.mult)
                    if j == 0:
                        step(last)
                out(last, ("nq", p))
            for t in range(TT):
                wait_out(dve, ("tiny", t))
                v4 = tqkv[:, t, 0:2 * TINY].rearrange("p (wa s f) -> p wa s f", s=2, f=16)
                x1, x2 = v4[:, :, 0, :], v4[:, :, 1, :]

                def table(name):
                    tab = k(name)[:, t * 32:(t + 1) * 32].rearrange("p (a f) -> p a f", f=16)
                    return tab

                tmp = [junk[:, j * 64:(j + 1) * 64].rearrange("p (wa f) -> p wa f", f=16) for j in range(4)]
                for j, (src, name) in enumerate(((x1, "tcos"), (x2, "tsin"), (x2, "tcos"), (x1, "tsin"))):
                    for wh in range(2):
                        step(V.tensor_tensor(tmp[j][:, 2 * wh:2 * wh + 2, :], src[:, 2 * wh:2 * wh + 2, :], table(name), ALU.mult))
                settle()
                step(V.tensor_tensor(x1, tmp[0], tmp[1], ALU.subtract))
                last = V.tensor_tensor(x2, tmp[2], tmp[3], ALU.add)
                if t == 0:
                    step(last)
                    settle()
            last.then_inc(sem("tiny_roped"), 1)
            for t in range(4):
                biased_out(("nv", t), nv[:, t, :])
            for t in range(TT):
                wait_full(dve, ("ts", t))
                step(V.tensor_reduce(small[:, 8 + t:9 + t], bank(("ts", t))[:, :], AX_X, ALU.max))
                settle()
                V.tensor_scalar(small[:, 10 + t:11 + t], small[:, 8 + t:9 + t], -TINY ** -0.5, None, ALU.mult).then_inc(sem("tiny_max"), 1)
            for t in range(TT):
                wait_out(dve, ("ts", t))
                step(V.reciprocal(small[:, 14 + t:15 + t], small[:, 12 + t:13 + t]))
                settle()
                V.tensor_scalar(pr[:, t, :], pr[:, t, :], small[:, 14 + t:15 + t], None, ALU.mult).then_inc(sem("tiny_probs"), 1)

            def na_out(t):
                dve.wait_ge(sem("na_summed"), NH * (t + 1))
                step(V.reciprocal(cols_na[1][:, t * NH:(t + 1) * NH], cols_na[1][:, t * NH:(t + 1) * NH]))
                settle()
                out(V.tensor_tensor(ob[:, t, :].rearrange("p (h d) -> p h d", d=NDH),
                                    bank(("nO", t))[:, :].rearrange("p (h d) -> p h d", d=NDH),
                                    cols_na[1][:, t * NH:(t + 1) * NH].unsqueeze(2).to_broadcast([P, NH, NDH]),
                                    ALU.mult), ("nO", t))

            dve.wait_ge(sem("posb_ready"), 1)
            fill = [(name, n, t) for name in "vu" for n in range(2) for t in range(TT)]
            for i in range(NA_STEPS + 1):
                if i < NA_STEPS:
                    t, h = divmod(i, NH)
                    wait_full(dve, ("ns", i))
                    lat = bank(("ns", i))[:, 0:S]
                    r0 = 2 * (TT - 1 - t)
                    step(V.tensor_tensor(lat, lat, posb[:, h, r0:r0 + ROWS, :].rearrange("p r c -> p (r c)"), ALU.add))
                    settle()
                    step(V.tensor_reduce(cols_na[0][:, i:i + 1], bank(("ns", i))[:, :], AX_X, ALU.max))
                    settle()
                    V.tensor_scalar(cols_na[0][:, i:i + 1], cols_na[0][:, i:i + 1], -1.0, None, ALU.mult).then_inc(sem("na_max"), 1)
                if i % 4 == 2 and i // 4 < len(fill):
                    name, n, t = fill[i // 4]
                    biased_out((name, n, t), (v_ if name == "v" else u_)[:, t, n * CHUNK:(n + 1) * CHUNK])
                if i == NH + 2:
                    na_out(0)
            na_out(1)
            for name, buf in (("ga", ga), ("gb", gb)):
                for n in range(2):
                    for t in range(TT):
                        biased_out((name, n, t), buf[:, t, n * CHUNK:(n + 1) * CHUNK])
            for t in range(TT):
                dve.wait_ge(sem("gelu_done"), t + 1)
                for n in range(2):
                    step(V.bn_stats(small[:, 40 + 6 * n:46 + 6 * n], v_[:, t, n * CHUNK:(n + 1) * CHUNK]))
                settle()
                step(V.bn_aggr(small[:, 52 + 2 * t:54 + 2 * t], small[:, 40:52]))
                settle()
            for t in range(TT):
                last = V.tensor_scalar(small[:, 18 + t:19 + t], small[:, 53 + 2 * t:54 + 2 * t], NORM_EPS, None, ALU.add)
                if t == 0:
                    step(last)
            last.then_inc(sem("v_var"), 1)
            dve.wait_ge(sem("v_root"), 1)
            step(V.reciprocal(small[:, 20:22], small[:, 20:22]))
            settle()
            dve.wait_ge(sem("sgu_landed"), 64)
            for t in range(TT):
                step(V.tensor_scalar(v_[:, t, :], v_[:, t, :], small[:, 52 + 2 * t:53 + 2 * t], small[:, 20 + t:21 + t],
                                     ALU.subtract, ALU.mult))
                settle()
                step(V.tensor_tensor(v_[:, t, :], v_[:, t, :], ln_g, ALU.mult))
                settle()
                V.tensor_tensor(v_[:, t, :], v_[:, t, :], ln_b, ALU.add).then_inc(sem("v_normed"), 1)
            for v in range(4):
                wait_full(dve, ("mod", v + 1))
                add_bias(("mod", v + 1), 16 + KT * v, KT)
            sc_ffn = m3[:, 32:40, 0]
            step(V.tensor_scalar(sc_ffn, sc_ffn, 1.0, None, ALU.add))
            settle()
            step(V.tensor_tensor(sc_ffn, sc_ffn, gain[:, KT:2 * KT], ALU.mult))
            settle()
            for v, f0 in enumerate((16, 40, 32, 24)):
                for n in range(2):
                    if v >= 2:
                        wait_full(dve, ("row", v - 2, n))
                    for j in range(4):
                        f = f0 + 4 * n + j
                        at = (v % 2) * CHUNK + j * P
                        last = V.tensor_scalar(mg[:, n, at:at + P], k("ident"), m3[:, f, 0:1], None, ALU.mult)
                        if j < 3:
                            step(last)
                    last.then_inc(sem("diag_ready"), 1)
                    if v >= 1:
                        wait_full(dve, ("row", v - 1, n))
                        out(V.tensor_copy(rows[:, v - 1, n * CHUNK:(n + 1) * CHUNK], bank(("row", v - 1, n))[:, :]), ("row", v - 1, n))
            for n in range(2):
                wait_full(dve, ("row", 3, n))
                out(V.tensor_copy(rows[:, 3, n * CHUNK:(n + 1) * CHUNK], bank(("row", 3, n))[:, :]), ("row", 3, n))
            dve.wait_ge(sem("gelu_done"), 2 * TT)
            for t in range(TT):
                for n in range(2):
                    wait_full(dve, ("sg", t, n))
                    for g in range(4):
                        gg = 4 * n + g
                        cut = u_[:, t, gg * P:(gg + 1) * P]
                        last = V.scalar_tensor_tensor(out=cut, in0=bank(("sg", t, n))[:, g * P:(g + 1) * P],
                                                      scalar=bs[:, gg:gg + 1], in1=cut, op0=ALU.add, op1=ALU.mult)
                        if g < 3:
                            step(last)
                    out(last, ("sg", t, n))
            dve.wait_ge(sem("gates_done"), 2 * TT)
            for n in range(2):
                for t in range(TT):
                    c = slice(n * CHUNK, (n + 1) * CHUNK)
                    wait_full(dve, ("upa", n, t))
                    out(V.tensor_tensor(ga[:, t, c], bank(("upa", n, t))[:, :], ga[:, t, c], ALU.mult), ("upa", n, t))
                    wait_full(dve, ("upb", n, t))
                    out(V.tensor_tensor(gb[:, t, c], bank(("upb", n, t))[:, :], gb[:, t, c], ALU.mult), ("upb", n, t))
                    wait_out(dve, ("upa", n, t))
                    wait_out(dve, ("upb", n, t))
                    V.tensor_tensor(mg[:, t, c], ga[:, t, c], gb[:, t, c], ALU.add).then_inc(sem("merged"), 1)
            for v in range(4):
                for n in range(2):
                    wait_out(dve, ("row", v, n))
            for n in range(2):
                for t in range(TT):
                    c = slice(n * CHUNK, (n + 1) * CHUNK)
                    wait_full(dve, ("wo", n, t))
                    out(V.tensor_tensor(ga[:, t, c], bank(("wo", n, t))[:, :], rows[:, 0, c], ALU.mult), ("wo", n, t))
                    wait_out(dve, ("wo", n, t))
                    step(V.tensor_tensor(x[:, t, c], x[:, t, c], ga[:, t, c], ALU.add))
            settle()
            for t in range(TT):
                last = V.tensor_tensor_reduce(junk[:, 0:D], x[:, t, :], x[:, t, :], 1.0 / D, NORM_EPS,
                                              ALU.mult, ALU.add, small[:, 24 + t:25 + t])
                if t == 0:
                    step(last)
                    settle()
            last.then_inc(sem("sums2"), 1)
            dve.wait_ge(sem("roots2"), 1)
            step(V.reciprocal(small[:, 26:28], small[:, 26:28]))
            settle()
            for t in range(TT):
                step(V.scalar_tensor_tensor(out=h2[:, t, :], in0=x[:, t, :], scalar=small[:, 26 + t:27 + t],
                                            in1=rows[:, 2, :], op0=ALU.mult, op1=ALU.mult))
                settle()
                V.tensor_tensor(h2[:, t, :], h2[:, t, :], rows[:, 3, :], ALU.add).then_inc(sem("h2_ready"), 1)
            dve.wait_ge(sem("router_landed"), 32)
            for t in range(TT):
                wait_out(dve, ("rt", t))
                step(V.tensor_tensor(biased[:, t, :], score[:, t, :], rt_b, ALU.add))
                settle()
                step(V.max(top[:, t, :], biased[:, t, :]))
                settle()
                step(V.match_replace(rep[:, t, :], top[:, t, :], biased[:, t, :], MASKED))
                settle()
                step(V.tensor_tensor(rep[:, t, :], rep[:, t, :], biased[:, t, :], ALU.not_equal))
                settle()
                step(V.tensor_tensor_reduce(wt[:, t, :], rep[:, t, :], score[:, t, :], 1.0, 0.0, ALU.mult, ALU.add,
                                            small[:, 28 + t:29 + t]))
                settle()
                step(V.reciprocal(small[:, 30 + t:31 + t], small[:, 28 + t:29 + t]))
                settle()
                step(V.tensor_scalar(wt[:, t, :], wt[:, t, :], small[:, 30 + t:31 + t], ROUTE_SCALE, ALU.mult, ALU.mult))
                settle()

            def hidden(job, base, it=0):
                for f in range(2):
                    dve.wait_ge(sem("silu_done"), base + f + 1 + 2 * it)
                    out(V.tensor_tensor(ffs[:, f, :], act_ff[:, f, :], bank((job, f))[:, S:2 * S], ALU.mult), (job, f))

            hidden("shg", 0)
            for n in range(2):
                for t in range(TT):
                    wait_full(dve, ("shd", n, t))
                    out(V.tensor_copy(y[:, t, n * CHUNK:(n + 1) * CHUNK], bank(("shd", n, t))[:, :]), ("shd", n, t))
            for n in range(2):
                for t in range(TT):
                    wait_out(dve, ("shd", n, t))
            with dve.Fori(0, E) as e:
                hidden("eg", 2, e)
                for n in range(2):
                    for t in range(TT):
                        c = slice(n * CHUNK, (n + 1) * CHUNK)
                        b, m, per = banks[("ed", n, t)]
                        dve.wait_ge(bank_free[b], m + e * per)
                        wait_full(dve, ("ed", n, t), e)
                        out(V.scalar_tensor_tensor(out=y[:, t, c], in0=bank(("ed", n, t))[:, :],
                                                   scalar=wt[:, t, bass.ds(e, 1)], in1=y[:, t, c],
                                                   op0=ALU.mult, op1=ALU.add), ("ed", n, t))
            for n in range(2):
                for t in range(TT):
                    wait_out(dve, ("ed", n, t), E - 1)
            for t in range(TT):
                step(V.tensor_tensor(y[:, t, :], y[:, t, :], rows[:, 1, :], ALU.mult))
                settle()
                step(V.tensor_tensor(x[:, t, :], x[:, t, :], y[:, t, :], ALU.add))
                settle()
            for t in range(TT):
                last = V.tensor_tensor_reduce(junk[:, 0:D], x[:, t, :], x[:, t, :], 1.0 / D, NORM_EPS,
                                              ALU.mult, ALU.add, small[:, 32 + t:33 + t])
                if t == 0:
                    step(last)
                    settle()
            last.then_inc(sem("sums3"), 1)
            dve.wait_ge(sem("roots3"), 1)
            step(V.reciprocal(small[:, 34:36], small[:, 34:36]))
            settle()
            dve.wait_ge(sem("fin_landed"), 16)
            for t in range(TT):
                V.scalar_tensor_tensor(out=x[:, t, :], in0=x[:, t, :], scalar=small[:, 34 + t:35 + t],
                                       in1=fin_g, op0=ALU.mult, op1=ALU.mult).then_inc(sem("x_new"), 1)
            dve.wait_ge(sem("x_new"), TT)

            before = count[0]
            count[2] = DVE_STEPS_PER_LAYER
            with dve.Fori(0, L2) as layer:
                def layer_norm(jobs, g, b, which):
                    for n in range(2):
                        for t in range(TT):
                            c = slice(n * CHUNK, (n + 1) * CHUNK)
                            wait_full(dve, (jobs, n, t), layer)
                            out(V.scalar_tensor_tensor(out=x[:, t, c], in0=x[:, t, c], scalar=ALPHA,
                                                       in1=bank((jobs, n, t))[:, :], op0=ALU.mult, op1=ALU.add), (jobs, n, t))
                    for n in range(2):
                        for t in range(TT):
                            wait_out(dve, (jobs, n, t), layer)
                    for t in range(TT):
                        for n in range(2):
                            step(V.bn_stats(small[:, 40 + 6 * n:46 + 6 * n], x[:, t, n * CHUNK:(n + 1) * CHUNK]))
                        settle(layer)
                        dve.sem_inc(sem("stats_read"), 1)
                        step(V.bn_aggr(lnm[:, 2 * t:2 * t + 2], small[:, 40:52]))
                        settle(layer)
                    for t in range(TT):
                        last = V.tensor_scalar(lnv[:, t:t + 1], lnm[:, 2 * t + 1:2 * t + 2], LN_EPS, None, ALU.add)
                        if t == 0:
                            step(last)
                    last.then_inc(sem("l_var"), 1)
                    dve.wait_ge(sem("l_root"), 2 * layer + which + 1)
                    step(V.reciprocal(lnv[:, 2:4], lnv[:, 2:4]))
                    settle(layer)
                    for t in range(TT):
                        step(V.tensor_scalar(x[:, t, :], x[:, t, :], lnm[:, 2 * t:2 * t + 1], lnv[:, 2 + t:3 + t],
                                             ALU.subtract, ALU.mult))
                        settle(layer)
                        step(V.tensor_tensor(x[:, t, :], x[:, t, :], g, ALU.mult))
                        settle(layer)
                        V.tensor_tensor(x[:, t, :], x[:, t, :], b, ALU.add).then_inc(sem("x_new"), 1)
                    dve.wait_ge(sem("x_new"), 2 * TT * layer + TT * (which + 2))

                for p in range(2):
                    wait_full(dve, ("qs", p), layer)
                    out(V.tensor_scalar(qsT[:, 2 * p:2 * p + 2, :].rearrange("p a b -> p (a b)"), bank(("qs", p))[:, :],
                                        DH2 ** -0.5, None, ALU.mult), ("qs", p))
                for t in range(TT):
                    wait_full(dve, ("vs", t), layer)
                    out(V.tensor_copy(vs[:, t, :], bank(("vs", t))[:, :]), ("vs", t))

                def rotate(which, t):
                    v3 = qk[:, which, t, :].rearrange("p (h d) -> p h d", d=DH2)
                    half = ROPE2 // 2
                    x1, x2 = v3[:, :, 0:half], v3[:, :, half:ROPE2]

                    def table(name):
                        return k(name)[:, t * half:(t + 1) * half].unsqueeze(1).to_broadcast([P, H2, half])

                    tmp = [rope[:, j, 0:H2 * half].rearrange("p (h f) -> p h f", f=half) for j in range(4)]
                    for j, (src, name) in enumerate(((x1, "pcos"), (x2, "psin"), (x2, "pcos"), (x1, "psin"))):
                        step(V.tensor_tensor(tmp[j], src, table(name), ALU.mult))
                    settle(layer)
                    step(V.tensor_tensor(x1, tmp[0], tmp[1], ALU.subtract))
                    V.tensor_tensor(x2, tmp[2], tmp[3], ALU.add).then_inc(sem("roped"), 1)

                def filler_out(i):
                    name, n, t = FILLERS[i]
                    key = (name, n, t)
                    if name in ("qm", "km", "vm"):
                        wait_full(dve, key, layer)
                        if name == "vm":
                            out(V.tensor_copy(vm[:, t, :], bank(key)[:, :]), key)
                        else:
                            which = ("qm", "km").index(name)
                            out(V.tensor_scalar(qk[:, which, t, :], bank(key)[:, :], (DH2 ** -0.5, 1.0)[which], None,
                                                ALU.mult), key)
                            wait_out(dve, key, layer)
                            rotate(which, t)
                    else:
                        wait_out(dve, key, layer)
                        g = gates[:, ("gs", "gm").index(name), t, n * CHUNK:(n + 1) * CHUNK]
                        step(V.tensor_scalar(g, g, 1.0, None, ALU.add))
                        settle(layer)
                        step(V.reciprocal(g, g))

                def heads_of(ap, nh):
                    return ap.rearrange("p (h k) -> p h k", h=nh)

                def stick_b(i):
                    t, h0, nh, keys = ITEMS[i]
                    e_, r_ = es[:, i % 2, :], rw[:, i % 2, :]
                    z = bank(("sc", i))[:, :]
                    dve.wait_ge(sem("ln_done"), NI * layer + i + 1)
                    step(V.scalar_tensor_tensor(out=e_, in0=z, scalar=0.0, in1=e_, op0=ALU.max, op1=ALU.add))
                    settle(layer)
                    diag = heads_of(e_, nh)[:, :, keys - P:keys]
                    step(V.tensor_tensor(diag, diag, k("past01").unsqueeze(1).to_broadcast([P, nh, P]), ALU.mult))
                    settle(layer)
                    if i >= 2:
                        wait_full(dve, ("wT", i - 2), layer)
                    for j in range(nh):
                        back = slice((j + 1) * keys - 1, j * keys - 1 if j else None, -1)
                        step(V.tensor_tensor_scan(r_[:, back], e_[:, back], k("zeros")[:, 0:keys], 0.0, ALU.add, ALU.add))
                    settle(layer)
                    out(V.tensor_tensor(r_, z, r_, ALU.subtract), ("sc", i))
                    wait_out(dve, ("sc", i), layer)
                    diag = heads_of(r_, nh)[:, :, keys - P:keys]
                    V.tensor_tensor(diag, diag, k("own_future").unsqueeze(1).to_broadcast([P, nh, P]), ALU.add)\
                        .then_inc(sem("log_weights"), 1)

                def block_max(i):
                    t, h0, nh, keys = ITEMS[i]
                    key = ("sc", NI + i)
                    wait_full(dve, key, layer)
                    diag = heads_of(bank(key)[:, :], nh)[:, :, keys - P:keys]
                    step(V.tensor_tensor(diag, diag, k("future").unsqueeze(1).to_broadcast([P, nh, P]), ALU.add))
                    settle(layer)
                    hh = t * H2 + h0
                    step(V.tensor_reduce(mbn[:, hh:hh + nh], heads_of(bank(key)[:, :], nh), AX_X, ALU.max))
                    settle(layer)
                    V.tensor_scalar(mbn[:, hh:hh + nh], mbn[:, hh:hh + nh], -1.0, None, ALU.mult).then_inc(sem("mb_max"), 1)

                def attention_out(b, t):
                    dve.wait_ge(sem("item_summed"), 2 * NI * layer + NI * b + LAST_OF_TILE[t] + 1)
                    key = ("o", b, t)
                    side = P // DH2
                    dst = o[:, b, t, :].rearrange("p (j s d) -> p s j d", s=side, d=DH2)
                    src = bank(key)[:, :].rearrange("p (s j d) -> p s j d", s=side, d=DH2)
                    if b == 0:
                        out(V.tensor_copy(dst, src), key)
                        return
                    ms = mbs[:, t * H2:(t + 1) * H2]
                    step(V.reciprocal(ms, ms))
                    settle(layer)
                    n = H2 // side
                    for s_ in range(side):
                        last = V.tensor_tensor(dst[:, s_], src[:, s_],
                                               ms[:, s_ * n:(s_ + 1) * n].unsqueeze(2).to_broadcast([P, n, DH2]), ALU.mult)
                        if s_ == 0:
                            step(last)
                    out(last, key)

                for i in range(2 * NI + 3):
                    if 1 <= i <= len(FILLERS):
                        filler_out(i - 1)
                    if NI <= i < 2 * NI:
                        block_max(i - NI)
                    if 1 <= i <= NI:
                        stick_b(i - 1)
                    for b in range(2):
                        for t in range(TT):
                            if i == NI * b + LAST_OF_TILE[t] + 3:
                                attention_out(b, t)
                settle(layer)
                for n in range(2):
                    for t in range(TT):
                        c = slice(n * CHUNK, (n + 1) * CHUNK)
                        for b, name in enumerate(("bs", "bm")):
                            wait_full(dve, (name, n, t), layer)
                            g = gates[:, b, t, c]
                            out(V.tensor_tensor(g, bank((name, n, t))[:, :], g, ALU.mult), (name, n, t))
                        wait_out(dve, ("bs", n, t), layer)
                        wait_out(dve, ("bm", n, t), layer)
                        V.tensor_tensor(lmg[:, t, c], gates[:, 0, t, c], gates[:, 1, t, c], ALU.add)\
                            .then_inc(sem("l_merged"), 1)
                dve.wait_ge(sem("ln_landed"), 64 * (layer + 1))
                layer_norm("l_wo", ln[:, 0, :], ln[:, 1, :], 0)
                for f in range(FT):
                    dve.wait_ge(sem("l_silu"), FT * layer + f + 1)
                    out(V.tensor_tensor(fh[:, f, :], silu[:, f % 2, :], bank(("fg", f))[:, S:2 * S], ALU.mult), ("fg", f))
                layer_norm("fd", ln[:, 2, :], ln[:, 3, :], 1)
            assert count[0] - before == DVE_STEPS_PER_LAYER, count[0] - before


def kernel(**inputs):
    import concourse.bacc as bacc
    from concourse.bass_utils import run_bass_kernel_spmd

    def arr(name):
        return np.asarray(inputs[name])

    def columns(v):
        return v.reshape(-1, P).T

    c = np.stack([arr("c")[0], arr("c_ctx")], -1)
    data = {
        "x": arr("x")[0], "ctx": arr("ctx")[0],
        "c_cols": c.reshape(KT, P, 2).transpose(1, 0, 2).reshape(P, 2 * KT),
        "b_ada_cols": columns(arr("b_ada")[0]),
        "gains": np.concatenate([columns(arr("norm_mix_g")[0]), columns(arr("norm_ffn_g")[0])], 1),
        "b_in": arr("b_in"), "b_in_cols": columns(arr("b_in")[0, COL_NQ:COL_NV]),
        "b_s_cols": arr("sgu_b_s")[0].T,
        "w_sT": arr("sgu_w_s")[0].transpose(2, 0, 1),
        "sgu_ln_g": arr("sgu_ln_g"), "sgu_ln_b": arr("sgu_ln_b"), "tiny_w_o": arr("tiny_w_o")[0],
        "na_rpb": arr("na_rpb"), "b_router": arr("b_router"),
        "final_norm_g": arr("final_norm_g").reshape(1, D),
        "consts": constants(),
    }
    for name in ("w_ada", "w_in", "w_up_a", "w_up_b", "w_out", "w_router", "w_e_gate", "w_e_up", "w_e_down",
                 "w_sh_gate", "w_sh_up", "w_sh_down"):
        data[name] = arr(name)[0]
    for name in ("w_in_2", "w_branch_sb_2", "w_branch_moba_2", "w_out_2", "ln_mix_g_2", "ln_mix_b_2",
                 "w_ffn_gate_2", "w_ffn_up_2", "w_ffn_down_2", "ln_ffn_g_2", "ln_ffn_b_2"):
        data[name] = arr(name)
    nc = bacc.Bacc("TRN2", target_bir_lowering=False, num_devices=1)
    arrays, handles = {}, {}
    for name, value in data.items():
        value = np.ascontiguousarray(value)
        arrays["in_" + name] = value
        handles[name] = nc.dram_tensor("in_" + name, value.shape, mybir.dt.from_np(value.dtype), kind="ExternalInput").ap()
    handles["out"] = nc.dram_tensor("out_0", (S, D), F32, kind="ExternalOutput").ap()
    handles["rpb_copies"] = nc.dram_tensor("rpb_copies", (GRID_W, data["na_rpb"].size), F32, kind="Internal").ap()
    build(nc, handles)
    r = run_bass_kernel_spmd(nc, [arrays], core_ids=[0])
    return r.results[0]["out_0"].reshape(1, S, D)
```

```python
from contextlib import ExitStack

import numpy as np

import concourse.bass as bass
from concourse import mybir

ALU = mybir.AluOpType
ACT = mybir.ActivationFunctionType
AX_X = mybir.AxisListType.X
F32 = mybir.dt.float32
F32R = mybir.dt.float32r
U32 = mybir.dt.uint32
I32 = mybir.dt.int32

P = 128
D = 1024
S = 256
TT = S // P
KT = D // P
CTX = 256
GRID_W = 64
ROWS = S // GRID_W
NORM_EPS = 1e-6
LN_EPS = 1e-5
GROUPS = 8
TINY = 64
NH, NDH = 16, 32
NW = NH * NDH
NA_ROWS, NA_COLS = 8, 16
E = 64
TOP_K = 8
FF = 256
ROUTE_SCALE = 2.5
CAP = 80
XB = 4
ROUND = 3
COL_U, COL_V, COL_TQ = 0, D, 2 * D
COL_NQ = COL_TQ + 3 * TINY
COL_NK, COL_NV = COL_NQ + NW, COL_NQ + 2 * NW
COL_GA = COL_NQ + 3 * NW
COL_GB = COL_GA + D
L2 = 2
H2, DH2 = 8, 64
W2 = H2 * DH2
ROPE2 = DH2 // 4
DFF = 2816
FT = DFF // P
ALPHA = (2 * L2) ** 0.25
CHUNK = 512
MASKED = -1e30
SLOTS = 9
SLOT = 2048
ARENA = 30464
DR = 6

CONST = {}
_at = 0
for _name, _n in [("ident", P), ("ones", P), ("past01", P), ("future", P), ("own_future", P),
                  ("window", GRID_W), ("zeros", S), ("tcos", TT * 32), ("tsin", TT * 32),
                  ("pcos", TT * 8), ("psin", TT * 8), ("earlier", P), ("slot", CAP), ("expert", E), ("from_end", E), ("token", TT)]:
    CONST[_name] = (_at, _n)
    _at += _n
N_CONST = _at


def constants():
    c = np.zeros((P, N_CONST), np.float32)

    def put(name, value):
        at, n = CONST[name]
        c[:, at:at + n] = np.asarray(value, np.float32).reshape(P, n)

    q, k = np.arange(P)[:, None], np.arange(P)[None, :]
    put("ident", q == k)
    put("ones", np.ones((P, P)))
    put("past01", k < q)
    put("future", np.where(k <= q, 0.0, MASKED))
    put("own_future", np.where(k < q, 0.0, MASKED))
    cq, ck = (np.arange(P) % GRID_W)[:, None], np.arange(GRID_W)[None, :]
    start = np.clip(cq - NA_COLS // 2, 0, GRID_W - NA_COLS)
    put("window", np.where((ck >= start) & (ck < start + NA_COLS), 0.0, MASKED))
    put("earlier", q < k)
    put("slot", np.broadcast_to(np.arange(1, CAP + 1), (P, CAP)))
    put("expert", np.broadcast_to(np.arange(E), (P, E)))
    put("from_end", np.broadcast_to(E - np.arange(E), (P, E)))
    put("token", np.arange(S).reshape(TT, P).T)
    tok = np.arange(S)
    quarter = TINY // 4
    pos = np.stack([tok // GRID_W, tok % GRID_W], -1).astype(np.float32)
    inv = np.float32(10000.0) ** (-np.arange(quarter, dtype=np.float32) / np.float32(quarter))
    ang = (pos[:, :, None] * inv).astype(np.float32).reshape(TT, P, 2 * quarter).transpose(1, 0, 2)
    put("tcos", np.cos(ang))
    put("tsin", np.sin(ang))
    inv = np.float32(500000.0) ** (-np.arange(0, ROPE2, 2, dtype=np.float32) / np.float32(ROPE2))
    ang = (tok.astype(np.float32)[:, None] * inv).astype(np.float32).reshape(TT, P, ROPE2 // 2).transpose(1, 0, 2)
    put("pcos", np.cos(ang))
    put("psin", np.sin(ang))
    return c


class Ring:

    def __init__(self, slots):
        self.slots = list(slots)
        self.at = 0
        self.count = {s: 0 for s in self.slots}
        self.place = {}
        self.owner = {s: None for s in self.slots}
        self.before = {}
        self.in_loop = None
        self.iterations = {}

    def take(self, key):
        s = self.slots[self.at % len(self.slots)]
        assert key not in self.place, key
        self.place[key] = (s, self.count[s], 0)
        self.before[key] = [self.owner[s]] if self.owner[s] is not None else []
        self.owner[s] = key
        self.count[s] += 1
        self.at += 1
        if self.in_loop is not None:
            self.in_loop[1].append(key)

    def loop(self):
        self.in_loop = (self.at, [], dict(self.count), dict(self.owner))

    def end_loop(self, iterations):
        at0, keys, start, owner0 = self.in_loop
        first = {}
        for key in keys:
            s, n, _ = self.place[key]
            self.place[key] = (s, n, self.count[s] - start[s])
            self.iterations[key] = iterations
            first.setdefault(s, key)
        for s, key in first.items():
            self.before[key] = self.before[key] + [("previous iteration", self.owner[s])]
        for s in self.slots:
            self.count[s] = start[s] + iterations * (self.count[s] - start[s])
        self.in_loop = None


HEAD = [2 * j + side for side in range(P // DH2) for j in range(H2 * DH2 // P)]
ITEMS = [(t, h, CHUNK // (P * (t + 1)), P * (t + 1))
         for t in range(TT) for h in range(0, H2, CHUNK // (P * (t + 1)))]
NI = len(ITEMS)
LAST_OF_TILE = [max(i for i, it in enumerate(ITEMS) if it[0] == t) for t in range(TT)]
NA_STEPS = TT * NH


def plan():
    main, long, hold = Ring([0, 1, 2]), Ring([3, 4, 5, 6]), Ring([7])
    units = Ring(range(SLOTS))
    freed_by, sources, order = {}, {}, []

    def unit(key, job, *source):
        units.take(key)
        freed_by[key] = job
        sources[key] = source
        order.append(key)

    def chunk(key, job, *source):
        for half in range(2):
            unit(key + (half,), job, "rows", *source, half)

    for n in (1, 0, 3, 2):
        chunk(("ada", n), ("mod", 0) if n % 2 else ("ada_summed", n // 2 + 1), "w_ada", n * CHUNK)
    main.take(("mod", 0))
    for g in range(4):
        main.take(("xT", g))
        main.take(("cT", g))
    unit(("win", "tiny"), ("tiny", 3), "tiny")
    for t in range(4):
        long.take(("tiny", t))
    chunk(("win", "nq"), ("nq", 1), "w_in", COL_NQ)
    for p in range(2):
        long.take(("nq", p))
    chunk(("win", "nk"), ("nk", 3), "w_in", COL_NK)
    for f in range(4):
        long.take(("nk", f))
    chunk(("win", "nv"), ("nv", 3), "w_in", COL_NV)
    for t in range(4):
        long.take(("nv", t))
    main.take(("tqT", 0))
    main.take(("tkT", 0))
    for t in range(TT):
        main.take(("ts", t))
    for t in range(TT):
        main.take(("tpT", t))
        main.take(("tO", t))
    for name, col in (("v", COL_V), ("u", COL_U)):
        for n in range(2):
            chunk(("win", name, n), (name, n, 1), "w_in", col + n * CHUNK)
            for t in range(TT):
                long.take((name, n, t))
    for i in range(NA_STEPS + 2):
        if i < NA_STEPS:
            main.take(("ns", i))
        if 1 <= i <= NA_STEPS:
            main.take(("npT", i - 1))
    for t in range(TT):
        hold.take(("nO", t))
    for i, (name, n) in enumerate(GATES):
        chunk(("win", name, n), (name, n, 1), "w_in", (COL_GA, COL_GB)[i // 2] + n * CHUNK)
        for j in (2 * i, 2 * i + 1):
            chunk(("ada", 4 + j), ("ada_summed", 3 + j), "w_ada", (4 + j) * CHUNK)
        for t in range(TT):
            long.take((name, n, t))
        if i:
            long.take(("row", 2 * i - 2))
            long.take(("row", 2 * i - 1))
    long.take(("row", 6))
    long.take(("row", 7))
    for t in range(TT):
        for n in range(2):
            main.take(("sg", t, n))
    for g in range(2):
        main.take(("obT", g))
    for g in range(4):
        main.take(("oaT", g))
    for n in range(2):
        chunk(("upa", n), ("upa", n, 1), "w_up_a", n * CHUNK)
        unit(("upb", n), ("upb", n, 1), "half", "w_up_b", n * CHUNK)
    for t in range(TT):
        for n in range(2):
            long.take(("upa", n, t))
            long.take(("upb", n, t))
    for g in range(4):
        main.take(("mT", g))
    for n in range(2):
        chunk(("wo", n), ("wo", n, 1), "w_out", n * CHUNK)
    for t in range(TT):
        for n in range(2):
            long.take(("wo", n, t))
    for g in range(4):
        main.take(("h2T", g))
    for t in range(TT):
        main.take(("rt", t))
    unit(("shg",), ("shg", 1), "ff", "w_sh_gate", 0)
    unit(("shu",), ("shg", 1), "ff", "w_sh_up", 0)
    unit(("shd",), ("shd", 1, 1), "down", "w_sh_down", 0)
    for f in range(2):
        main.take(("shg", f))
    for t in range(TT):
        main.take(("rk", t))
    main.take(("cnt", 0))
    for i in range(2):
        hold.take(("ix", i))
    for n in range(2):
        for t in range(TT):
            long.take(("shd", n, t))

    def expert_step(which, down_which, turn):
        if which is not None:
            unit(("eg", which), ("gu", which), "expert", "w_e_gate")
            unit(("eu", which), ("gu", which), "expert", "w_e_up")
            main.take(("gu", which))
        if turn is not None:
            for half in range(2):
                main.take(("gT", turn, half))
        if down_which is not None:
            unit(("ed", down_which), ("yd", down_which, 1), "expert", "w_e_down")
            for n in range(2):
                long.take(("yd", down_which, n))

    expert_step(None, None, "first")
    expert_step("first", None, "second")
    for r in (main, long, units):
        r.loop()
    for j in range(ROUND):
        expert_step(j, j, j)
    for r in (main, long, units):
        r.end_loop((E - 1) // ROUND)
    expert_step(None, "last", None)
    for r in (main, long, hold, units):
        r.loop()
    for g in range(4):
        main.take(("l_xT", g))
    for name, at in (("qs", 0), ("ks", 1)):
        chunk(("l_in", name), (name, 1), "w_in_2", at * W2)
        for p in range(2):
            long.take((name, p))
    chunk(("l_in", "vs"), ("vs", 1), "w_in_2", 2 * W2)
    for t in range(TT):
        long.take(("vs", t))
    for i in range(2 * NI + 2):
        if i < 2 * NI:
            main.take(("sc", i))
        if i < len(FILLERS):
            name, n, t = FILLERS[i]
            if t == 0:
                chunk(("l_in", name, n), (name, n, 1), "w_in_2", 3 * W2 + FILL_NAMES.index((name, n)) * CHUNK)
            long.take((name, n, t))
        if 1 <= i <= 2 * NI:
            main.take(("wT", i - 1))
        if i == NI - 1:
            for name in ("qmT", "kmT"):
                for p in range(2):
                    long.take((name, p))
    for b in range(2):
        for t in range(TT):
            hold.take(("o", b, t))
    for b in range(2):
        for p in range(2):
            main.take(("oT", b, p))
    for n in range(2):
        unit(("bs", n), ("bs", n, 1), "half", "w_branch_sb_2", n * CHUNK)
        unit(("bm", n), ("bm", n, 1), "half", "w_branch_moba_2", n * CHUNK)
    for t in range(TT):
        for n in range(2):
            long.take(("bs", n, t))
            long.take(("bm", n, t))
    for g in range(4):
        main.take(("l_mT", g))
    for n in range(2):
        chunk(("l_wo", n), ("l_wo", n, 1), "w_out_2", n * CHUNK)
    for t in range(TT):
        for n in range(2):
            long.take(("l_wo", n, t))
    for g in range(4):
        main.take(("l_yT", g))
    for t in range(TT):
        for n in range(2):
            long.take(("fd", n, t))
    for u, key in enumerate(FFN_UNITS):
        name, pair = key
        kind, source = {"fg": ("ff", "w_ffn_gate_2"), "fu": ("ff", "w_ffn_up_2"), "fd": ("down", "w_ffn_down_2")}[name]
        unit(key, ("split", u), kind, source, pair * FF)
    for f in range(FT):
        main.take(("fg", f))
    for r in (main, long, hold, units):
        r.end_loop(L2)
    banks = {**main.place, **long.place, **hold.place}
    return banks, units, freed_by, sources, order


GATES = [(name, n) for name in ("ga", "gb") for n in range(2)]
ROW_OF_CHUNK = [0, 0, 3, 3, 2, 2, 1, 1]
FILL_NAMES = [("qm", 0), ("km", 0), ("vm", 0), ("gs", 0), ("gs", 1), ("gm", 0), ("gm", 1)]
FILLERS = [(name, n, t) for name, n in FILL_NAMES for t in range(TT)]
FFN_UNITS = [("fg", 0), ("fu", 0)]
for _pair in range(1, FT // 2):
    FFN_UNITS += [("fg", _pair), ("fu", _pair), ("fd", _pair - 1)]
FFN_UNITS.append(("fd", FT // 2 - 1))
NU = len(FFN_UNITS)
SPLIT_SLOTS = 4
LAYER_KEYS = ("l_in", "bs", "bm", "l_wo", "fg", "fu", "fd")
DVE_STEPS_PER_LAYER = 100


def build(nc, a):
    banks, units, freed_by, sources, order = plan()
    ctx = ExitStack()
    with ctx:
        def sb(name, *dims, dt=F32):
            return ctx.enter_context(nc.sbuf_tensor(name, [P, *dims], dt))

        sems = {}

        def sem(name):
            if name not in sems:
                sems[name] = ctx.enter_context(nc.semaphore(name))
            return sems[name]

        psum = [ctx.enter_context(nc.psum_tensor(f"bank{b}", [P, CHUNK], F32)) for b in range(8)]
        bank_full = [sem(f"bank_full{b}") for b in range(8)]
        bank_free = [sem(f"bank_free{b}") for b in range(8)]
        landed = [sem(f"weights_landed{s}") for s in range(SLOTS)]

        ring = sb("weight_ring", SLOTS, SLOT)
        const = sb("const", N_CONST)
        x = sb("x", TT, D)
        cols = sb("cols", 440)
        token_of = sb("token_of", E + 1, dt=U32)
        token_now = sb("token_now", ROUND, dt=U32)
        row_of = sb("row_of", TT * TOP_K, dt=U32)
        counts = sb("counts", 2 * E + 2, dt=I32)
        with nc.sbuf_tensor("arena", [P, ARENA], F32) as arena:
            pass
        split = sb("split", 22528, dt=F32R)

        def k(name, *dims):
            at, n = CONST[name]
            v = const[:, at:at + n]
            return v

        class Columns:
            def __init__(self):
                self.at = 0

            def take(self, n):
                self.at += n
                assert self.at <= 440
                return cols[:, self.at - n:self.at]

        cc = Columns()
        c_col = cc.take(2 * KT)
        ada_b = cc.take(2 * KT)
        gain = cc.take(KT)
        in_b = cc.take(8)
        bs = cc.take(GROUPS)
        loaded_cols = cols[:, 0:cc.at]
        sc_col = cc.take(2 * KT)
        mod = cc.take(4 * KT)
        mixA = cc.take(2 * KT)
        small = cc.take(64)
        cols_na = cc.take(NA_STEPS), cc.take(NA_STEPS)
        mbn, mbs = cc.take(TT * H2), cc.take(TT * H2)
        w_of, pos_of, row_f = (cc.take(TT * TOP_K) for _ in range(3))
        lnm, lnv = cc.take(2 * TT), cc.take(2 * TT)

        def area(at, *dims):
            n = int(np.prod(dims))
            assert at + n <= ARENA
            v = arena[:, at:at + n]
            if len(dims) == 2:
                return v.rearrange("p (a b) -> p a b", b=dims[1])
            if len(dims) == 3:
                return v.rearrange("p (a b c) -> p a b c", b=dims[1], c=dims[2])
            return v

        posb = area(0, NH, DR, GRID_W)
        ga, gb, mg = area(0, TT, D), area(2048, TT, D), area(4096, TT, D)
        hT = area(6144, KT, 2 * S)
        oaT, mT = area(6144, KT, S), area(8192, KT, S)
        xn, cn = area(10240, TT, D), area(12288, TT, D)
        v_, u_ = xn, cn
        nqT, nkT, nv = area(14336, 4, S), area(15360, 4, 2 * S), area(17408, 4, NW)
        rows = area(14336, 4, D)
        pr, prT = area(19456, 2, CHUNK), area(20480, 2, CHUNK)
        junk = area(19456, 2048)
        ln_g, ln_b = area(21504, D), area(22528, D)
        wsT = area(23552, GROUPS, P)
        w_tiny = area(24576, D)
        tqkv = area(25600, 4, 3 * TINY)
        tT = area(26368, 6 * P)
        ttT = area(27136, S)
        bias = area(27392, 2, CHUNK)
        ob, obT = area(28416, TT, NW), area(29440, 4, S)
        ada0 = area(28416, 2, 2, CHUNK)
        ada = area(4096, 4, CHUNK)
        ffn_g = area(29440, D)
        fin_g = area(28416, D)
        h2, h2T = area(0, TT, D), area(2048, KT, S)
        y = area(4096, TT, D)
        act_ff = area(6144, 2, S)
        ffs = area(6656, 2, S)
        w_rt = area(7168, KT, E)
        rt_b = area(7680, E)
        score, biased, rep_, wt = (area(7744 + 128 * i, TT, E) for i in range(4))
        top = area(8256, TT, 8)
        pos = area(8272, TT, E)
        over = area(8400, TT, E)
        xg = area(8704, ROUND, D)
        xgT = area(11776, ROUND, KT * CAP)
        sil = area(13696, ROUND, 2 * CAP)
        hid = area(24576, ROUND, 2 * CAP)
        ys = area(21504, ROUND, D)
        onehot = area(19456, ROUND, TT * XB * CAP)
        back = [area(at + i * D, D) for at in (18432, 25088) for i in range(3)]
        xT = area(0, KT, S)
        qsT, ksT, vs = area(2048, 4, S), area(3072, 4, S), area(4096, TT, W2)
        qk = area(5120, 2, TT, W2)
        qmT, kmT, vm = area(7168, 4, S), area(8192, 4, S), area(9216, TT, W2)
        gates = area(10240, 2, TT, D)
        o = area(14336, 2, TT, W2)
        oT = area(16384, 2, 4 * S)
        lmg, lmT = area(18432, TT, D), area(20480, KT, S)
        ln = area(22528, 4, D)
        es, rw, wT_ = area(26624, 2, CHUNK), area(27648, 2, CHUNK), area(28672, 2, CHUNK)
        rope = area(29696, 4, 128)
        silu = area(26624, 2, S)
        fh32 = area(27136, 4, S)
        xs = split[:, 0:2 * KT * S].rearrange("p (w k t) -> p w k t", w=2, k=KT)
        fh = split[:, 4096:4096 + 8 * S].rearrange("p (f w t) -> p f w t", f=4, w=2)
        ws = split[:, 6144:6144 + SPLIT_SLOTS * 2 * SLOT].rearrange("p (s w n) -> p s w n", s=SPLIT_SLOTS, w=2)

        def bank(key):
            return psum[banks[key][0]]

        def wait_bank(eng, key, it=0):
            b, n, per = banks[key]
            if n or per:
                eng.wait_ge(bank_free[b], n + it * per)

        def wait_full(eng, key, it=0):
            b, n, per = banks[key]
            eng.wait_ge(bank_full[b], n + 1 + it * per)

        def wait_out(eng, key, it=0):
            b, n, per = banks[key]
            eng.wait_ge(bank_free[b], n + 1 + it * per)

        def full(ins, key):
            ins.then_inc(bank_full[banks[key][0]], 1)

        def out(ins, key):
            ins.then_inc(bank_free[banks[key][0]], 1)

        def wait_around(eng, first, key, it):
            wait_out(eng, first)
            b, n, per = banks[key]
            assert n + 1 > per
            eng.wait_ge(bank_free[b], n + 1 - per + it * per)

        def wait_weights(eng, key, it=0):
            s, n, per = units.place[key]
            eng.wait_ge(landed[s], 16 * (n + 1 + it * per))

        def w(key, rows_, cols_):
            s = units.place[key][0]
            return ring[:, s, 0:rows_ * cols_].rearrange("p (k n) -> p k n", n=cols_)

        def wait_split(eng, u, it):
            eng.wait_ge(sem("split_ready"), NU * it + NU + u + 1)

        pieces = [(COL_TQ, 3 * TINY, ("tiny", 3)), (COL_NV, CHUNK, ("nv", 3))]
        for name, col in (("v", COL_V), ("u", COL_U), ("ga", COL_GA), ("gb", COL_GB)):
            for n in range(2):
                pieces.append((col + n * CHUNK, CHUNK, (name, n, 1)))
        piece_of = {p[2][:-1]: i for i, p in enumerate(pieces)}

        def wait_piece(eng, i):
            eng.wait_ge(sem(f"bias_landed{i % 2}"), 16 * (i // 2 + 1))

        block = ctx.enter_context(nc.Block())

        def overflow(eng, body, after=None):
            eng.wait_ge(sem("counts_ready"), 1)
            most = eng.value_load(counts[0:1, E:E + 1], min_val=0, max_val=S)
            with eng.If(most > CAP):
                with eng.Fori(0, E) as e:
                    n = eng.value_load(counts[0:1, bass.ds(e, 1)], min_val=0, max_val=S)
                    with eng.If(n > CAP):
                        body(e, eng.value_load(counts[0:1, bass.ds(e + E + 1, 1)], min_val=0, max_val=E - 1))
                if after:
                    after(eng.value_load(counts[0:1, 2 * E + 1:2 * E + 2], min_val=1, max_val=E))

        @block.sync
        def _(sp):
            def load(key, it=0):
                s = units.place[key][0]
                for before in units.before[key]:
                    back = before[0] == "previous iteration"
                    job = freed_by[before[1] if back else before]
                    if job[0] == "split":
                        sp.wait_ge(sem("split_ready"), NU * it + (0 if back else NU) + job[1] + 1)
                        sp.sem_inc(sem("slots_freed"), 1)
                        continue
                    if job[0] == "ada_summed":
                        sp.wait_ge(sem("ada_summed"), job[1])
                        continue
                    at = (it - 1) if back else it
                    if not back and units.iterations.get(before) != units.iterations.get(key):
                        at = units.iterations.get(before, 1) - 1
                    b, n, per = banks[job]
                    if back:
                        assert n + 1 > per, (key, job)
                    sp.wait_ge(bank_full[b], n + 1 + at * per)
                    if not isinstance(at, int):
                        sp.sem_inc(sem("slots_freed"), 1)
                kind, *src = sources[key]
                if kind == "rows":
                    name, col, half = src
                    m = a[name][it] if name.endswith("_2") else a[name]
                    dst = w(key, 4, CHUNK)
                    view = m[half * CHUNK:(half + 1) * CHUNK, col:col + CHUNK]
                elif kind == "half":
                    name, col = src
                    m = a[name][it] if name.endswith("_2") else a[name]
                    dst, view = w(key, 4, CHUNK), m[:, col:col + CHUNK]
                elif kind == "tiny":
                    dst, view = w(key, KT, 3 * TINY), a["w_in"][:, COL_TQ:COL_NQ]
                elif kind == "ff":
                    name, col = src
                    m = a[name][it] if name.endswith("_2") else a[name]
                    dst, view = w(key, KT, FF), m[:, col:col + FF]
                elif kind == "down":
                    name, row = src
                    m = a[name][it] if name.endswith("_2") else a[name]
                    dst, view = w(key, 2, D), m[row:row + FF, :]
                else:
                    which = key[1]
                    e = it if it is not None else 0
                    if which == "last":
                        e = E - 1
                    elif which == "first":
                        e = 0
                    else:
                        e = it * ROUND + which + (0 if src[0] == "w_e_down" else 1)
                    view = a[src[0]][e].rearrange("(p k) n -> p k n", p=P)
                    dst = w(key, 2, D) if src[0] == "w_e_down" else w(key, KT, FF)
                    sp.dma_start(dst, view).then_inc(landed[s], 16)
                    return
                sp.dma_start(dst, view.rearrange("(k p) n -> p k n", p=P)).then_inc(landed[s], 16)

            def is_expert(key):
                return key[0] in ("eg", "eu", "ed")

            sp.dma_start(loaded_cols, a["cols"]).then_inc(sem("cols_landed"), 16)
            sp.dma_start(x[:, :, :], a["x"].rearrange("(t p) d -> p t d", p=P)).then_inc(sem("x_landed"), 16)
            sp.dma_start(cn, a["ctx"].rearrange("(t p) d -> p t d", p=P)).then_inc(sem("ctx_landed"), 16)
            sp.dma_start(const[:, :], a["consts"]).then_inc(sem("const_landed"), 16)
            for key in order:
                if key[0] not in LAYER_KEYS and (not is_expert(key) or key[1] == "first"):
                    load(key)
            with sp.Fori(0, (E - 1) // ROUND) as it:
                for key in order:
                    if is_expert(key) and key[1] in range(ROUND):
                        load(key, it)
            load(("ed", "last"))

            def loads(e, done):
                sp.wait_ge(sem("over_tensor"), 6 * done + 1)
                sp.sem_inc(sem("slots_freed"), 1)
                for j, (name, rows_, cols_) in enumerate((("w_e_gate", KT, FF), ("w_e_up", KT, FF), ("w_e_down", 2, D))):
                    sp.dma_start(ring[:, j, :].rearrange("p (k n) -> p k n", n=cols_),
                                 a[name][e].rearrange("(k p) n -> p k n", p=P)).then_inc(sem("over_landed"), 16)

            def slots_back(total):
                sp.wait_ge(sem("over_tensor"), 6 * total + 1)
                sp.sem_inc(sem("slots_freed"), 1)

            overflow(sp, loads, slots_back)
            sp.wait_ge(sem("row_added"), TT * TOP_K - 4)
            with sp.Fori(0, L2) as layer:
                for key in order:
                    if key[0] in LAYER_KEYS:
                        load(key, layer)
            for t in range(TT):
                sp.wait_ge(sem("x_new"), 2 * TT * L2 + t + 1)
                sp.dma_start(a["out"][t * P:(t + 1) * P, :], x[:, t, :]).then_inc(sem("stored"), 16)
            sp.wait_ge(sem("stored"), 16 * TT)

        @block.gpsimd
        def _(pool):
            def bcast(name, at, n):
                return bass.AP(tensor=a[name].tensor, offset=at, ap=[[0, P], [1, n]])

            for i, (col, n, _) in enumerate(pieces[:2]):
                pool.dma_start(bias[:, i, 0:n], bcast("b_in", col, n)).then_inc(sem(f"bias_landed{i}"), 16)
            width = 2 * NA_COLS - 1
            table = NH * (2 * NA_ROWS - 1) * width
            pool.dma_start(a["rpb_copies"], bass.AP(tensor=a["na_rpb"].tensor, offset=0, ap=[[0, GRID_W], [1, table]]))\
                .then_inc(sem("copies_stored"), 16)
            pool.wait_ge(sem("copies_stored"), 16)
            for half in range(2):
                first = NA_ROWS - 1 - (TT - 1) * 2 - half
                for r in range(DR):
                    pool.dma_start(
                        posb[half * GRID_W:(half + 1) * GRID_W, :, r, :],
                        bass.AP(tensor=a["rpb_copies"].tensor, offset=(first + r) * width + NA_COLS - 1,
                                ap=[[table - 1, GRID_W], [(2 * NA_ROWS - 1) * width, NH], [1, GRID_W]]),
                    ).then_inc(sem("posb_landed"), 16)
            pool.dma_start(ln_g, bcast("sgu_ln_g", 0, D)).then_inc(sem("sgu_landed"), 16)
            pool.dma_start(ln_b, bcast("sgu_ln_b", 0, D)).then_inc(sem("sgu_landed"), 16)
            pool.dma_start(wsT, a["w_sT"]).then_inc(sem("sgu_landed"), 16)
            pool.dma_start(w_tiny[0:TINY, :], a["tiny_w_o"]).then_inc(sem("sgu_landed"), 16)
            pool.wait_ge(sem("const_landed"), 16)
            pool.wait_ge(sem("posb_landed"), 16 * 2 * DR)
            flat = posb.rearrange("p h r c -> p (h r) c")
            nc.gpsimd.tensor_tensor(flat, flat, k("window").unsqueeze(1).to_broadcast([P, NH * DR, GRID_W]),
                                    ALU.add).then_inc(sem("posb_ready"), 1)
            for i, (col, n, _) in enumerate(pieces):
                if i == 8:
                    pool.wait_ge(sem("na_summed"), NA_STEPS)
                    for v, at in enumerate((2, 5, 4, 3)):
                        pool.dma_start(rows[:, v, :], bcast("b_ada", at * D, D)).then_inc(sem("rows_landed"), 16)
                    pool.dma_start(ffn_g, bcast("norm_ffn_g", 0, D)).then_inc(sem("rows_landed"), 16)
                if i >= 2:
                    wait_out(pool, pieces[i - 2][2])
                    pool.dma_start(bias[:, i % 2, 0:n], bcast("b_in", col, n)).then_inc(sem(f"bias_landed{i % 2}"), 16)
            wait_out(pool, ("oaT", 3))
            wait_out(pool, ("obT", 1))
            pool.dma_start(fin_g, bcast("final_norm_g", 0, D)).then_inc(sem("fin_landed"), 16)
            wait_full(pool, ("upb", 1, 1))
            pool.dma_start(w_rt, a["w_router"].rearrange("(k p) n -> p k n", p=P)).then_inc(sem("router_landed"), 16)
            pool.dma_start(rt_b, bcast("b_router", 0, E)).then_inc(sem("router_landed"), 16)

            def gather(e, slot):
                nc.gpsimd.tensor_copy(token_now[0:CAP, slot:slot + 1], token_of[0:CAP, bass.ds(e, 1)])\
                    .then_inc(sem("token_now_ready"), 1)
                pool.wait_ge(sem("token_now_ready"), e + 1)
                pool.sem_inc(sem("gathers_begun"), 1)
                nc.gpsimd.indirect_dma_start(
                    out=xg[0:CAP, slot, :], out_offset=None, in_=a["h2_rows"],
                    in_offset=bass.IndirectOffsetOnAxis(ap=token_now[0:CAP, slot:slot + 1], axis=0),
                ).then_inc(sem(f"gathered{slot}"), 16)

            pool.wait_ge(sem("h2_stored"), 16)
            wait_out(pool, ("ix", 0))
            gather(0, 0)
            gather(1, 1)
            wait_out(pool, ("ix", 1))
            with pool.Fori(0, (E - 1) // ROUND) as it:
                for j in range(ROUND):
                    b, n, per = banks[("gT", j, 1)]
                    assert n + 1 > per
                    pool.wait_ge(bank_full[b], n + 1 - per + it * per)
                    if j:
                        wait_full(pool, ("gT", ("first", "second")[j - 1], 1))
                    gather(it * ROUND + j + 2, (j + 2) % ROUND)
            pool.wait_ge(sem("row_of_ready"), 1)
            for i in range(TT * TOP_K):
                j, t = divmod(i, TT)
                if t == 0:
                    last_e = E - TOP_K + j
                    for e in range(last_e - 2, last_e + 1) if j == 0 else (last_e,):
                        pool.wait_ge(sem(f"rows_stored{e % ROUND}"), 16 * (2 + e // ROUND))
                if i >= len(back):
                    pool.wait_ge(sem("row_added"), i - len(back) + 1)
                at = t * TOP_K + j
                nc.gpsimd.indirect_dma_start(
                    out=back[i % len(back)], out_offset=None, in_=a["expert_rows"][0:E - TOP_K + j + 1].rearrange("e c d -> (e c) d"),
                    in_offset=bass.IndirectOffsetOnAxis(ap=row_of[:, at:at + 1], axis=0),
                ).then_inc(sem(f"returned{i % len(back)}"), 16)
            with pool.Fori(0, L2) as layer:
                pool.wait_ge(sem("x_new"), TT + 2 * TT * layer)
                for j, name in enumerate(("ln_mix_g_2", "ln_mix_b_2", "ln_ffn_g_2", "ln_ffn_b_2")):
                    row = a[name][layer]
                    pool.dma_start(ln[:, j, :], row.partition_broadcast(P)).then_inc(sem("ln_landed"), 16)

        def wait_weights_of_item(eng, i, it):
            if i < NI:
                eng.wait_ge(sem("stick_weights"), NI * it + i + 1)
            else:
                wait_out(eng, ("sc", i), it)

        @block.tensor
        def _(pe):
            mm = nc.tensor.matmul

            def turn(dst, src, m=P):
                return nc.tensor.transpose(dst, src, k("ident")[0:m, 0:m])

            def turns(key, pieces_, it=0):
                wait_bank(pe, key, it)
                for j, src in enumerate(pieces_):
                    last = turn(bank(key)[0:src.shape[1], j * P:(j + 1) * P], src)
                full(last, key)

            def turn_pair(key, src, g):
                turns(key, [src[:, t, (2 * g + j) * P:(2 * g + j + 1) * P] for j in range(2) for t in range(TT)])

            def turn_tile(name, src, t, it=0):
                count_ = src.shape[2] // CHUNK
                for half in range(count_):
                    turns(name + (count_ * t + half,), [src[:, t, (4 * half + j) * P:(4 * half + j + 1) * P] for j in range(4)], it)

            def wait_tile(name, t, halves=2, it=0):
                for half in range(halves):
                    wait_out(pe, name + (halves * t + half,), it)

            def token_major(key, left, t, units_, kts, it=0, cols_=CHUNK, done=True):
                wait_bank(pe, key, it)
                n = 0
                for uk in units_:
                    wait_weights(pe, uk, it)
                    wv = w(uk, kts, cols_)
                    for j in range(kts):
                        last = mm(bank(key)[:, 0:cols_], left[:, n, t * P:(t + 1) * P], wv[:, j, :],
                                  start=(n == 0), stop=(n == kts * len(units_) - 1))
                        n += 1
                full(last, key)

            def feature_major(key, right, tokens, units_, fts, it=0):
                wait_bank(pe, key, it)
                for s_, f in enumerate(fts):
                    for n in range(KT):
                        uk = units_[n // 4]
                        if s_ == 0 and n % 4 == 0:
                            wait_weights(pe, uk, it)
                        last = mm(bank(key)[:, s_ * tokens:(s_ + 1) * tokens],
                                  w(uk, 4, CHUNK)[:, n % 4, f * P:(f + 1) * P], right[:, n, 0:tokens],
                                  start=(n == 0), stop=(n == KT - 1))
                full(last, key)

            def both(key):
                return [key + (0,), key + (1,)]

            pe.wait_ge(sem("silu_ready"), 1)
            job = ("mod", 0)
            for n in (1, 3):
                for u in both(("ada", n)):
                    wait_weights(pe, u)
                for f in range(4):
                    at = 2 * (4 * n + f)
                    for kt in range(KT):
                        mm(bank(job)[:, at:at + 2], w(("ada", n, kt // 4), 4, CHUNK)[:, kt % 4, f * P:(f + 1) * P],
                           sc_col[:, 2 * kt:2 * kt + 2], start=(kt == 0), stop=(kt == KT - 1))
            pe.wait_ge(sem("const_landed"), 16)
            for n in (0, 2):
                pe.wait_ge(sem("ada_summed"), n // 2 + 1)
                for f in range(4):
                    for which in range(2):
                        at = 2 * (4 * n + f) + which
                        last = mm(bank(job)[:, at:at + 1], ada0[:, n // 2, which, f * P:(f + 1) * P], k("ones")[:, 0:1],
                                  start=True, stop=True)
            full(last, job)
            for g in range(4):
                pe.wait_ge(sem("x_normed"), 2 * TT)
                turn_pair(("xT", g), xn, g)
                turn_pair(("cT", g), cn, g)
            for g in range(4):
                wait_out(pe, ("xT", g))
                wait_out(pe, ("cT", g))
            for t in range(4):
                token_major(("tiny", t), hT, t, [("win", "tiny")], KT, cols_=3 * TINY)
            for p in range(2):
                feature_major(("nq", p), hT, S, both(("win", "nq")), (2 * p, 2 * p + 1))
            for f in range(4):
                feature_major(("nk", f), hT, 2 * S, both(("win", "nk")), (f,))
            for t in range(4):
                token_major(("nv", t), hT, t, both(("win", "nv")), 4)
            pe.wait_ge(sem("tiny_roped"), 1)
            turns(("tqT", 0), [tqkv[:, t, 0:TINY] for t in range(TT)])
            turns(("tkT", 0), [tqkv[:, t, TINY:2 * TINY] for t in range(4)])
            wait_out(pe, ("tqT", 0))
            wait_out(pe, ("tkT", 0))
            for t in range(TT):
                wait_bank(pe, ("ts", t))
                full(mm(bank(("ts", t))[:, :], tT[0:TINY, t * P:(t + 1) * P], tT[0:TINY, S:S + CHUNK],
                        start=True, stop=True), ("ts", t))
            for t in range(TT):
                pe.wait_ge(sem("tiny_probs"), t + 1)
                turns(("tpT", t), [pr[:, t, j * P:(j + 1) * P] for j in range(4)])
                wait_out(pe, ("tpT", t))
                wait_bank(pe, ("tO", t))
                for j in range(4):
                    last = mm(bank(("tO", t))[0:TINY, 0:P], tqkv[:, j, 2 * TINY:3 * TINY],
                              prT[:, t, j * P:(j + 1) * P], start=(j == 0), stop=(j == 3))
                full(last, ("tO", t))

            fill = [(name, n, t) for name in "vu" for n in range(2) for t in range(TT)]
            for p in range(2):
                wait_out(pe, ("nq", p))
            for f in range(4):
                wait_out(pe, ("nk", f))
            for t in range(4):
                wait_out(pe, ("nv", t))
            for i in range(NA_STEPS + 2):
                if i < NA_STEPS:
                    t, h = divmod(i, NH)
                    r = h % 4 * NDH
                    wait_bank(pe, ("ns", i))
                    full(mm(bank(("ns", i))[:, :], nqT[r:r + NDH, h // 4, t * P:(t + 1) * P],
                            nkT[r:r + NDH, h // 4, :], start=True, stop=True), ("ns", i))
                if i < NA_STEPS:
                    name, n, t = fill[i // 4]
                    q, weights = i % 4, ("win", name, n, i % 4 // 2)
                    if q == 0:
                        wait_bank(pe, (name, n, t))
                    if q % 2 == 0:
                        wait_weights(pe, weights)
                    for kt in (2 * q, 2 * q + 1):
                        last = mm(bank((name, n, t))[:, :], hT[:, kt, t * P:(t + 1) * P], w(weights, 4, CHUNK)[:, kt % 4, :],
                                  start=(kt == 0), stop=(kt == KT - 1))
                    if q == 3:
                        full(last, (name, n, t))
                if 1 <= i <= NA_STEPS:
                    wait_out(pe, ("ns", i - 1))
                    turns(("npT", i - 1), [pr[:, (i - 1) % 2, j * P:(j + 1) * P] for j in range(4)])
                if i >= 2:
                    t, h = divmod(i - 2, NH)
                    wait_out(pe, ("npT", i - 2))
                    if h == 0:
                        wait_bank(pe, ("nO", t))
                    for j in range(4):
                        last = mm(bank(("nO", t))[:, h * NDH:(h + 1) * NDH], prT[:, (i - 2) % 2, j * P:(j + 1) * P],
                                  nv[:, j, h * NDH:(h + 1) * NDH], start=(j == 0), stop=(j == 3))
                    last.then_inc(sem("na_summed"), 1)
            def spread(i):
                pe.wait_ge(sem("ada_summed"), 3 + i)
                wait_bank(pe, ("row", i))
                full(mm(bank(("row", i))[:, :], k("ones"), ada[:, i % 4, :], start=True, stop=True), ("row", i))

            for i, (name, n) in enumerate(GATES):
                for t in range(TT):
                    token_major((name, n, t), hT, t, both(("win", name, n)), 4)
                if i:
                    spread(2 * i - 2)
                    spread(2 * i - 1)
            spread(6)
            spread(7)
            pe.wait_ge(sem("sgu_landed"), 64)
            for t in range(TT):
                wait_out(pe, ("tO", t))
                pe.wait_ge(sem("v_normed"), t + 1)
                for n in range(2):
                    key = ("sg", t, n)
                    wait_bank(pe, key)
                    for g in range(4):
                        at = (4 * n + g) * P
                        mm(bank(key)[:, g * P:(g + 1) * P], ttT[0:TINY, t * P:(t + 1) * P], w_tiny[0:TINY, at:at + P],
                           start=True, stop=False)
                        last = mm(bank(key)[:, g * P:(g + 1) * P], wsT[:, 4 * n + g, :], v_[:, t, at:at + P],
                                  start=False, stop=True)
                    full(last, key)
            for t in range(TT):
                wait_out(pe, ("nO", t))
                turn_tile(("obT",), ob, t)
            for t in range(TT):
                for n in range(2):
                    wait_out(pe, ("sg", t, n))
                turn_tile(("oaT",), u_, t)
            for t in range(TT):
                wait_tile(("oaT",), t)
                wait_tile(("obT",), t, 1)
                for n in range(2):
                    token_major(("upa", n, t), oaT, t, both(("upa", n)), 4)
                    token_major(("upb", n, t), obT, t, [("upb", n)], 4)
            pe.wait_ge(sem("merged"), TT)
            turn_tile(("mT",), mg, 0)
            wait_tile(("mT",), 0)
            token_major(("wo", 0, 0), mT, 0, both(("wo", 0)), 4)
            pe.wait_ge(sem("merged"), 2 * TT)
            turn_tile(("mT",), mg, 1)
            token_major(("wo", 1, 0), mT, 0, both(("wo", 1)), 4)
            wait_tile(("mT",), 1)
            for n in range(2):
                token_major(("wo", n, 1), mT, 1, both(("wo", n)), 4)
            for t in range(TT):
                pe.wait_ge(sem("h2_ready"), t + 1)
                turn_tile(("h2T",), h2, t)
            pe.wait_ge(sem("router_landed"), 32)
            for t in range(TT):
                wait_tile(("h2T",), t)
                wait_bank(pe, ("rt", t))
                for kt in range(KT):
                    last = mm(bank(("rt", t))[:, 0:E], h2T[:, kt, t * P:(t + 1) * P], w_rt[:, kt, :],
                              start=(kt == 0), stop=(kt == KT - 1))
                full(last, ("rt", t))

            def gate_up(key, right, gk, uk, f, f_in_unit, it=0):
                wait_bank(pe, key, it)
                for j, unit_key in enumerate((gk, uk)):
                    wait_weights(pe, unit_key, it)
                    for kt in range(KT):
                        last = mm(bank(key)[:, j * S:(j + 1) * S], w(unit_key, KT, FF)[:, kt, f_in_unit * P:(f_in_unit + 1) * P],
                                  right[:, kt, :], start=(kt == 0), stop=(kt == KT - 1))
                full(last, key)

            for f in range(2):
                gate_up(("shg", f), h2T, ("shg",), ("shu",), f, f)
            pe.wait_ge(sem("chosen"), TT)
            for t in range(TT):
                wait_bank(pe, ("rk", t))
                for other in range(t + 1):
                    last = mm(bank(("rk", t))[:, 0:E], k("earlier" if other == t else "ones"), rep_[:, other, :],
                              start=(other == 0), stop=(other == t))
                full(last, ("rk", t))
            wait_bank(pe, ("cnt", 0))
            for t in range(TT):
                last = mm(bank(("cnt", 0))[:, 0:E], k("ones"), rep_[:, t, :], start=(t == 0), stop=(t == TT - 1))
            full(last, ("cnt", 0))

            for i, batches in enumerate((range(1), range(1, E // XB))):
                wait_bank(pe, ("ix", i))
                for b in batches:
                    pe.wait_ge(sem("onehot_ready"), TT * (b + 1))
                    for j in range(XB):
                        for t in range(TT):
                            at = (t * XB + j) * CAP
                            last = mm(bank(("ix", i))[0:CAP, XB * b + j:XB * b + j + 1], onehot[:, b % ROUND, at:at + CAP],
                                      k("token")[:, t:t + 1], start=(t == 0), stop=(t == TT - 1))
                    if b == batches[-1]:
                        last.then_inc(sem("slots_found"), 1)
                    else:
                        last.then_inc(sem("onehot_used"), 1)

            for f in range(2):
                wait_out(pe, ("shg", f))
            wait_weights(pe, ("shd",))
            for n in range(2):
                for t in range(TT):
                    key = ("shd", n, t)
                    wait_bank(pe, key)
                    for f in range(2):
                        last = mm(bank(key)[:, :], ffs[:, f, t * P:(t + 1) * P],
                                  w(("shd",), 2, D)[:, f, n * CHUNK:(n + 1) * CHUNK], start=(f == 0), stop=(f == 1))
                    full(last, key)

            def turn_rows(which, slot, it=0):
                for half in range(2):
                    key = ("gT", which, half)
                    wait_bank(pe, key, it)
                    for j in range(4):
                        src = xg[0:CAP, slot, :].rearrange("c (p k) -> c k p", k=KT)[:, 4 * half + j, :]
                        last = turn(bank(key)[:, j * CAP:(j + 1) * CAP], src, CAP)
                    full(last, key)

            def expert_hidden(which, slot, it=0):
                key = ("gu", which)
                wait_bank(pe, key, it)
                for j, u in enumerate(("eg", "eu")):
                    wait_weights(pe, (u, which), it)
                    wv = w((u, which), KT, FF).rearrange("p k (m f) -> p k f m", f=2)
                    for f in range(2):
                        at = (2 * j + f) * CAP
                        for kt in range(KT):
                            last = mm(bank(key)[:, at:at + CAP], wv[:, kt, f, :], xgT[:, slot, kt * CAP:(kt + 1) * CAP],
                                      start=(kt == 0), stop=(kt == KT - 1))
                full(last, key)

            def expert_down(which, slot, it=0):
                wait_weights(pe, ("ed", which), it)
                for n in range(2):
                    key = ("yd", which, n)
                    wait_bank(pe, key, it)
                    for f in range(2):
                        last = mm(bank(key)[0:CAP, :], hid[:, slot, f * CAP:(f + 1) * CAP],
                                  w(("ed", which), 2, D)[:, f, n * CHUNK:(n + 1) * CHUNK], start=(f == 0), stop=(f == 1))
                    full(last, key)

            pe.wait_ge(sem("gathered0"), 16)
            turn_rows("first", 0)
            for half in range(2):
                wait_out(pe, ("gT", "first", half))
            expert_hidden("first", 0)
            pe.wait_ge(sem("gathered1"), 16)
            turn_rows("second", 1)
            with pe.Fori(0, (E - 1) // ROUND) as it:
                for j in range(ROUND):
                    for half in range(2):
                        if j:
                            wait_out(pe, ("gT", j - 1, half), it)
                        else:
                            wait_around(pe, ("gT", "second", half), ("gT", ROUND - 1, half), it)
                    expert_hidden(j, (j + 1) % ROUND, it)
                    s_ = (j + 2) % ROUND
                    pe.wait_ge(sem(f"gathered{s_}"), 16 * (it + (2 if s_ < 2 else 1)))
                    turn_rows(j, s_, it)
                    if j:
                        wait_out(pe, ("gu", j - 1), it)
                    else:
                        wait_around(pe, ("gu", "first"), ("gu", ROUND - 1), it)
                    expert_down(j, j, it)
            wait_out(pe, ("gu", ROUND - 1), (E - 1) // ROUND - 1)
            expert_down("last", 0)

            def products(e, done):
                pe.wait_ge(sem("over_landed"), 48 * done + 48)
                pe.wait_ge(sem("over_vector"), 6 * done + 1)
                for f in range(2):
                    for j in range(2):
                        wv = ring[:, j, :].rearrange("p (k n) -> p k n", n=FF)
                        for kt in range(KT):
                            last = mm(psum[f][:, j * S:(j + 1) * S], wv[:, kt, f * P:(f + 1) * P], h2T[:, kt, :],
                                      start=(kt == 0), stop=(kt == KT - 1))
                    last.then_inc(sem("over_tensor"), 1)
                pe.wait_ge(sem("over_vector"), 6 * done + 3)
                wv = ring[:, 2, :].rearrange("p (k n) -> p k n", n=D)
                for n in range(2):
                    for t in range(TT):
                        for f in range(2):
                            last = mm(psum[2 + 2 * n + t][:, :], ffs[:, f, t * P:(t + 1) * P],
                                      wv[:, f, n * CHUNK:(n + 1) * CHUNK], start=(f == 0), stop=(f == 1))
                        last.then_inc(sem("over_tensor"), 1)

            for n in range(2):
                wait_out(pe, ("yd", "last", n))
            pe.sem_inc(sem("over_tensor"), 1)
            overflow(pe, products)
            with pe.Fori(0, L2) as layer:
                for t in range(TT):
                    pe.wait_ge(sem("x_new"), t + 1 + 2 * TT * layer)
                    turn_tile(("l_xT",), x, t, layer)
                for g in range(4):
                    wait_out(pe, ("l_xT", g), layer)
                for name in ("qs", "ks"):
                    for p in range(2):
                        feature_major((name, p), xT, S, both(("l_in", name)), (2 * p, 2 * p + 1), layer)
                for t in range(TT):
                    token_major(("vs", t), xT, t, both(("l_in", "vs")), 4, layer)
                for name in ("qs", "ks", "vs"):
                    for p in range(2):
                        wait_out(pe, (name, p), layer)
                for i in range(2 * NI + 2):
                    if i < 2 * NI:
                        b = i // NI
                        if i == NI:
                            for name in ("qmT", "kmT"):
                                for p in range(2):
                                    wait_out(pe, (name, p), layer)
                            for t in range(TT):
                                wait_out(pe, ("vm", 0, t), layer)
                        t, h0, nh, keys = ITEMS[i % NI]
                        q, kk = ((qsT, ksT), (qmT, kmT))[b]
                        wait_bank(pe, ("sc", i), layer)
                        for j in range(nh):
                            h = HEAD[h0 + j]
                            r = h % 2 * DH2
                            last = mm(bank(("sc", i))[:, j * keys:(j + 1) * keys], q[r:r + DH2, h // 2, t * P:(t + 1) * P],
                                      kk[r:r + DH2, h // 2, 0:keys], start=True, stop=True)
                        full(last, ("sc", i))
                    if i < len(FILLERS):
                        name, n, t = FILLERS[i]
                        token_major((name, n, t), xT, t, both(("l_in", name, n)), 4, layer)
                    if 1 <= i <= 2 * NI:
                        wait_weights_of_item(pe, i - 1, layer)
                        turns(("wT", i - 1), [rw[:, (i - 1) % 2, j * P:(j + 1) * P] for j in range(4)], layer)
                    if i >= 2:
                        b, (t, h0, nh, keys) = (i - 2) // NI, ITEMS[(i - 2) % NI]
                        wait_out(pe, ("wT", i - 2), layer)
                        if h0 == 0:
                            wait_bank(pe, ("o", b, t), layer)
                        val = (vs, vm)[b]
                        kts = keys // P
                        for j in range(nh):
                            h, to = HEAD[h0 + j], (h0 + j) * DH2
                            for kt in range(kts):
                                at = (j * kts + kt) * P
                                last = mm(bank(("o", b, t))[:, to:to + DH2], wT_[:, i % 2, at:at + P],
                                          val[:, kt, h * DH2:(h + 1) * DH2], start=(kt == 0), stop=(kt == kts - 1))
                        last.then_inc(sem("item_summed"), 1)
                    if i == NI - 1:
                        pe.wait_ge(sem("roped"), 2 * TT * (layer + 1))
                        for which, name in enumerate(("qmT", "kmT")):
                            for t in range(TT):
                                turn_tile((name,), qk[:, which], t, layer)
                for b in range(2):
                    for t in range(TT):
                        wait_out(pe, ("o", b, t), layer)
                        turn_tile(("oT", b), o[:, b], t, layer)
                for b in range(2):
                    for p in range(2):
                        wait_out(pe, ("oT", b, p), layer)
                ot = [oT[:, b, :].rearrange("p (f t) -> p f t", t=S) for b in range(2)]
                for t in range(TT):
                    for n in range(2):
                        token_major(("bs", n, t), ot[0], t, [("bs", n)], 4, layer)
                        token_major(("bm", n, t), ot[1], t, [("bm", n)], 4, layer)
                pe.wait_ge(sem("l_merged"), 2 * TT * layer + 2)
                turn_tile(("l_mT",), lmg, 0, layer)
                wait_tile(("l_mT",), 0, 2, layer)
                token_major(("l_wo", 0, 0), lmT, 0, both(("l_wo", 0)), 4, layer)
                pe.wait_ge(sem("l_merged"), 2 * TT * (layer + 1))
                turn_tile(("l_mT",), lmg, 1, layer)
                token_major(("l_wo", 1, 0), lmT, 0, both(("l_wo", 1)), 4, layer)
                wait_tile(("l_mT",), 1, 2, layer)
                for n in range(2):
                    token_major(("l_wo", n, 1), lmT, 1, both(("l_wo", n)), 4, layer)
                for t in range(TT):
                    pe.wait_ge(sem("x_new"), TT + t + 1 + 2 * TT * layer)
                    turn_tile(("l_yT",), x, t, layer)
                for g in range(4):
                    wait_out(pe, ("l_yT", g), layer)
                PASSES = ((0, 0), (0, 1), (1, 0))
                for pair in range(FT // 2 + 1):
                    if pair < FT // 2:
                        for f in range(2):
                            key = ("fg", 2 * pair + f)
                            wait_bank(pe, key, layer)
                            for j, name in enumerate(("fg", "fu")):
                                u = FFN_UNITS.index((name, pair))
                                if f == 0:
                                    wait_split(pe, u, layer)
                                wv = ws[:, u % SPLIT_SLOTS].rearrange("p w (k n) -> p w k n", n=FF)
                                for kt in range(KT):
                                    for i, (a_, b_) in enumerate(PASSES):
                                        last = mm(bank(key)[:, j * S:(j + 1) * S], wv[:, a_, kt, f * P:(f + 1) * P],
                                                  xs[:, b_, kt, :], start=(kt == 0 and i == 0), stop=(kt == KT - 1 and i == 2))
                            full(last, key)
                    if pair:
                        d = pair - 1
                        u = FFN_UNITS.index(("fd", d))
                        pe.wait_ge(sem("hidden_split"), FT * layer + 2 * pair)
                        wait_split(pe, u, layer)
                        wv = ws[:, u % SPLIT_SLOTS].rearrange("p w (k n) -> p w k n", n=D)
                        for t in range(TT):
                            for n in range(2):
                                key = ("fd", n, t)
                                if d == 0:
                                    wait_bank(pe, key, layer)
                                for f in range(2):
                                    for i, (a_, b_) in enumerate(PASSES):
                                        last = mm(bank(key)[:, :], fh[:, (2 * d + f) % 4, a_, t * P:(t + 1) * P],
                                                  wv[:, b_, f, n * CHUNK:(n + 1) * CHUNK],
                                                  start=(d == 0 and f == 0 and i == 0),
                                                  stop=(d == FT // 2 - 1 and f == 1 and i == 2))
                                if d == FT // 2 - 1:
                                    full(last, key)
                        if d < FT // 2 - 1:
                            last.then_inc(sem("down_done"), 1)

        @block.scalar
        def _(act):
            A = nc.scalar.activation

            def turned(name, dst, halves=2, it=0, tiles=range(TT)):
                for t in tiles:
                    for half in range(halves):
                        key = name + (halves * t + half,)
                        wait_full(act, key, it)
                        out(A(dst[:, 4 * half:4 * half + 4, t * P:(t + 1) * P],
                              bank(key)[:, :].rearrange("p (a b) -> p a b", b=P), ACT.Copy), key)

            act.wait_ge(sem("cols_landed"), 16)
            A(sc_col, c_col, ACT.Silu).then_inc(sem("silu_ready"), 1)
            act.wait_ge(sem("norm_sums"), 1)
            A(small[:, 4:8], small[:, 0:4], ACT.Sqrt).then_inc(sem("norm_roots"), 1)
            act.wait_ge(sem("mix_scale"), 1)
            for g in range(4):
                wait_full(act, ("cT", g))
                for j in range(2):
                    ft = 2 * g + j
                    last = A(hT[:, ft, S:2 * S], bank(("cT", g))[:, j * S:(j + 1) * S], ACT.Identity,
                             bias=mod[:, 2 * ft + 1:2 * ft + 2], scale=mixA[:, 2 * ft + 1:2 * ft + 2])
                out(last, ("cT", g))
            for f in range(4):
                wait_full(act, ("nk", f))
                out(A(nkT[:, f, :], bank(("nk", f))[:, :], ACT.Identity, bias=in_b[:, 4 + f:5 + f]), ("nk", f))
            wait_full(act, ("tqT", 0))
            out(A(tT[0:TINY, 0:S], bank(("tqT", 0))[0:TINY, 0:S], ACT.Copy), ("tqT", 0))
            wait_full(act, ("tkT", 0))
            out(A(tT[0:TINY, S:S + CHUNK], bank(("tkT", 0))[0:TINY, :], ACT.Copy), ("tkT", 0))
            for t in range(TT):
                act.wait_ge(sem("tiny_max"), t + 1)
                out(A(pr[:, t, :], bank(("ts", t))[:, :], ACT.Exp, bias=small[:, 10 + t:11 + t], scale=TINY ** -0.5,
                      accum_out=small[:, 12 + t:13 + t]), ("ts", t))
            for t in range(TT):
                wait_full(act, ("tpT", t))
                out(A(prT[:, t, :], bank(("tpT", t))[:, :], ACT.Copy), ("tpT", t))
                wait_full(act, ("tO", t))
                out(A(ttT[0:TINY, t * P:(t + 1) * P], bank(("tO", t))[0:TINY, 0:P], ACT.Copy), ("tO", t))
            for i in range(NA_STEPS + 1):
                if i < NA_STEPS:
                    act.wait_ge(sem("na_max"), i + 1)
                    if i >= 2:
                        wait_full(act, ("npT", i - 2))
                    out(A(pr[:, i % 2, :], bank(("ns", i))[:, :], ACT.Exp, bias=cols_na[0][:, i:i + 1],
                          accum_out=cols_na[1][:, i:i + 1]), ("ns", i))
                if i >= 1:
                    j = i - 1
                    wait_full(act, ("npT", j))
                    if j >= 2:
                        act.wait_ge(sem("na_summed"), j - 1)
                    out(A(prT[:, j % 2, :], bank(("npT", j))[:, :], ACT.Copy), ("npT", j))
            for which, (buf, name) in enumerate(((v_, "v"), (u_, "u"))):
                for t in range(TT):
                    for n in range(2):
                        wait_out(act, (name, n, t))
                    A(buf[:, t, :], buf[:, t, :], ACT.Gelu).then_inc(sem("gelu_done"), 1)
            act.wait_ge(sem("v_var"), 1)
            A(small[:, 20:22], small[:, 18:20], ACT.Sqrt).then_inc(sem("v_root"), 1)
            for buf, name in ((ga, "ga"), (gb, "gb")):
                for t in range(TT):
                    for n in range(2):
                        wait_out(act, (name, n, t))
                    A(buf[:, t, :], buf[:, t, :], ACT.Sigmoid).then_inc(sem("gates_done"), 1)
            turned(("obT",), obT, 1)
            turned(("oaT",), oaT)
            turned(("mT",), mT)
            for t in range(TT):
                act.wait_ge(sem("sums2"), t + 1)
                A(small[:, 26 + t:27 + t], small[:, 24 + t:25 + t], ACT.Sqrt).then_inc(sem("roots2"), 1)
            turned(("h2T",), h2T)
            for t in range(TT):
                wait_full(act, ("rt", t))
                out(A(score[:, t, :], bank(("rt", t))[:, 0:E], ACT.Sigmoid), ("rt", t))

            def silus(job, it=0):
                for f in range(2):
                    wait_full(act, (job, f), it)
                    A(act_ff[:, f, :], bank((job, f))[:, 0:S], ACT.Silu).then_inc(sem("silu_done"), 1)

            act.wait_ge(sem("h2_ready"), TT)
            act.dma_start(a["h2_rows"].rearrange("(t p) d -> p t d", p=P), h2).then_inc(sem("h2_stored"), 16)
            silus("shg")

            def rows_out(which, slot, it=0):
                wait_full(act, ("gT", which, 0), it)
                out(A(xgT[:, slot, 0:4 * CAP], bank(("gT", which, 0))[:, 0:4 * CAP], ACT.Copy), ("gT", which, 0))

            def silu_of(which, slot, it=0):
                wait_full(act, ("gu", which), it)
                A(sil[:, slot, :], bank(("gu", which))[:, 0:2 * CAP], ACT.Silu).then_inc(sem("sil_done"), 1)

            def output(which, slot, it, row):
                act.wait_ge(sem(f"rows_stored{slot}"), 16 * (it + 1))
                wait_full(act, ("yd", which, 0), it)
                out(A(ys[0:CAP, slot, 0:CHUNK], bank(("yd", which, 0))[0:CAP, :], ACT.Copy), ("yd", which, 0))
                for n in range(2):
                    wait_out(act, ("yd", which, n), it)
                act.dma_start(a["expert_rows"][row], ys[0:CAP, slot, :]).then_inc(sem(f"rows_stored{slot}"), 16)

            for s_ in range(ROUND):
                act.sem_inc(sem(f"rows_stored{s_}"), 16)
            rows_out("first", 0)
            silu_of("first", 0)
            rows_out("second", 1)
            with act.Fori(0, (E - 1) // ROUND) as it:
                for j in range(ROUND):
                    silu_of(j, (j + 1) % ROUND, it)
                    rows_out(j, (j + 2) % ROUND, it)
                    output(j, j, it, it * ROUND + j)
            output("last", 0, (E - 1) // ROUND, E - 1)

            def silus_over(e, done):
                for f in range(2):
                    act.wait_ge(sem("over_tensor"), 6 * done + 2 + f)
                    A(act_ff[:, f, :], psum[f][:, 0:S], ACT.Silu).then_inc(sem("over_scalar"), 1)

            overflow(act, silus_over)
            for t in range(TT):
                act.wait_ge(sem("sums3"), t + 1)
                A(small[:, 34 + t:35 + t], small[:, 32 + t:33 + t], ACT.Sqrt).then_inc(sem("roots3"), 1)

            with act.Fori(0, L2) as layer:
                turned(("l_xT",), xT, 2, layer)
                for p in range(2):
                    wait_full(act, ("ks", p), layer)
                    out(A(ksT[:, 2 * p:2 * p + 2, :].rearrange("p a b -> p (a b)"), bank(("ks", p))[:, :], ACT.Copy), ("ks", p))
                for i in range(2 * NI + 3):
                    if 1 <= i <= len(FILLERS):
                        name, n, t = FILLERS[i - 1]
                        if name in ("gs", "gm"):
                            wait_full(act, (name, n, t), layer)
                            out(A(gates[:, ("gs", "gm").index(name), t, n * CHUNK:(n + 1) * CHUNK],
                                  bank((name, n, t))[:, :], ACT.Exp, scale=-1.0), (name, n, t))
                    if 2 <= i <= 2 * NI + 1:
                        j = i - 2
                        wait_full(act, ("wT", j), layer)
                        act.wait_ge(sem("item_summed"), 2 * NI * layer + j - 1) if j >= 2 else None
                        out(A(wT_[:, j % 2, :], bank(("wT", j))[:, :], ACT.Copy), ("wT", j))
                    if i == NI:
                        for name, dst in (("qmT", qmT), ("kmT", kmT)):
                            turned((name,), dst, 1, layer)
                    if i < NI:
                        wait_full(act, ("sc", i), layer)
                        A(es[:, i % 2, :], bank(("sc", i))[:, :], ACT.Abs).then_inc(sem("abs_ready"), 1)
                        act.wait_ge(sem("abs_ready"), NI * layer + i + 1)
                        A(es[:, i % 2, :], es[:, i % 2, :], ACT.Exp, scale=-1.0).then_inc(sem("exp_done"), 1)
                        act.wait_ge(sem("exp_done"), NI * layer + i + 1)
                        A(es[:, i % 2, :], es[:, i % 2, :], ACT.Ln, bias=1.0).then_inc(sem("ln_done"), 1)
                    if NI <= i < 2 * NI:
                        t, h0, nh, keys = ITEMS[i - NI]
                        act.wait_ge(sem("mb_max"), NI * layer + i - NI + 1)
                        if i >= 2:
                            wait_full(act, ("wT", i - 2), layer)
                        for j in range(nh):
                            hh = t * H2 + h0 + j
                            last = A(rw[:, i % 2, j * keys:(j + 1) * keys], bank(("sc", i))[:, j * keys:(j + 1) * keys],
                                     ACT.Exp, bias=mbn[:, hh:hh + 1], accum_out=mbs[:, hh:hh + 1])
                        out(last, ("sc", i))
                    if 1 <= i <= NI:
                        act.wait_ge(sem("log_weights"), NI * layer + i)
                        A(rw[:, (i - 1) % 2, :], rw[:, (i - 1) % 2, :], ACT.Exp).then_inc(sem("stick_weights"), 1)
                for b in range(2):
                    turned(("oT", b), oT[:, b, :].rearrange("p (f t) -> p f t", t=S), 1, layer)
                turned(("l_mT",), lmT, 2, layer)

                def high(u):
                    name, pair = FFN_UNITS[u]
                    wait_weights(act, (name, pair), layer)
                    if name == "fg" and pair >= 3:
                        act.wait_ge(sem("down_done"), (FT // 2 - 1) * layer + pair - 2)
                    A(ws[:, u % SPLIT_SLOTS, 0, :], ring[:, units.place[(name, pair)][0], :], ACT.Copy)\
                        .then_inc(sem("high_ready"), 1)

                high(0)
                high(1)
                for t in range(TT):
                    act.wait_ge(sem("l_var"), 2 * TT * layer + t + 1)
                    A(lnv[:, 2 + t:3 + t], lnv[:, t:t + 1], ACT.Sqrt).then_inc(sem("l_root"), 1)
                for g in range(4):
                    wait_full(act, ("l_yT", g), layer)
                    A(xs[:, 0, 4 * (g % 2):4 * (g % 2) + 4, g // 2 * P:(g // 2 + 1) * P],
                      bank(("l_yT", g))[:, :].rearrange("p (a b) -> p a b", b=P), ACT.Copy).then_inc(sem("y_high"), 1)
                for pair in range(FT // 2):
                    if pair < FT // 2 - 1:
                        high(FFN_UNITS.index(("fg", pair + 1)))
                    for f in (2 * pair, 2 * pair + 1):
                        wait_full(act, ("fg", f), layer)
                        if f >= 2:
                            wait_out(act, ("fg", f - 2), layer)
                        A(silu[:, f % 2, :], bank(("fg", f))[:, 0:S], ACT.Silu).then_inc(sem("l_silu"), 1)
                        wait_out(act, ("fg", f), layer)
                        A(fh[:, f % 4, 0, :], fh32[:, f % 4, :], ACT.Copy).then_inc(sem("hidden_high"), 1)
                    if pair < FT // 2 - 1:
                        high(FFN_UNITS.index(("fu", pair + 1)))
                    high(FFN_UNITS.index(("fd", pair)))
                for t in range(TT):
                    act.wait_ge(sem("l_var"), 2 * TT * layer + TT + t + 1)
                    A(lnv[:, 2 + t:3 + t], lnv[:, t:t + 1], ACT.Sqrt).then_inc(sem("l_root"), 1)

        @block.vector
        def _(dve):
            V = nc.vector
            own = sem("vector_step")
            count = [0, 0, 0]

            def step(ins, it=0):
                ins.then_inc(own, 1)
                count[0] += 1
                return ins

            def settle(it=None):
                dve.wait_ge(own, count[0] if it is None else count[0] + it * count[2])

            def rms(src, at, slot):
                for t in range(TT):
                    step(V.tensor_tensor_reduce(junk[:, 0:D], src[:, t, :], src[:, t, :], 1.0 / D, NORM_EPS,
                                                ALU.mult, ALU.add, small[:, at + t:at + t + 1]))
                    settle()

            dve.wait_ge(sem("x_landed"), 16)
            rms(x, 0, 0)
            dve.wait_ge(sem("ctx_landed"), 16)
            rms(cn, 2, 0)
            step(V.tensor_copy(small[:, 0:4], small[:, 0:4]))
            settle()
            V.tensor_copy(small[:, 0:4], small[:, 0:4]).then_inc(sem("norm_sums"), 1)
            dve.wait_ge(sem("norm_roots"), 1)
            step(V.reciprocal(small[:, 4:8], small[:, 4:8]))
            settle()
            for t in range(TT):
                V.tensor_scalar(xn[:, t, :], x[:, t, :], small[:, 4 + t:5 + t], None, ALU.mult).then_inc(sem("x_normed"), 1)
                V.tensor_scalar(cn[:, t, :], cn[:, t, :], small[:, 6 + t:7 + t], None, ALU.mult).then_inc(sem("x_normed"), 1)

            def ada_products(n, into, whiches):
                for kt in range(KT):
                    if kt % 4 == 0:
                        wait_weights(dve, ("ada", n, kt // 4))
                    wv = w(("ada", n, kt // 4), 4, CHUNK)[:, kt % 4, :]
                    for i, which in enumerate(whiches):
                        scale = sc_col[:, 2 * kt + which:2 * kt + which + 1]
                        if kt == 0:
                            last = V.tensor_scalar(into[i], wv, scale, None, ALU.mult)
                        else:
                            last = V.scalar_tensor_tensor(out=into[i], in0=wv, scalar=scale, in1=into[i],
                                                          op0=ALU.mult, op1=ALU.add)
                        if (kt, i) != (KT - 1, len(whiches) - 1):
                            step(last)
                    if kt < KT - 1:
                        settle()
                last.then_inc(sem("ada_summed"), 1)

            dve.wait_ge(sem("silu_ready"), 1)
            for n in (0, 2):
                ada_products(n, [ada0[:, n // 2, which, :] for which in range(2)], range(2))
            dve.wait_ge(sem("cols_landed"), 16)
            dve.wait_ge(sem("const_landed"), 16)
            wait_full(dve, ("mod", 0))
            m3 = mod.rearrange("p (f w) -> p f w", w=2)

            def add_bias(key, f0, nf):
                out(V.tensor_tensor(m3[:, f0:f0 + nf, :], bank(key)[:, 0:2 * nf].rearrange("p (f w) -> p f w", w=2),
                                    ada_b[:, f0:f0 + nf].unsqueeze(2).to_broadcast([P, nf, 2]), ALU.add), key)
                wait_out(dve, key)

            add_bias(("mod", 0), 0, 16)
            step(V.tensor_scalar(mixA, mod[:, 2 * KT:4 * KT], 1.0, None, ALU.add))
            settle()
            a3 = mixA.rearrange("p (f w) -> p f w", w=2)
            V.tensor_tensor(a3, a3, gain[:, 0:KT].unsqueeze(2).to_broadcast([P, KT, 2]), ALU.mult).then_inc(sem("mix_scale"), 1)
            dve.wait_ge(sem("mix_scale"), 1)
            for g in range(4):
                wait_full(dve, ("xT", g))
                for j in range(2):
                    ft = 2 * g + j
                    last = V.tensor_scalar(hT[:, ft, 0:S], bank(("xT", g))[:, j * S:(j + 1) * S],
                                           mixA[:, 2 * ft:2 * ft + 1], mod[:, 2 * ft:2 * ft + 1], ALU.mult, ALU.add)
                    if j == 0:
                        step(last)
                out(last, ("xT", g))

            def biased_out(key, dst, n=CHUNK, lo=0):
                wait_full(dve, key)
                i = piece_of[key[:-1]]
                wait_piece(dve, i)
                out(V.tensor_tensor(dst, bank(key)[:, lo:n], bias[:, i % 2, lo:n], ALU.add), key)

            for t in range(4):
                lo = 0 if t < TT else TINY
                biased_out(("tiny", t), tqkv[:, t, lo:], 3 * TINY, lo)
            for p in range(2):
                wait_full(dve, ("nq", p))
                for j in range(2):
                    f = 2 * p + j
                    last = V.tensor_scalar(nqT[:, f, :], bank(("nq", p))[:, j * S:(j + 1) * S], in_b[:, f:f + 1],
                                           NDH ** -0.5, ALU.add, ALU.mult)
                    if j == 0:
                        step(last)
                out(last, ("nq", p))
            for t in range(TT):
                wait_out(dve, ("tiny", t))
                v4 = tqkv[:, t, 0:2 * TINY].rearrange("p (wa s f) -> p wa s f", s=2, f=16)
                x1, x2 = v4[:, :, 0, :], v4[:, :, 1, :]

                def table(name):
                    tab = k(name)[:, t * 32:(t + 1) * 32].rearrange("p (a f) -> p a f", f=16)
                    return tab

                tmp = [junk[:, j * 64:(j + 1) * 64].rearrange("p (wa f) -> p wa f", f=16) for j in range(4)]
                for j, (src, name) in enumerate(((x1, "tcos"), (x2, "tsin"), (x2, "tcos"), (x1, "tsin"))):
                    for wh in range(2):
                        step(V.tensor_tensor(tmp[j][:, 2 * wh:2 * wh + 2, :], src[:, 2 * wh:2 * wh + 2, :], table(name), ALU.mult))
                settle()
                step(V.tensor_tensor(x1, tmp[0], tmp[1], ALU.subtract))
                last = V.tensor_tensor(x2, tmp[2], tmp[3], ALU.add)
                if t == 0:
                    step(last)
                    settle()
            last.then_inc(sem("tiny_roped"), 1)
            for t in range(4):
                biased_out(("nv", t), nv[:, t, :])
            for t in range(TT):
                wait_full(dve, ("ts", t))
                step(V.tensor_reduce(small[:, 8 + t:9 + t], bank(("ts", t))[:, :], AX_X, ALU.max))
                settle()
                V.tensor_scalar(small[:, 10 + t:11 + t], small[:, 8 + t:9 + t], -TINY ** -0.5, None, ALU.mult).then_inc(sem("tiny_max"), 1)
            for t in range(TT):
                wait_out(dve, ("ts", t))
                step(V.reciprocal(small[:, 14 + t:15 + t], small[:, 12 + t:13 + t]))
                settle()
                V.tensor_scalar(pr[:, t, :], pr[:, t, :], small[:, 14 + t:15 + t], None, ALU.mult).then_inc(sem("tiny_probs"), 1)

            def na_out(t):
                dve.wait_ge(sem("na_summed"), NH * (t + 1))
                step(V.reciprocal(cols_na[1][:, t * NH:(t + 1) * NH], cols_na[1][:, t * NH:(t + 1) * NH]))
                settle()
                out(V.tensor_tensor(ob[:, t, :].rearrange("p (h d) -> p h d", d=NDH),
                                    bank(("nO", t))[:, :].rearrange("p (h d) -> p h d", d=NDH),
                                    cols_na[1][:, t * NH:(t + 1) * NH].unsqueeze(2).to_broadcast([P, NH, NDH]),
                                    ALU.mult), ("nO", t))

            dve.wait_ge(sem("posb_ready"), 1)
            fill = [(name, n, t) for name in "vu" for n in range(2) for t in range(TT)]
            for i in range(NA_STEPS + 1):
                if i < NA_STEPS:
                    t, h = divmod(i, NH)
                    wait_full(dve, ("ns", i))
                    lat = bank(("ns", i))[:, 0:S]
                    r0 = 2 * (TT - 1 - t)
                    step(V.tensor_tensor(lat, lat, posb[:, h, r0:r0 + ROWS, :].rearrange("p r c -> p (r c)"), ALU.add))
                    settle()
                    step(V.tensor_reduce(cols_na[0][:, i:i + 1], bank(("ns", i))[:, :], AX_X, ALU.max))
                    settle()
                    V.tensor_scalar(cols_na[0][:, i:i + 1], cols_na[0][:, i:i + 1], -1.0, None, ALU.mult).then_inc(sem("na_max"), 1)
                if i and i % 4 == 0:
                    name, n, t = fill[i // 4 - 1]
                    biased_out((name, n, t), (v_ if name == "v" else u_)[:, t, n * CHUNK:(n + 1) * CHUNK])
                if i == NH + 2:
                    na_out(0)
            na_out(1)
            for t in range(TT):
                dve.wait_ge(sem("gelu_done"), t + 1)
                for n in range(2):
                    step(V.bn_stats(small[:, 40 + 6 * n:46 + 6 * n], v_[:, t, n * CHUNK:(n + 1) * CHUNK]))
                settle()
                step(V.bn_aggr(small[:, 52 + 2 * t:54 + 2 * t], small[:, 40:52]))
                settle()
            for t in range(TT):
                last = V.tensor_scalar(small[:, 18 + t:19 + t], small[:, 53 + 2 * t:54 + 2 * t], NORM_EPS, None, ALU.add)
                if t == 0:
                    step(last)
            last.then_inc(sem("v_var"), 1)
            dve.wait_ge(sem("v_root"), 1)
            step(V.reciprocal(small[:, 20:22], small[:, 20:22]))
            settle()
            dve.wait_ge(sem("sgu_landed"), 64)
            for t in range(TT):
                step(V.scalar_tensor_tensor(out=v_[:, t, :], in0=v_[:, t, :], scalar=small[:, 52 + 2 * t:53 + 2 * t],
                                            in1=ln_g, op0=ALU.subtract, op1=ALU.mult))
                settle()
                V.scalar_tensor_tensor(out=v_[:, t, :], in0=v_[:, t, :], scalar=small[:, 20 + t:21 + t],
                                       in1=ln_b, op0=ALU.mult, op1=ALU.add).then_inc(sem("v_normed"), 1)
            def row_out(i):
                v, c = ROW_OF_CHUNK[i], slice(i % 2 * CHUNK, (i % 2 + 1) * CHUNK)
                wait_full(dve, ("row", i))
                dve.wait_ge(sem("rows_landed"), 80)
                out(V.tensor_tensor(rows[:, v, c], bank(("row", i))[:, :], rows[:, v, c], ALU.add), ("row", i))
                if v == 2:
                    wait_out(dve, ("row", i))
                    step(V.scalar_tensor_tensor(out=rows[:, v, c], in0=rows[:, v, c], scalar=1.0, in1=ffn_g[:, c],
                                                op0=ALU.add, op1=ALU.mult))

            for i, (name, n) in enumerate(GATES):
                for t in range(TT):
                    if i >= 2:
                        wait_full(dve, ("row", 2 * i + t - 4))
                    ada_products(4 + 2 * i + t, [ada[:, (2 * i + t) % 4, :]], (0,))
                    biased_out((name, n, t), (ga, gb)[i // 2][:, t, n * CHUNK:(n + 1) * CHUNK])
                if i:
                    row_out(2 * i - 2)
                    row_out(2 * i - 1)
            row_out(6)
            row_out(7)
            dve.wait_ge(sem("gelu_done"), 2 * TT)
            for t in range(TT):
                for n in range(2):
                    wait_full(dve, ("sg", t, n))
                    for g in range(4):
                        gg = 4 * n + g
                        cut = u_[:, t, gg * P:(gg + 1) * P]
                        last = V.scalar_tensor_tensor(out=cut, in0=bank(("sg", t, n))[:, g * P:(g + 1) * P],
                                                      scalar=bs[:, gg:gg + 1], in1=cut, op0=ALU.add, op1=ALU.mult)
                        if g < 3:
                            step(last)
                    out(last, ("sg", t, n))
            dve.wait_ge(sem("gates_done"), 2 * TT)
            for t in range(TT):
                for n in range(2):
                    c = slice(n * CHUNK, (n + 1) * CHUNK)
                    wait_full(dve, ("upa", n, t))
                    out(V.tensor_tensor(ga[:, t, c], bank(("upa", n, t))[:, :], ga[:, t, c], ALU.mult), ("upa", n, t))
                    wait_full(dve, ("upb", n, t))
                    out(V.tensor_tensor(gb[:, t, c], bank(("upb", n, t))[:, :], gb[:, t, c], ALU.mult), ("upb", n, t))
                    wait_out(dve, ("upa", n, t))
                    wait_out(dve, ("upb", n, t))
                    V.tensor_tensor(mg[:, t, c], ga[:, t, c], gb[:, t, c], ALU.add).then_inc(sem("merged"), 1)
            for i in range(8):
                wait_out(dve, ("row", i))
            for t in range(TT):
                for n in range(2):
                    c = slice(n * CHUNK, (n + 1) * CHUNK)
                    wait_full(dve, ("wo", n, t))
                    out(V.tensor_tensor(ga[:, t, c], bank(("wo", n, t))[:, :], rows[:, 0, c], ALU.mult), ("wo", n, t))
                    wait_out(dve, ("wo", n, t))
                    step(V.tensor_tensor(x[:, t, c], x[:, t, c], ga[:, t, c], ALU.add))
                settle()
                V.tensor_tensor_reduce(junk[:, 0:D], x[:, t, :], x[:, t, :], 1.0 / D, NORM_EPS,
                                       ALU.mult, ALU.add, small[:, 24 + t:25 + t]).then_inc(sem("sums2"), 1)
                step(V.tensor_tensor(h2[:, t, :], x[:, t, :], rows[:, 2, :], ALU.mult))
                dve.wait_ge(sem("roots2"), t + 1)
                step(V.reciprocal(small[:, 26 + t:27 + t], small[:, 26 + t:27 + t]))
                settle()
                V.scalar_tensor_tensor(out=h2[:, t, :], in0=h2[:, t, :], scalar=small[:, 26 + t:27 + t],
                                       in1=rows[:, 3, :], op0=ALU.mult, op1=ALU.add).then_inc(sem("h2_ready"), 1)
            dve.wait_ge(sem("router_landed"), 32)
            for t in range(TT):
                wait_out(dve, ("rt", t))
                step(V.tensor_tensor(biased[:, t, :], score[:, t, :], rt_b, ALU.add))
                settle()
                step(V.max(top[:, t, :], biased[:, t, :]))
                settle()
                step(V.match_replace(rep_[:, t, :], top[:, t, :], biased[:, t, :], MASKED))
                settle()
                step(V.tensor_tensor(rep_[:, t, :], rep_[:, t, :], biased[:, t, :], ALU.not_equal))
                settle()
                step(V.tensor_tensor_reduce(wt[:, t, :], rep_[:, t, :], score[:, t, :], 1.0, 0.0, ALU.mult, ALU.add,
                                            small[:, 28 + t:29 + t]))
                settle()
                step(V.reciprocal(small[:, 30 + t:31 + t], small[:, 28 + t:29 + t]))
                settle()
                step(V.tensor_scalar(wt[:, t, :], wt[:, t, :], small[:, 30 + t:31 + t], ROUTE_SCALE, ALU.mult, ALU.mult))
                V.tensor_tensor(biased[:, t, :], rep_[:, t, :], k("from_end"), ALU.mult).then_inc(sem("chosen"), 1)
            dve.wait_ge(sem("chosen"), TT)
            for t in range(TT):
                step(V.max(row_f[:, t * TOP_K:(t + 1) * TOP_K], biased[:, t, :]))
            for f in range(2):
                dve.wait_ge(sem("silu_done"), f + 1)
                out(V.tensor_tensor(ffs[:, f, :], act_ff[:, f, :], bank(("shg", f))[:, S:2 * S], ALU.mult), ("shg", f))
            settle()
            for t in range(TT):
                wait_full(dve, ("rk", t))
                out(V.scalar_tensor_tensor(out=pos[:, t, :], in0=bank(("rk", t))[:, 0:E], scalar=1.0, in1=rep_[:, t, :],
                                           op0=ALU.add, op1=ALU.mult), ("rk", t))
            wait_full(dve, ("cnt", 0))
            step(V.tensor_reduce(small[:, 36:37], bank(("cnt", 0))[:, 0:E], AX_X, ALU.max))
            out(V.tensor_copy(counts[:, 0:E], bank(("cnt", 0))[:, 0:E]), ("cnt", 0))
            step(V.memset(counts[:, E + 1:E + 2], 0))
            step(V.memset(token_of[:, :], 0))
            wait_out(dve, ("cnt", 0))
            step(V.tensor_scalar(biased[:, 0, :], counts[:, 0:E], float(CAP), None, ALU.is_gt))
            settle()
            step(V.tensor_tensor_scan(biased[:, 1, :], biased[:, 0, :], k("zeros")[:, 0:E], 0.0, ALU.add, ALU.add))
            settle()
            step(V.tensor_copy(counts[:, E + 2:], biased[:, 1, :]))
            settle()
            V.tensor_copy(counts[:, E:E + 1], small[:, 36:37]).then_inc(sem("counts_ready"), 1)
            for t in range(TT):
                wait_out(dve, ("rk", t))

            def onehots(b):
                for t in range(TT):
                    if b >= ROUND and b - ROUND >= 1:
                        dve.wait_ge(sem("onehot_used"), b - ROUND)
                    elif b == ROUND:
                        dve.wait_ge(sem("slots_found"), 1)
                    V.tensor_tensor(onehot[:, b % ROUND, t * XB * CAP:(t + 1) * XB * CAP].rearrange("p (e c) -> p e c", e=XB),
                                    k("slot").unsqueeze(1).to_broadcast([P, XB, CAP]),
                                    pos[:, t, XB * b:XB * (b + 1)].unsqueeze(2).to_broadcast([P, XB, CAP]),
                                    ALU.is_equal).then_inc(sem("onehot_ready"), 1)

            def choice(i):
                t = i // TOP_K
                for src, dst in ((pos, pos_of), (wt, w_of)):
                    step(V.scalar_tensor_tensor(out=biased[:, t, :], in0=k("expert"), scalar=row_f[:, i:i + 1],
                                                in1=src[:, t, :], op0=ALU.is_equal, op1=ALU.mult,
                                                accum_out=dst[:, i:i + 1]))
                    settle()

            onehots(0)
            for t in range(TT):
                at = t * TOP_K
                step(V.tensor_scalar(row_f[:, at:at + TOP_K], row_f[:, at:at + TOP_K], -1.0, float(E), ALU.mult, ALU.add))
                step(V.tensor_scalar(over[:, t, :], pos[:, t, :], float(CAP), None, ALU.is_gt))
            settle()
            dve.wait_ge(sem("slots_found"), 1)
            out(V.tensor_copy(token_of[0:CAP, 0:XB], bank(("ix", 0))[0:CAP, 0:XB]), ("ix", 0))
            for b in range(1, E // XB):
                onehots(b)
                choice(b - 1)
            choice(TT * TOP_K - 1)
            for t in range(TT):
                step(V.tensor_tensor(over[:, t, :], over[:, t, :], wt[:, t, :], ALU.mult))
            dve.wait_ge(sem("slots_found"), 2)
            out(V.tensor_copy(token_of[0:CAP, XB:E], bank(("ix", 1))[0:CAP, XB:E]), ("ix", 1))

            step(V.scalar_tensor_tensor(out=row_f, in0=row_f, scalar=float(CAP), in1=pos_of, op0=ALU.mult, op1=ALU.add))
            step(V.tensor_scalar(pos_of, pos_of, float(CAP), None, ALU.is_le))
            settle()
            step(V.tensor_tensor(w_of, w_of, pos_of, ALU.mult))
            step(V.scalar_tensor_tensor(out=row_f, in0=row_f, scalar=-1.0, in1=pos_of, op0=ALU.add, op1=ALU.mult))
            settle()
            V.tensor_copy(row_of[:, :], row_f).then_inc(sem("row_of_ready"), 1)
            for n in range(2):
                for t in range(TT):
                    wait_full(dve, ("shd", n, t))
                    out(V.tensor_copy(y[:, t, n * CHUNK:(n + 1) * CHUNK], bank(("shd", n, t))[:, :]), ("shd", n, t))
            for n in range(2):
                for t in range(TT):
                    wait_out(dve, ("shd", n, t))

            def rows_out(which, slot, it=0):
                wait_full(dve, ("gT", which, 1), it)
                out(V.tensor_copy(xgT[:, slot, 4 * CAP:], bank(("gT", which, 1))[:, 0:4 * CAP]), ("gT", which, 1))

            def hidden(which, slot, e, it=0):
                dve.wait_ge(sem("sil_done"), e + 1)
                out(V.tensor_tensor(hid[:, slot, :], sil[:, slot, :], bank(("gu", which))[:, 2 * CAP:4 * CAP], ALU.mult),
                    ("gu", which))

            def output(which, slot, it=0):
                dve.wait_ge(sem(f"rows_stored{slot}"), 16 * (it + 1))
                wait_full(dve, ("yd", which, 1), it)
                out(V.tensor_copy(ys[0:CAP, slot, CHUNK:], bank(("yd", which, 1))[0:CAP, :]), ("yd", which, 1))

            rows_out("first", 0)
            hidden("first", 0, 0)
            rows_out("second", 1)
            with dve.Fori(0, (E - 1) // ROUND) as it:
                for j in range(ROUND):
                    hidden(j, (j + 1) % ROUND, it * ROUND + j + 1, it)
                    rows_out(j, (j + 2) % ROUND, it)
                    output(j, j, it)
            output("last", 0, (E - 1) // ROUND)
            dve.sem_inc(sem("over_vector"), 1)

            def sums(e, done):
                for f in range(2):
                    dve.wait_ge(sem("over_scalar"), 2 * done + f + 1)
                    V.tensor_tensor(ffs[:, f, :], act_ff[:, f, :], psum[f][:, S:2 * S], ALU.mult)\
                        .then_inc(sem("over_vector"), 1)
                for n in range(2):
                    for t in range(TT):
                        c = slice(n * CHUNK, (n + 1) * CHUNK)
                        dve.wait_ge(sem("over_tensor"), 6 * done + 4 + 2 * n + t)
                        V.scalar_tensor_tensor(out=y[:, t, c], in0=psum[2 + 2 * n + t][:, :], scalar=over[:, t, bass.ds(e, 1)],
                                               in1=y[:, t, c], op0=ALU.mult, op1=ALU.add).then_inc(sem("over_vector"), 1)
                dve.wait_ge(sem("over_vector"), 6 * done + 7)
                dve.sem_inc(sem("expert_added"), 1)

            overflow(dve, sums)
            for i in range(TT * TOP_K):
                j, t = divmod(i, TT)
                at = t * TOP_K + j
                dve.wait_ge(sem(f"returned{i % len(back)}"), 16 * (i // len(back) + 1))
                if j:
                    dve.wait_ge(sem("row_added"), i - TT + 1)
                V.scalar_tensor_tensor(out=y[:, t, :], in0=back[i % len(back)], scalar=w_of[:, at:at + 1], in1=y[:, t, :],
                                       op0=ALU.mult, op1=ALU.add).then_inc(sem("row_added"), 1)
            dve.wait_ge(sem("row_added"), TT * TOP_K)
            dve.wait_ge(sem("fin_landed"), 16)
            for t in range(TT):
                step(V.tensor_tensor(y[:, t, :], y[:, t, :], rows[:, 1, :], ALU.mult))
                settle()
                step(V.tensor_tensor(x[:, t, :], x[:, t, :], y[:, t, :], ALU.add))
                settle()
                V.tensor_tensor_reduce(y[:, t, :], x[:, t, :], x[:, t, :], 1.0 / D, NORM_EPS,
                                       ALU.mult, ALU.add, small[:, 32 + t:33 + t]).then_inc(sem("sums3"), 1)
            for t in range(TT):
                dve.wait_ge(sem("roots3"), t + 1)
                step(V.reciprocal(small[:, 34 + t:35 + t], small[:, 34 + t:35 + t]))
                settle()
                V.scalar_tensor_tensor(out=x[:, t, :], in0=x[:, t, :], scalar=small[:, 34 + t:35 + t],
                                       in1=fin_g, op0=ALU.mult, op1=ALU.mult).then_inc(sem("x_new"), 1)
            dve.wait_ge(sem("x_new"), TT)

            before = count[0]
            count[2] = DVE_STEPS_PER_LAYER
            dve.sem_inc(sem("split_ready"), NU)
            with dve.Fori(0, L2) as layer:
                def layer_norm(jobs, g, b, which):
                    for t in range(TT):
                        for n in range(2):
                            c = slice(n * CHUNK, (n + 1) * CHUNK)
                            wait_full(dve, (jobs, n, t), layer)
                            out(V.scalar_tensor_tensor(out=x[:, t, c], in0=x[:, t, c], scalar=ALPHA,
                                                       in1=bank((jobs, n, t))[:, :], op0=ALU.mult, op1=ALU.add), (jobs, n, t))
                            wait_out(dve, (jobs, n, t), layer)
                            step(V.bn_stats(small[:, 40 + 6 * n:46 + 6 * n], x[:, t, c]))
                        settle(layer)
                        dve.sem_inc(sem("stats_read"), 1)
                        step(V.bn_aggr(lnm[:, 2 * t:2 * t + 2], small[:, 40:52]))
                        settle(layer)
                        V.tensor_scalar(lnv[:, t:t + 1], lnm[:, 2 * t + 1:2 * t + 2], LN_EPS, None, ALU.add)\
                            .then_inc(sem("l_var"), 1)
                        step(V.scalar_tensor_tensor(out=x[:, t, :], in0=x[:, t, :], scalar=lnm[:, 2 * t:2 * t + 1],
                                                    in1=g, op0=ALU.subtract, op1=ALU.mult))
                        dve.wait_ge(sem("l_root"), 2 * TT * layer + TT * which + t + 1)
                        step(V.reciprocal(lnv[:, 2 + t:3 + t], lnv[:, 2 + t:3 + t]))
                        settle(layer)
                        V.scalar_tensor_tensor(out=x[:, t, :], in0=x[:, t, :], scalar=lnv[:, 2 + t:3 + t],
                                               in1=b, op0=ALU.mult, op1=ALU.add).then_inc(sem("x_new"), 1)
                    dve.wait_ge(sem("x_new"), 2 * TT * layer + TT * (which + 2))

                for p in range(2):
                    wait_full(dve, ("qs", p), layer)
                    out(V.tensor_scalar(qsT[:, 2 * p:2 * p + 2, :].rearrange("p a b -> p (a b)"), bank(("qs", p))[:, :],
                                        DH2 ** -0.5, None, ALU.mult), ("qs", p))
                for t in range(TT):
                    wait_full(dve, ("vs", t), layer)
                    out(V.tensor_copy(vs[:, t, :], bank(("vs", t))[:, :]), ("vs", t))

                def rotate(which, t):
                    v3 = qk[:, which, t, :].rearrange("p (h d) -> p h d", d=DH2)
                    half = ROPE2 // 2
                    x1, x2 = v3[:, :, 0:half], v3[:, :, half:ROPE2]

                    def table(name):
                        return k(name)[:, t * half:(t + 1) * half].unsqueeze(1).to_broadcast([P, H2, half])

                    tmp = [rope[:, j, 0:H2 * half].rearrange("p (h f) -> p h f", f=half) for j in range(4)]
                    for j, (src, name) in enumerate(((x1, "pcos"), (x2, "psin"), (x2, "pcos"), (x1, "psin"))):
                        step(V.tensor_tensor(tmp[j], src, table(name), ALU.mult))
                    settle(layer)
                    step(V.tensor_tensor(x1, tmp[0], tmp[1], ALU.subtract))
                    V.tensor_tensor(x2, tmp[2], tmp[3], ALU.add).then_inc(sem("roped"), 1)

                def filler_out(i):
                    name, n, t = FILLERS[i]
                    key = (name, n, t)
                    if name in ("qm", "km", "vm"):
                        wait_full(dve, key, layer)
                        if name == "vm":
                            out(V.tensor_copy(vm[:, t, :], bank(key)[:, :]), key)
                        else:
                            which = ("qm", "km").index(name)
                            out(V.tensor_scalar(qk[:, which, t, :], bank(key)[:, :], (DH2 ** -0.5, 1.0)[which], None,
                                                ALU.mult), key)
                            wait_out(dve, key, layer)
                            rotate(which, t)
                    else:
                        wait_out(dve, key, layer)
                        g = gates[:, ("gs", "gm").index(name), t, n * CHUNK:(n + 1) * CHUNK]
                        step(V.tensor_scalar(g, g, 1.0, None, ALU.add))
                        settle(layer)
                        step(V.reciprocal(g, g))

                def heads_of(ap, nh):
                    return ap.rearrange("p (h k) -> p h k", h=nh)

                def stick_b(i):
                    t, h0, nh, keys = ITEMS[i]
                    e_, r_ = es[:, i % 2, :], rw[:, i % 2, :]
                    z = bank(("sc", i))[:, :]
                    dve.wait_ge(sem("ln_done"), NI * layer + i + 1)
                    step(V.scalar_tensor_tensor(out=e_, in0=z, scalar=0.0, in1=e_, op0=ALU.max, op1=ALU.add))
                    settle(layer)
                    diag = heads_of(e_, nh)[:, :, keys - P:keys]
                    step(V.tensor_tensor(diag, diag, k("past01").unsqueeze(1).to_broadcast([P, nh, P]), ALU.mult))
                    settle(layer)
                    if i >= 2:
                        wait_full(dve, ("wT", i - 2), layer)
                    for j in range(nh):
                        back = slice((j + 1) * keys - 1, j * keys - 1 if j else None, -1)
                        step(V.tensor_tensor_scan(r_[:, back], e_[:, back], k("zeros")[:, 0:keys], 0.0, ALU.add, ALU.add))
                    settle(layer)
                    out(V.tensor_tensor(r_, z, r_, ALU.subtract), ("sc", i))
                    wait_out(dve, ("sc", i), layer)
                    diag = heads_of(r_, nh)[:, :, keys - P:keys]
                    V.tensor_tensor(diag, diag, k("own_future").unsqueeze(1).to_broadcast([P, nh, P]), ALU.add)\
                        .then_inc(sem("log_weights"), 1)

                def block_max(i):
                    t, h0, nh, keys = ITEMS[i]
                    key = ("sc", NI + i)
                    wait_full(dve, key, layer)
                    diag = heads_of(bank(key)[:, :], nh)[:, :, keys - P:keys]
                    step(V.tensor_tensor(diag, diag, k("future").unsqueeze(1).to_broadcast([P, nh, P]), ALU.add))
                    settle(layer)
                    hh = t * H2 + h0
                    step(V.tensor_reduce(mbn[:, hh:hh + nh], heads_of(bank(key)[:, :], nh), AX_X, ALU.max))
                    settle(layer)
                    V.tensor_scalar(mbn[:, hh:hh + nh], mbn[:, hh:hh + nh], -1.0, None, ALU.mult).then_inc(sem("mb_max"), 1)

                def attention_out(b, t):
                    dve.wait_ge(sem("item_summed"), 2 * NI * layer + NI * b + LAST_OF_TILE[t] + 1)
                    key = ("o", b, t)
                    side = P // DH2
                    dst = o[:, b, t, :].rearrange("p (j s d) -> p s j d", s=side, d=DH2)
                    src = bank(key)[:, :].rearrange("p (s j d) -> p s j d", s=side, d=DH2)
                    if b == 0:
                        out(V.tensor_copy(dst, src), key)
                        return
                    ms = mbs[:, t * H2:(t + 1) * H2]
                    step(V.reciprocal(ms, ms))
                    settle(layer)
                    n = H2 // side
                    for s_ in range(side):
                        last = V.tensor_tensor(dst[:, s_], src[:, s_],
                                               ms[:, s_ * n:(s_ + 1) * n].unsqueeze(2).to_broadcast([P, n, DH2]), ALU.mult)
                        if s_ == 0:
                            step(last)
                    out(last, key)

                for i in range(2 * NI + 3):
                    if 1 <= i <= len(FILLERS):
                        filler_out(i - 1)
                    if NI <= i < 2 * NI:
                        block_max(i - NI)
                    if 1 <= i <= NI:
                        stick_b(i - 1)
                    for b in range(2):
                        for t in range(TT):
                            if i == NI * b + LAST_OF_TILE[t] + 3:
                                attention_out(b, t)
                settle(layer)
                for t in range(TT):
                    for n in range(2):
                        c = slice(n * CHUNK, (n + 1) * CHUNK)
                        for b, name in enumerate(("bs", "bm")):
                            wait_full(dve, (name, n, t), layer)
                            g = gates[:, b, t, c]
                            out(V.tensor_tensor(g, bank((name, n, t))[:, :], g, ALU.mult), (name, n, t))
                        wait_out(dve, ("bs", n, t), layer)
                        wait_out(dve, ("bm", n, t), layer)
                        V.tensor_tensor(lmg[:, t, c], gates[:, 0, t, c], gates[:, 1, t, c], ALU.add)\
                            .then_inc(sem("l_merged"), 1)
                dve.wait_ge(sem("ln_landed"), 64 * (layer + 1))

                def low(u):
                    key = FFN_UNITS[u]
                    dve.wait_ge(sem("high_ready"), NU * layer + u + 1)
                    V.tensor_tensor(ws[:, u % SPLIT_SLOTS, 1, :], ring[:, units.place[key][0], :],
                                    ws[:, u % SPLIT_SLOTS, 0, :], ALU.subtract).then_inc(sem("split_ready"), 1)

                low(0)
                low(1)
                layer_norm("l_wo", ln[:, 0, :], ln[:, 1, :], 0)
                for g in range(4):
                    dve.wait_ge(sem("y_high"), 4 * layer + g + 1)
                    at = (slice(None), slice(4 * (g % 2), 4 * (g % 2) + 4), slice(g // 2 * P, (g // 2 + 1) * P))
                    out(V.tensor_tensor(xs[:, 1][at], bank(("l_yT", g))[:, :].rearrange("p (a b) -> p a b", b=P),
                                        xs[:, 0][at], ALU.subtract), ("l_yT", g))
                for pair in range(FT // 2):
                    if pair < FT // 2 - 1:
                        low(FFN_UNITS.index(("fg", pair + 1)))
                    for f in (2 * pair, 2 * pair + 1):
                        dve.wait_ge(sem("l_silu"), FT * layer + f + 1)
                        out(V.tensor_tensor(fh32[:, f % 4, :], silu[:, f % 2, :], bank(("fg", f))[:, S:2 * S], ALU.mult),
                            ("fg", f))
                        dve.wait_ge(sem("hidden_high"), FT * layer + f + 1)
                        V.tensor_tensor(fh[:, f % 4, 1, :], fh32[:, f % 4, :], fh[:, f % 4, 0, :], ALU.subtract)\
                            .then_inc(sem("hidden_split"), 1)
                    if pair < FT // 2 - 1:
                        low(FFN_UNITS.index(("fu", pair + 1)))
                    low(FFN_UNITS.index(("fd", pair)))
                layer_norm("fd", ln[:, 2, :], ln[:, 3, :], 1)
            assert count[0] - before == DVE_STEPS_PER_LAYER, count[0] - before


def kernel(**inputs):
    import concourse.bacc as bacc
    from concourse.bass_utils import run_bass_kernel_spmd

    def arr(name):
        return np.asarray(inputs[name])

    def columns(v):
        return v.reshape(-1, P).T

    c = np.stack([arr("c")[0], arr("c_ctx")], -1)
    data = {
        "x": arr("x")[0], "ctx": arr("ctx")[0],
        "cols": np.concatenate([c.reshape(KT, P, 2).transpose(1, 0, 2).reshape(P, 2 * KT),
                                columns(arr("b_ada")[0, :2 * D]), columns(arr("norm_mix_g")[0]),
                                columns(arr("b_in")[0, COL_NQ:COL_NV]), arr("sgu_b_s")[0].T], 1),
        "b_ada": arr("b_ada"), "norm_ffn_g": arr("norm_ffn_g"),
        "b_in": arr("b_in"),
        "w_sT": arr("sgu_w_s")[0].transpose(2, 0, 1),
        "sgu_ln_g": arr("sgu_ln_g"), "sgu_ln_b": arr("sgu_ln_b"), "tiny_w_o": arr("tiny_w_o")[0],
        "na_rpb": arr("na_rpb"), "b_router": arr("b_router"),
        "final_norm_g": arr("final_norm_g").reshape(1, D),
        "consts": constants(),
    }
    for name in ("w_ada", "w_in", "w_up_a", "w_up_b", "w_out", "w_router", "w_e_gate", "w_e_up", "w_e_down",
                 "w_sh_gate", "w_sh_up", "w_sh_down"):
        data[name] = arr(name)[0]
    for name in ("w_in_2", "w_branch_sb_2", "w_branch_moba_2", "w_out_2", "ln_mix_g_2", "ln_mix_b_2",
                 "w_ffn_gate_2", "w_ffn_up_2", "w_ffn_down_2", "ln_ffn_g_2", "ln_ffn_b_2"):
        data[name] = arr(name)
    nc = bacc.Bacc("TRN2", target_bir_lowering=False, num_devices=1)
    arrays, handles = {}, {}
    for name, value in data.items():
        value = np.ascontiguousarray(value)
        arrays["in_" + name] = value
        handles[name] = nc.dram_tensor("in_" + name, value.shape, mybir.dt.from_np(value.dtype), kind="ExternalInput").ap()
    handles["out"] = nc.dram_tensor("out_0", (S, D), F32, kind="ExternalOutput").ap()
    handles["rpb_copies"] = nc.dram_tensor("rpb_copies", (GRID_W, data["na_rpb"].size), F32, kind="Internal").ap()
    handles["h2_rows"] = nc.dram_tensor("h2_rows", (S, D), F32, kind="Internal").ap()
    handles["expert_rows"] = nc.dram_tensor("expert_rows", (E, CAP, D), F32, kind="Internal").ap()
    build(nc, handles)
    r = run_bass_kernel_spmd(nc, [arrays], core_ids=[0])
    return r.results[0]["out_0"].reshape(1, S, D)
```
